# Optimizing a Trainium2 kernel written in Bass

```python
import math
import jax, jax.numpy as jnp
from jax import lax
import numpy as np

D_MODEL = 2048
BATCH = 1
SEQ = 512
DEPTH = 1
DEC_BATCH = 8
DEC_SEQ = 4
PAST_LEN = 4096
PAGE_SIZE = 128

HEAD = 128
D_MIX = D_MODEL
D_A = D_MIX // 4
D_B = D_MIX // 4
D_C = D_MIX - D_A - D_B
H_A = D_A // HEAD
DQ_A = HEAD // 2
DV_A = HEAD
H_B = D_B // HEAD
DH_B = HEAD
CMP_BLOCK = 64
N_SEL = 16
WINDOW = 512
H_C = D_C // HEAD
DQK_C = HEAD // 2
DV_C = HEAD
CONV_W = 4
MLSTM_CHUNK = 64
Q_BLOCK = 128
EPS = 1e-6

IN_WIDTHS = (
    H_A * 2 * DQ_A, H_A * 2 * DQ_A, D_A, D_A,
    D_B, 6 * DH_B, 3 * H_B, D_B,
    2 * H_C * DQK_C, D_C, 2 * H_C, D_C, D_C,
)
N_IN = sum(IN_WIDTHS)

kernel_name = 'hybrid_diffattn_nsa_mlstm_step'

def rms_norm(x, g):
    xf = x.astype(jnp.float32)
    y = xf * lax.rsqrt(jnp.mean(xf * xf, axis=-1, keepdims=True) + EPS)
    return (y * g.astype(jnp.float32)).astype(x.dtype)

def masked_softmax(s, mask):
    s = jnp.where(mask, s.astype(jnp.float32), -jnp.inf)
    m = jnp.max(s, axis=-1, keepdims=True)
    m = jnp.where(jnp.isfinite(m), m, 0.0)
    p = jnp.exp(s - m)
    return p / jnp.maximum(jnp.sum(p, axis=-1, keepdims=True), 1e-30)

def _query_block(T):
    return Q_BLOCK if T % Q_BLOCK == 0 else T

def map_query_blocks(fn, q, q_pos):
    B, T = q.shape[:2]
    qb = _query_block(T)
    nb = T // qb
    qs = jnp.moveaxis(q.reshape(B, nb, qb, *q.shape[2:]), 1, 0)
    out = lax.map(lambda xs: fn(xs[0], xs[1]), (qs, q_pos.reshape(nb, qb)))
    return jnp.moveaxis(out, 0, 1).reshape(B, T, *out.shape[3:])

def diff_attention(q, k, v, q_pos, k_pos, lam):
    kf = k.astype(jnp.float32)
    vf = v.astype(jnp.float32)
    scale = DQ_A ** -0.5

    def block(qb, pos):
        s = jnp.einsum('bqhcd,bkhcd->bchqk', qb.astype(jnp.float32), kf) * scale
        p = masked_softmax(s, k_pos[None, :] <= pos[:, None])
        w = p[:, 0] - lam * p[:, 1]
        return jnp.einsum('bhqk,bkhv->bqhv', w, vf)

    return map_query_blocks(block, q, q_pos)

def nsa_compressed_selected(q, kv, q_pos, w_pool, g_kc):
    B, L = kv.shape[:2]
    nblk = -(-L // CMP_BLOCK)
    pad = nblk * CMP_BLOCK - L
    kvb = jnp.pad(kv, ((0, 0), (0, pad), (0, 0), (0, 0))).reshape(B, nblk, CMP_BLOCK, 4, DH_B)
    wp = w_pool.astype(jnp.float32)
    kcb = rms_norm(jnp.einsum('bnpd,p->bnd', kvb[:, :, :, 0].astype(jnp.float32), wp[0]), g_kc)
    vcb = jnp.einsum('bnpd,p->bnd', kvb[:, :, :, 1].astype(jnp.float32), wp[1])
    ksb = kvb[:, :, :, 2]
    vsb = kvb[:, :, :, 3]
    n_top = min(N_SEL, nblk)
    blk_ids = jnp.arange(nblk)
    scale = DH_B ** -0.5

    def block(qb, pos):
        Q = qb.shape[1]
        qf = qb.astype(jnp.float32)
        cur = pos // CMP_BLOCK
        cmask = blk_ids[None, :] < cur[:, None]
        sc = jnp.einsum('bqhd,bnd->bqhn', qf, kcb) * scale
        pc = masked_softmax(sc, cmask[None, :, None, :])
        o_cmp = jnp.einsum('bqhn,bnd->bqhd', pc, vcb)
        imp = jnp.where(cmask[None], jnp.sum(pc, axis=2), -1.0)
        top_v, top_i = lax.top_k(imp, n_top)
        idx = jnp.concatenate([top_i, jnp.broadcast_to(cur[None, :, None], (B, Q, 1)).astype(top_i.dtype)], axis=-1)
        valid = jnp.concatenate([top_v >= 0.0, jnp.ones((B, Q, 1), bool)], axis=-1)
        kg = jax.vmap(lambda a, i: a[i])(ksb, idx).astype(jnp.float32)
        vg = jax.vmap(lambda a, i: a[i])(vsb, idx).astype(jnp.float32)
        kpos = idx[..., None] * CMP_BLOCK + jnp.arange(CMP_BLOCK)
        smask = valid[..., None] & (kpos <= pos[None, :, None, None])
        ss = jnp.einsum('bqhd,bqnpd->bqhnp', qf, kg) * scale
        ps = masked_softmax(ss.reshape(B, Q, H_B, -1), smask.reshape(B, Q, 1, -1))
        o_sel = jnp.einsum('bqhk,bqkd->bqhd', ps, vg.reshape(B, Q, -1, DH_B))
        return jnp.stack([o_cmp, o_sel], axis=-2)

    return map_query_blocks(block, q, q_pos)

def window_attention_banded(q, k, v):
    B, T = q.shape[:2]
    qb = _query_block(T)
    nb = T // qb
    span = WINDOW + qb
    kpad = jnp.pad(k, ((0, 0), (WINDOW, 0), (0, 0)))
    vpad = jnp.pad(v, ((0, 0), (WINDOW, 0), (0, 0)))
    idx = jnp.arange(nb)[:, None] * qb + jnp.arange(span)[None, :]
    k_pos = idx - WINDOW
    q_pos = jnp.arange(nb)[:, None] * qb + jnp.arange(qb)[None, :]
    kg = kpad[:, idx].astype(jnp.float32)
    vg = vpad[:, idx].astype(jnp.float32)
    diff = q_pos[:, :, None] - k_pos[:, None, :]
    mask = (k_pos[:, None, :] >= 0) & (diff >= 0) & (diff < WINDOW)
    s = jnp.einsum('bnqhd,bnkd->bnqhk', q.reshape(B, nb, qb, H_B, DH_B).astype(jnp.float32), kg) * DH_B ** -0.5
    p = masked_softmax(s, mask[None, :, :, None, :])
    return jnp.einsum('bnqhk,bnkd->bnqhd', p, vg).reshape(B, T, H_B, DH_B)

def window_attention_dense(q, k, v, q_pos, k_pos):
    s = jnp.einsum('bqhd,bkd->bqhk', q.astype(jnp.float32), k.astype(jnp.float32)) * DH_B ** -0.5
    diff = q_pos[:, None] - k_pos[None, :]
    mask = (diff >= 0) & (diff < WINDOW)
    p = masked_softmax(s, mask[None, :, None, :])
    return jnp.einsum('bqhk,bkd->bqhd', p, v.astype(jnp.float32))

def mlstm_chunkwise(q, k, v, i_pre, f_pre, C0, n0, m0):
    B, T, H, dk = q.shape
    dv = v.shape[-1]
    L = math.gcd(T, MLSTM_CHUNK)
    nc = T // L

    def to_chunks(a):
        return jnp.moveaxis(a.astype(jnp.float32).reshape(B, nc, L, *a.shape[2:]), 1, 0)

    causal = jnp.tril(jnp.ones((L, L), bool))

    def step(carry, xs):
        C, n, m = carry
        qc, kc, vc, ic, fc = xs
        b = jnp.cumsum(jax.nn.log_sigmoid(fc), axis=1)
        D = b[:, :, None, :] - b[:, None, :, :] + ic[:, None, :, :]
        D = jnp.where(causal[None, :, :, None], D, -jnp.inf)
        inter = b + m[:, None, :]
        m_t = jnp.maximum(inter, jnp.max(D, axis=2))
        w_intra = jnp.exp(D - m_t[:, :, None, :])
        w_inter = jnp.exp(inter - m_t)
        qk = jnp.einsum('bthd,bshd->btsh', qc, kc) * w_intra
        num = w_inter[..., None] * jnp.einsum('bhvd,bthd->bthv', C, qc) + jnp.einsum('btsh,bshv->bthv', qk, vc)
        den = w_inter * jnp.einsum('bhd,bthd->bth', n, qc) + jnp.sum(qk, axis=2)
        h = num / jnp.maximum(jnp.abs(den), jnp.exp(-m_t))[..., None]
        bL = b[:, -1]
        dec = bL[:, None, :] - b + ic
        m_new = jnp.maximum(bL + m, jnp.max(dec, axis=1))
        wk = jnp.exp(dec - m_new[:, None, :])
        carry_scale = jnp.exp(bL + m - m_new)
        C_new = carry_scale[..., None, None] * C + jnp.einsum('bsh,bshv,bshd->bhvd', wk, vc, kc)
        n_new = carry_scale[..., None] * n + jnp.einsum('bsh,bshd->bhd', wk, kc)
        return (C_new, n_new, m_new), h

    carry, hs = lax.scan(step, (C0.astype(jnp.float32), n0.astype(jnp.float32), m0.astype(jnp.float32)),
                         (to_chunks(q), to_chunks(k), to_chunks(v), to_chunks(i_pre), to_chunks(f_pre)))
    return jnp.moveaxis(hs, 0, 1).reshape(B, T, H, dv), carry

def mixer_layer(x, l, lw, past, past_len, win_buf):
    (norm_g, w_in, w_out, a_qk_g, a_lambda, a_out_g, b_qk_g, b_cmp_w,
     c_conv_w, c_conv_b, c_gate_b, c_out_g) = lw
    B, T, _ = x.shape
    f32 = jnp.float32
    h = rms_norm(x, norm_g)
    proj = jnp.einsum('btd,dn->btn', h, w_in)
    splits = np.cumsum(IN_WIDTHS)[:-1].tolist()
    (aq, ak, av, az, bq, bkv, bg, bz, cqk, cv, cif, co, cz) = jnp.split(proj, splits, axis=-1)
    q_pos = past_len + jnp.arange(T)

    lam_init = 0.8 - 0.6 * math.exp(-0.3 * l)
    qa = rms_norm(aq.reshape(B, T, H_A, 2, DQ_A), a_qk_g[0])
    ka = rms_norm(ak.reshape(B, T, H_A, 2, DQ_A), a_qk_g[1])
    new_a = jnp.stack([ka.reshape(B, T, H_A, HEAD), av.reshape(B, T, H_A, DV_A)], axis=2)
    kv_a = new_a if past is None else jnp.concatenate([past[0].astype(new_a.dtype), new_a], axis=1)
    L = kv_a.shape[1]
    lp = a_lambda.astype(f32)
    lam = jnp.exp(jnp.sum(lp[0] * lp[1])) - jnp.exp(jnp.sum(lp[2] * lp[3])) + lam_init
    oa = diff_attention(qa, kv_a[:, :, 0].reshape(B, L, H_A, 2, DQ_A), kv_a[:, :, 1], q_pos, jnp.arange(L), lam)
    oa = rms_norm(oa, a_out_g) * (1.0 - lam_init)
    ya = oa.reshape(B, T, D_A) * jax.nn.silu(az.astype(f32))

    qb_ = rms_norm(bq.reshape(B, T, H_B, DH_B), b_qk_g[0])
    bkv = bkv.reshape(B, T, 6, DH_B)
    new_b = jnp.stack([bkv[:, :, 0], bkv[:, :, 1], rms_norm(bkv[:, :, 2], b_qk_g[2]), bkv[:, :, 3]], axis=2)
    new_w = jnp.stack([rms_norm(bkv[:, :, 4], b_qk_g[3]), bkv[:, :, 5]], axis=2)
    if past is None:
        kv_b = new_b
        o_win = window_attention_banded(qb_, new_w[:, :, 0], new_w[:, :, 1])
        win_state = jnp.concatenate([jnp.zeros((B, win_buf, 2, DH_B), new_w.dtype), new_w], axis=1)[:, -win_buf:]
    else:
        kv_b = jnp.concatenate([past[1].astype(new_b.dtype), new_b], axis=1)
        w_all = jnp.concatenate([past[2].astype(new_w.dtype), new_w], axis=1)
        k_pos_w = past_len - win_buf + jnp.arange(win_buf + T)
        o_win = window_attention_dense(qb_, w_all[:, :, 0], w_all[:, :, 1], q_pos, k_pos_w)
        win_state = w_all[:, -win_buf:]
    o_cs = nsa_compressed_selected(qb_, kv_b, q_pos, b_cmp_w, b_qk_g[1])
    g = jax.nn.sigmoid(bg.astype(f32).reshape(B, T, H_B, 3))
    ob = g[..., 0:1] * o_cs[..., 0, :] + g[..., 1:2] * o_cs[..., 1, :] + g[..., 2:3] * o_win
    yb = ob.reshape(B, T, D_B) * jax.nn.silu(bz.astype(f32))

    buf = jnp.zeros((B, CONV_W - 1, cqk.shape[-1]), cqk.dtype) if past is None else past[3].astype(cqk.dtype)
    xp = jnp.concatenate([buf, cqk], axis=1)
    conv_state = xp[:, -(CONV_W - 1):]
    acc = c_conv_b.astype(f32)
    for j in range(CONV_W):
        acc = acc + xp[:, j:j + T].astype(f32) * c_conv_w[j].astype(f32)
    qk_c = jax.nn.silu(acc)
    qc = qk_c[..., :H_C * DQK_C].reshape(B, T, H_C, DQK_C) * (DQK_C ** -0.5)
    kc = qk_c[..., H_C * DQK_C:].reshape(B, T, H_C, DQK_C)
    vc = cv.reshape(B, T, H_C, DV_C)
    gif = cif.astype(f32).reshape(B, T, 2, H_C) + c_gate_b.astype(f32)
    if past is None:
        C0 = jnp.zeros((B, H_C, DV_C, DQK_C), f32)
        n0 = jnp.zeros((B, H_C, DQK_C), f32)
        m0 = jnp.zeros((B, H_C), f32)
    else:
        C0, n0, m0 = past[4], past[5], past[6]
    hc, (C1, n1, m1) = mlstm_chunkwise(qc, kc, vc, gif[:, :, 0], gif[:, :, 1], C0, n0, m0)
    hc = rms_norm(hc, c_out_g) * jax.nn.sigmoid(co.astype(f32).reshape(B, T, H_C, DV_C))
    yc = hc.reshape(B, T, D_C) * jax.nn.silu(cz.astype(f32))

    mix = jnp.concatenate([ya, yb, yc], axis=-1)
    y = x + jnp.einsum('btm,md->btd', mix, w_out.astype(f32)).astype(x.dtype)
    return y, (new_a, new_b, win_state, conv_state, C1, n1, m1)

def setup_inputs(seed: int = 0) -> dict:
    key = jax.random.key(seed)
    ks = jax.random.split(key, 32)
    n_pages = PAST_LEN // PAGE_SIZE
    used = DEC_BATCH * n_pages
    n_pool = used + max(1, used // 4)
    win_buf = min(WINDOW, PAST_LEN)
    nrm = jax.random.normal
    inp = {}
    inp['x_prompt'] = nrm(ks[0], (BATCH, SEQ, D_MODEL), jnp.float32)
    inp['x_sample'] = nrm(ks[1], (DEC_BATCH, DEC_SEQ, D_MODEL), jnp.float32)
    inp['cache_a_kv'] = nrm(ks[2], (DEPTH, n_pool, PAGE_SIZE, 2, H_A, HEAD), jnp.float32)
    inp['cache_b_kv'] = nrm(ks[3], (DEPTH, n_pool, PAGE_SIZE, 4, DH_B), jnp.float32)
    inp['state_b_win'] = nrm(ks[4], (DEPTH, DEC_BATCH, win_buf, 2, DH_B), jnp.float32)
    inp['state_c_conv'] = nrm(ks[5], (DEPTH, DEC_BATCH, CONV_W - 1, 2 * H_C * DQK_C), jnp.float32)
    inp['state_c_C'] = 0.1 * nrm(ks[6], (DEPTH, DEC_BATCH, H_C, DV_C, DQK_C), jnp.float32)
    inp['state_c_n'] = 0.1 * nrm(ks[7], (DEPTH, DEC_BATCH, H_C, DQK_C), jnp.float32)
    inp['state_c_m'] = nrm(ks[8], (DEPTH, DEC_BATCH, H_C), jnp.float32)
    perm = jax.random.permutation(ks[9], n_pool)
    inp['page_table'] = perm[:used].reshape(DEC_BATCH, n_pages).astype(jnp.int32)
    inp['norm_g'] = 1.0 + 0.02 * nrm(ks[10], (DEPTH, D_MODEL), jnp.float32)
    inp['w_in'] = nrm(ks[11], (DEPTH, D_MODEL, N_IN), jnp.float32) * D_MODEL ** -0.5
    inp['w_out'] = nrm(ks[12], (DEPTH, D_MIX, D_MODEL), jnp.float32) * D_MIX ** -0.5
    inp['a_qk_g'] = 1.0 + 0.02 * nrm(ks[13], (DEPTH, 2, DQ_A), jnp.float32)
    inp['a_lambda'] = 0.1 * nrm(ks[14], (DEPTH, 4, DQ_A), jnp.float32)
    inp['a_out_g'] = 1.0 + 0.02 * nrm(ks[15], (DEPTH, DV_A), jnp.float32)
    inp['b_qk_g'] = 1.0 + 0.02 * nrm(ks[16], (DEPTH, 4, DH_B), jnp.float32)
    inp['b_cmp_w'] = (1.0 + 0.1 * nrm(ks[17], (DEPTH, 2, CMP_BLOCK), jnp.float32)) / CMP_BLOCK
    inp['c_conv_w'] = nrm(ks[18], (DEPTH, CONV_W, 2 * H_C * DQK_C), jnp.float32) * CONV_W ** -0.5
    inp['c_conv_b'] = 0.02 * nrm(ks[19], (DEPTH, 2 * H_C * DQK_C), jnp.float32)
    gate_noise = 0.1 * nrm(ks[20], (DEPTH, 2, H_C), jnp.float32)
    inp['c_gate_b'] = gate_noise + jnp.array([0.0, 3.0], jnp.float32)[None, :, None]
    inp['c_out_g'] = 1.0 + 0.02 * nrm(ks[21], (DEPTH, DV_C), jnp.float32)
    return inp

def reference(x_prompt, x_sample, cache_a_kv, cache_b_kv, state_b_win, state_c_conv, state_c_C,
              state_c_n, state_c_m, page_table, norm_g, w_in, w_out, a_qk_g, a_lambda, a_out_g,
              b_qk_g, b_cmp_w, c_conv_w, c_conv_b, c_gate_b, c_out_g):
    weights = (norm_g, w_in, w_out, a_qk_g, a_lambda, a_out_g, b_qk_g, b_cmp_w,
               c_conv_w, c_conv_b, c_gate_b, c_out_g)
    db, n_pages = page_table.shape
    past_len = n_pages * PAGE_SIZE
    win_buf = state_b_win.shape[2]
    hp, hs = x_prompt, x_sample
    new_p = [[] for _ in range(7)]
    new_s = [[] for _ in range(7)]
    for l in range(DEPTH):
        lw = tuple(w[l] for w in weights)
        hp, st_p = mixer_layer(hp, l, lw, None, 0, win_buf)
        past = (cache_a_kv[l][page_table].reshape(db, past_len, 2, H_A, HEAD),
                cache_b_kv[l][page_table].reshape(db, past_len, 4, DH_B),
                state_b_win[l], state_c_conv[l], state_c_C[l], state_c_n[l], state_c_m[l])
        hs, st_s = mixer_layer(hs, l, lw, past, past_len, win_buf)
        for lst, a in zip(new_p, st_p):
            lst.append(a)
        for lst, a in zip(new_s, st_s):
            lst.append(a)
    a_kv_p, b_kv_p, win_p, conv_p, C_p, n_p, m_p = [jnp.stack(lst) for lst in new_p]
    a_kv_s, b_kv_s, win_s, conv_s, C_s, n_s, m_s = [jnp.stack(lst) for lst in new_s]
    return (hp, hs, a_kv_p, a_kv_s, b_kv_p, b_kv_s, win_p, win_s, conv_p, conv_s,
            C_p, C_s, n_p, n_s, m_p, m_s)


_drawn_inputs = setup_inputs


def setup_inputs(seed=0):
    import zlib

    import numpy as np

    out = dict(_drawn_inputs(seed))
    spreads = {}
    factors = {'cache_b_kv': 6.674,
     'a_qk_g': 3.63,
     'a_out_g': 8.0,
     'b_qk_g': 4.117,
     'b_cmp_w': 8.0,
     'c_out_g': 8.0}
    for name, (base, spread) in spreads.items():
        noise = np.random.default_rng([zlib.crc32(name.encode()), seed]).standard_normal(out[name].shape)
        drawn = base * np.exp(spread * noise) if base else spread * noise
        out[name] = __import__('jax').numpy.asarray(drawn.astype(out[name].dtype))
    for name, factor in factors.items():
        out[name] = (out[name] * factor).astype(out[name].dtype)
    return out
```

```python
from contextlib import ExitStack

import concourse.bass as bass
from concourse import mybir

F32 = mybir.dt.float32
I32 = mybir.dt.int32
ACT = mybir.ActivationFunctionType
ALU = mybir.AluOpType
AX_X = mybir.AxisListType.X

P = 128
D = 2048
KC = D // P
SEQ = 512
DB, DT = 8, 4
NS = DB * DT
ROWS = SEQ + NS
PT = SEQ // P
TILES = [(P * t, P) for t in range(PT)] + [(SEQ, NS)]
N_IN = 7964
HEAD = 128
HA, HB, HC = 4, 4, 8
DC = 64
PAGE = 128
PAGES = 32
PAST = PAGE * PAGES
CMP = 64
NBLK = PAST // CMP
WIN = 512
EPS = 1e-6
LAM0 = 0.8 - 0.6
NEG = -1.0e30
A_SCALE = DC ** -0.5
B_SCALE = HEAD ** -0.5

C_AQ, C_AZ, C_BQ, C_BG, C_BZ = 0, 1536, 2048, 3328, 3340
C_CQK, C_CV, C_CIF, C_CO, C_CZ = 3852, 4876, 5900, 5916, 6940
T_AQ, T_AK, T_AV, T_BQ, T_KC = 0, 512, 1024, 1536, 2048
T_VC, T_KS, T_VS, T_KW, T_VW = 2176, 2304, 2432, 2560, 2688
TW = 2816
X_AQ, X_AK, X_BQ, X_KS, X_KW = 0, 4, 8, 12, 13
XCH = 14
X_COL = [T_AQ + HEAD * h for h in range(HA)] + [T_AK + HEAD * h for h in range(HA)] \
    + [T_BQ + HEAD * h for h in range(HB)] + [T_KS, T_KW]
SLAB = 512


class Stage:

    def __init__(self, nc, name):
        self.nc, self.name, self.stack, self.used = nc, name, ExitStack(), []

    def __enter__(self):
        self.stack.__enter__()
        return self

    def __exit__(self, *e):
        if self.used and e[0] is None:
            self.nc.clear_and_free_semaphores(self.used)
            self.nc.all_engine_barrier()
        return self.stack.__exit__(*e)

    def sb(self, name, shape, dt=F32):
        return self.stack.enter_context(self.nc.sbuf_tensor(f"{self.name}_{name}", shape, dt))

    def ps(self, name, shape, dt=F32):
        return self.stack.enter_context(self.nc.psum_tensor(f"{self.name}_{name}", shape, dt))

    def sem(self, name):
        self.used.append(self.nc.alloc_semaphore(f"{self.name}_{name}"))
        return self.used[-1]

    def sems(self, name, n):
        return [self.sem(f"{name}{i}") for i in range(n)]


class Chain:

    def __init__(self, eng, sem):
        self.eng, self.sem, self.n = eng, sem, 0

    def __call__(self, ins):
        self.n += 1
        ins.then_inc(self.sem, 1)
        self.eng.wait_ge(self.sem, self.n)


def project(nc, d, k):
    NSLAB = -(-N_IN // SLAB)
    LAST = N_IN - (NSLAB - 1) * SLAB
    LOOPS = (NSLAB - 4) // 2
    with Stage(nc, "pj") as s:
        x = s.sb("x", [P, 2, D])
        sq = s.sb("sq", [P, D])
        ssq = s.sb("ssq", [P, 8])
        rms = s.sb("rms", [P, 8])
        rstd = s.sb("rstd", [P, 8])
        gain = s.sb("gain", [P, KC])
        eps = s.sb("eps", [P, 1])
        w = s.sb("w", [P, 2, KC, SLAB])
        out = s.sb("out", [P, 5, SLAB])
        ps = [s.ps(f"ps{i}", [P, SLAB]) for i in range(8)]
        xT = s.sb("xT", [P, KC, ROWS])

        x_loaded = s.sems("x_loaded", 2)
        gain_loaded = s.sem("gain_loaded")
        ident_ready = s.sem("ident_ready")
        squared = s.sem("squared")
        rooted = s.sem("rooted")
        inverted = s.sem("inverted")
        scaled = s.sem("scaled")
        turned = s.sem("turned")
        xT_ready = s.sem("xT_ready")
        w_loaded = s.sems("w_loaded", 2)
        product_ready = s.sems("product_ready", 5)
        evacuated = s.sems("evacuated", 5)
        stored = s.sems("stored", 5)
        w_used = s.sem("w_used")
        wv = d.w_in.rearrange("(c p) n -> p c n", p=P)

        with nc.Block() as block:
            @block.sync
            def _(sp):
                def load_x(t):
                    r0, rows = TILES[t]
                    src = d.x_prompt[r0:r0 + rows, :] if t < PT else d.x_sample
                    if t >= 2:
                        sp.wait_ge(turned, 4 * (t - 1))
                    sp.dma_start(x[0:rows, t % 2, :], src).then_inc(x_loaded[t % 2], 16)

                def load_w(j, b, width):
                    sp.dma_start(w[:, b, :, 0:width],
                                 wv[:, :, bass.ds(j * 2 * SLAB + b * SLAB, width)]).then_inc(w_loaded[b], 16)

                def store(j, b, width):
                    for t, (r0, rows) in enumerate(TILES):
                        sp.wait_ge(evacuated[t], j * 2 + b + 2)
                        sp.dma_start(d.proj[r0:r0 + rows, bass.ds(j * 2 * SLAB + b * SLAB, width)],
                                     out[0:rows, t, 0:width]).then_inc(stored[t], 16)

                for t in range(5):
                    sp.sem_inc(stored[t], 16)
                load_x(0)
                load_x(1)
                load_w(0, 0, SLAB)
                for t in range(2, 5):
                    load_x(t)
                load_w(0, 1, SLAB)
                with sp.Fori(0, LOOPS) as j:
                    for b in range(2):
                        store(j, b, SLAB)
                        sp.wait_ge(w_used, j * 2 + b + 1)
                        load_w(j + 1, b, SLAB)
                for j in range(LOOPS, NSLAB // 2):
                    for b in range(2):
                        width = LAST if 2 * j + b == NSLAB - 1 else SLAB
                        store(j, b, width)
                        if 2 * j + b + 2 < NSLAB:
                            sp.wait_ge(w_used, j * 2 + b + 1)
                            load_w(j + 1, b, LAST if 2 * j + b + 3 == NSLAB else SLAB)
                for t in range(5):
                    sp.wait_ge(stored[t], 16 + 16 * NSLAB)

            @block.gpsimd
            def _(pool):
                pool.dma_start(gain[:], d.norm_g.rearrange("(c p) -> p c", p=P),
                               allow_slow_non_contiguous=True).then_inc(gain_loaded, 16)
                pool.memset(eps[:], EPS).then_inc(ident_ready, 1)
                pool.memset(k.ident[:], 0.0).then_inc(ident_ready, 1)
                pool.wait_ge(ident_ready, 2)
                pool.affine_select(out=k.ident[:], in_=k.ident[:], compare_op=ALU.not_equal, fill=1.0,
                                   base=0, pattern=[[-1, P]], channel_multiplier=1).then_inc(ident_ready, 1)

            @block.scalar
            def _(act):
                act.wait_ge(ident_ready, 1)
                for t, (_, rows) in enumerate(TILES):
                    act.wait_ge(x_loaded[t % 2], 16 * (t // 2 + 1))
                    act.activation(sq[0:rows, :], x[0:rows, t % 2, :], ACT.Square,
                                   accum_out=ssq[0:rows, t:t + 1]).then_inc(squared, 1)
                    act.wait_ge(squared, t + 1)
                    act.activation(rms[0:rows, t:t + 1], ssq[0:rows, t:t + 1], ACT.Sqrt,
                                   bias=eps[0:rows, :], scale=1.0 / D).then_inc(rooted, 1)

                def evacuate(j, b, width):
                    for t in (1, 3):
                        rows = TILES[t][1]
                        act.wait_ge(product_ready[t], j * 2 + b + 1)
                        act.wait_ge(stored[t], j * 32 + 16 * b + 16)
                        act.activation(out[0:rows, t, 0:width], ps[t][0:rows, 0:width],
                                       ACT.Copy).then_inc(evacuated[t], 1)

                with act.Fori(0, LOOPS) as j:
                    for b in range(2):
                        evacuate(j, b, SLAB)
                for j in range(LOOPS, NSLAB // 2):
                    for b in range(2):
                        evacuate(j, b, LAST if 2 * j + b == NSLAB - 1 else SLAB)

            @block.vector
            def _(dve):
                for t in range(5):
                    dve.sem_inc(evacuated[t], 1)
                dve.wait_ge(gain_loaded, 16)
                n = 0
                for t, (r0, rows) in enumerate(TILES):
                    dve.wait_ge(rooted, t + 1)
                    dve.reciprocal(rstd[0:rows, t:t + 1], rms[0:rows, t:t + 1]).then_inc(inverted, 1)
                    dve.wait_ge(inverted, t + 1)
                    dve.tensor_scalar(x[0:rows, t % 2, :], x[0:rows, t % 2, :], rstd[0:rows, t:t + 1],
                                      None, ALU.mult).then_inc(scaled, 1)
                    for q in range(4):
                        n += 1
                        dve.wait_ge(turned, n)
                        dve.tensor_tensor(
                            xT[:, 4 * q:4 * q + 4, r0:r0 + rows],
                            ps[n % 2 + 5][:, :].rearrange("p (c r) -> p c r", c=4)[:, :, 0:rows],
                            gain[:, 4 * q:4 * q + 4].unsqueeze(2).broadcast_to([P, 4, rows]),
                            ALU.mult).then_inc(xT_ready, 1)

                def evacuate(j, b, width):
                    for t in (0, 2, 4):
                        rows = TILES[t][1]
                        dve.wait_ge(product_ready[t], j * 2 + b + 1)
                        dve.wait_ge(stored[t], j * 32 + 16 * b + 16)
                        dve.tensor_copy(out[0:rows, t, 0:width],
                                        ps[t][0:rows, 0:width]).then_inc(evacuated[t], 1)

                with dve.Fori(0, LOOPS) as j:
                    for b in range(2):
                        evacuate(j, b, SLAB)
                for j in range(LOOPS, NSLAB // 2):
                    for b in range(2):
                        evacuate(j, b, LAST if 2 * j + b == NSLAB - 1 else SLAB)

            @block.tensor
            def _(pe):
                pe.wait_ge(ident_ready, 3)
                n = 0
                for t, (r0, rows) in enumerate(TILES):
                    pe.wait_ge(scaled, t + 1)
                    for q in range(4):
                        n += 1
                        if n > 2:
                            pe.wait_ge(xT_ready, n - 2)
                        for c in range(4):
                            col = (4 * q + c) * P
                            last = pe.transpose(ps[n % 2 + 5][:, c * P:c * P + rows],
                                                x[0:rows, t % 2, col:col + P], k.ident[0:rows, 0:rows])
                        last.then_inc(turned, 1)

                def multiply(j, b, width):
                    pe.wait_ge(w_loaded[b], j * 16 + 16)
                    for t, (r0, rows) in enumerate(TILES):
                        pe.wait_ge(evacuated[t], j * 2 + b + 1)
                        for c in range(KC):
                            last = pe.matmul(ps[t][0:rows, 0:width], xT[:, c, r0:r0 + rows],
                                             w[:, b, c, 0:width], start=(c == 0), stop=(c == KC - 1))
                        last.then_inc(product_ready[t], 1)
                    pe.wait_ge(product_ready[4], j * 2 + b + 1)
                    pe.sem_inc(w_used, 1)

                pe.wait_ge(xT_ready, 20)
                with pe.Fori(0, LOOPS) as j:
                    for b in range(2):
                        multiply(j, b, SLAB)
                for j in range(LOOPS, NSLAB // 2):
                    for b in range(2):
                        multiply(j, b, LAST if 2 * j + b == NSLAB - 1 else SLAB)


def prepare(nc, d, k):
    with Stage(nc, "pr") as s:
        sq = s.sb("sq", [P, 1792])
        ss = s.sb("ss", [P, 5, 32])
        rms = s.sb("rms", [P, 5, 32])
        rstd = s.sb("rstd", [P, 5, 32])
        eps = s.sb("eps", [P, 1])
        ga = s.sb("ga", [P, 2, DC])
        gb = s.sb("gb", [P, 4, HEAD])
        ps = [s.ps(f"ps{i}", [P, 512]) for i in range(4)]
        tiles_loaded = s.sems("tiles_loaded", 5)
        gains_loaded = s.sem("gains_loaded")
        dve_step = s.sem("dve_step")
        eps_ready = s.sem("eps_ready")
        summed = s.sem("summed")
        rooted = s.sem("rooted")
        normed = s.sem("normed")
        turned = s.sem("turned")
        copied = s.sem("copied")
        stored = s.sem("stored")
        NQ = -(-XCH // 4)

        def tile(t):
            return k.rows_p[:, t, :] if t < PT else k.rows_s[:, :]

        with nc.Block() as block:
            @block.sync
            def _(sp):
                for t, (r0, rows) in enumerate(TILES):
                    sp.dma_start(tile(t)[0:rows, 0:T_BQ], d.proj[r0:r0 + rows, 0:C_AZ]).then_inc(tiles_loaded[t], 16)
                    sp.dma_start(tile(t)[0:rows, T_BQ:TW],
                                 d.proj[r0:r0 + rows, C_BQ:C_BG]).then_inc(tiles_loaded[t], 16)
                n = 0
                for b in range(DB):
                    sp.dma_start(d.win_s[b, 0:WIN - DT, :], d.b_win[b, DT:WIN, :]).then_inc(stored, 16)
                    n += 16
                for t, (r0, rows) in enumerate(TILES):
                    a, b, win = ((d.a_kv_p, d.b_kv_p, d.win_p) if t < PT else (d.a_kv_s, d.b_kv_s, None))
                    q0 = r0 if t < PT else 0
                    sp.wait_ge(normed, t + 1)
                    sp.dma_start(a[q0:q0 + rows, :], tile(t)[0:rows, T_AK:T_BQ]).then_inc(stored, 16)
                    sp.dma_start(b[q0:q0 + rows, :], tile(t)[0:rows, T_KC:T_KW]).then_inc(stored, 16)
                    n += 32
                    if win is not None:
                        sp.dma_start(win[q0:q0 + rows, :], tile(t)[0:rows, T_KW:TW]).then_inc(stored, 16)
                        n += 16
                for b in range(DB):
                    sp.dma_start(d.win_s[b, WIN - DT:WIN, :],
                                 tile(4)[DT * b:DT * b + DT, T_KW:TW]).then_inc(stored, 16)
                    n += 16
                sp.wait_ge(stored, n)

            @block.gpsimd
            def _(pool):
                pool.memset(eps[:], EPS).then_inc(eps_ready, 1)
                pool.dma_start(ga[:], d.a_qk_g.partition_broadcast(P)).then_inc(gains_loaded, 16)
                pool.dma_start(gb[:], d.b_qk_g.partition_broadcast(P)).then_inc(gains_loaded, 16)

            @block.scalar
            def _(act):
                act.wait_ge(eps_ready, 1)
                for t, (r0, rows) in enumerate(TILES):
                    act.wait_ge(summed, t + 1)
                    act.activation(rms[0:rows, t, 0:22], ss[0:rows, t, 0:22], ACT.Sqrt,
                                   bias=eps[0:rows, :]).then_inc(rooted, 1)
                n = 0
                for t, (r0, rows) in enumerate(TILES):
                    for q in range(NQ):
                        m = min(4, XCH - 4 * q)
                        n += 1
                        act.wait_ge(turned, n)
                        act.activation(k.attT[:, 4 * q:4 * q + m, r0:r0 + rows],
                                       ps[n % 4][:, :].rearrange("p (c r) -> p c r", c=4)[:, 0:m, 0:rows],
                                       ACT.Copy).then_inc(copied, 1)

            @block.vector
            def _(dve):
                step = Chain(dve, dve_step)
                dve.wait_ge(gains_loaded, 32)
                step(dve.tensor_scalar(ga[:, 0, :], ga[:, 0, :], A_SCALE, None, ALU.mult))
                step(dve.tensor_scalar(gb[:, 0, :], gb[:, 0, :], B_SCALE, None, ALU.mult))

                def heads(t, rows):
                    T = tile(t)
                    v = lambda c0, n, w: T[0:rows, c0:c0 + n * w].rearrange("p (h w) -> p h w", w=w)
                    return [(v(T_AQ, 8, DC), 0, ga[0:rows, 0, :]), (v(T_AK, 8, DC), 8, ga[0:rows, 1, :]),
                            (v(T_BQ, HB, HEAD), 16, gb[0:rows, 0, :]), (v(T_KS, 1, HEAD), 20, gb[0:rows, 2, :]),
                            (v(T_KW, 1, HEAD), 21, gb[0:rows, 3, :])]

                for t, (r0, rows) in enumerate(TILES):
                    dve.wait_ge(tiles_loaded[t], 32)
                    if t:
                        dve.wait_ge(dve_step, step.n)
                    at = 0
                    for v, c, _ in heads(t, rows):
                        n, w = v.shape[1], v.shape[2]
                        last = dve.tensor_tensor(sq[0:rows, at:at + n * w].rearrange("p (h w) -> p h w", w=w),
                                                 v, v, ALU.mult)
                        at += n * w
                        step(last)
                    step(dve.tensor_reduce(ss[0:rows, t, 0:16], sq[0:rows, 0:1024].rearrange(
                        "p (h w) -> p h w", w=DC), AX_X, ALU.add))
                    step(dve.tensor_reduce(ss[0:rows, t, 16:22], sq[0:rows, 1024:1792].rearrange(
                        "p (h w) -> p h w", w=HEAD), AX_X, ALU.add))
                    step(dve.tensor_scalar(ss[0:rows, t, 0:16], ss[0:rows, t, 0:16], 1.0 / DC, None, ALU.mult))
                    dve.tensor_scalar(ss[0:rows, t, 16:22], ss[0:rows, t, 16:22], 1.0 / HEAD, None,
                                      ALU.mult).then_inc(summed, 1)
                for t, (r0, rows) in enumerate(TILES):
                    dve.wait_ge(rooted, t + 1)
                    step(dve.reciprocal(rstd[0:rows, t, 0:22], rms[0:rows, t, 0:22]))
                    parts = heads(t, rows)
                    for v, c, _ in parts:
                        n, w = v.shape[1], v.shape[2]
                        step(dve.tensor_tensor(v, v, rstd[0:rows, t, c:c + n].unsqueeze(2).broadcast_to(
                            [rows, n, w]), ALU.mult))
                    for i, (v, c, g) in enumerate(parts):
                        n, w = v.shape[1], v.shape[2]
                        last = dve.tensor_tensor(v, v, g.unsqueeze(1).broadcast_to([rows, n, w]), ALU.mult)
                        if i < len(parts) - 1:
                            step(last)
                    last.then_inc(normed, 1)

            @block.tensor
            def _(pe):
                n = 0
                for t, (r0, rows) in enumerate(TILES):
                    pe.wait_ge(normed, t + 1)
                    for q in range(NQ):
                        n += 1
                        if n > 4:
                            pe.wait_ge(copied, n - 4)
                        for c in range(4 * q, min(4 * q + 4, XCH)):
                            last = pe.transpose(ps[n % 4][:, (c % 4) * P:(c % 4) * P + rows],
                                                tile(t)[0:rows, X_COL[c]:X_COL[c] + P],
                                                k.ident[0:rows, 0:rows])
                        last.then_inc(turned, 1)


def constants(nc, d, k):
    with Stage(nc, "ct") as s:
        lp = s.sb("lp", [P, 4, DC])
        prod = s.sb("prod", [P, 2, DC])
        dots = s.sb("dots", [P, 2])
        exps = s.sb("exps", [P, 2])
        loaded = s.sem("loaded")
        zeroed = s.sem("zeroed")
        made = s.sem("made")
        dve_step = s.sem("dve_step")
        dotted = s.sem("dotted")
        exped = s.sem("exped")
        with nc.Block() as block:
            @block.gpsimd
            def _(pool):
                pool.memset(k.eps[:], EPS).then_inc(made, 1)
                pool.memset(k.ones[:], 1.0).then_inc(made, 1)
                pool.memset(k.causal[:], 0.0).then_inc(zeroed, 1)
                pool.memset(k.poolw[:], 0.0).then_inc(zeroed, 1)
                pool.wait_ge(zeroed, 2)
                pool.affine_select(out=k.causal[:], in_=k.causal[:], compare_op=ALU.is_ge, fill=NEG,
                                   base=0, pattern=[[-1, P]], channel_multiplier=1).then_inc(made, 1)
                for a in range(2):
                    for j in range(2):
                        pool.dma_start(k.poolw[CMP * j:CMP * (j + 1), a, j:j + 1],
                                       d.b_cmp_w[a, :].unsqueeze(1)).then_inc(loaded, 16)
                pool.dma_start(lp[:], d.a_lambda.partition_broadcast(P)).then_inc(loaded, 16)
                pool.dma_start(k.g_kc[:], d.b_qk_g[1, :].unsqueeze(1)).then_inc(loaded, 16)
                pool.wait_ge(made, 3)
                pool.wait_ge(loaded, 96)

            @block.vector
            def _(dve):
                step = Chain(dve, dve_step)
                dve.wait_ge(loaded, 96)
                step(dve.tensor_tensor(prod[:], lp[:, 0:4:2, :], lp[:, 1:4:2, :], ALU.mult))
                dve.tensor_reduce(dots[:], prod[:], AX_X, ALU.add).then_inc(dotted, 1)
                dve.wait_ge(exped, 1)
                step(dve.tensor_tensor(k.neglam[:], exps[:, 1:2], exps[:, 0:1], ALU.subtract))
                step(dve.tensor_scalar(k.neglam[:], k.neglam[:], -LAM0, None, ALU.add))

            @block.scalar
            def _(act):
                act.wait_ge(dotted, 1)
                act.activation(exps[:], dots[:], ACT.Exp).then_inc(exped, 1)


def prompt_attend(nc, d, k):
    units = []
    for t in range(PT):
        for h in range(HA):
            units += [(t, 0, X_AK + h, X_AQ + h, DC * c, T_AV + HEAD * h) for c in range(2)]
        units += [(t, 1, X_KS, X_BQ + h, 0, T_VS) for h in range(HB)]
        units += [(t, 2, X_KW, X_BQ + h, 0, T_VW) for h in range(HB)]
    pvs = []
    for u, (t, sec, _, _, p0, vcol) in enumerate(units):
        if sec == 0 and p0 == 0:
            continue
        head = (u % 16) // 2 if sec == 0 else (u % 16) % 4
        pvs.append((u, t, sec, head, vcol))
    NU, NV = len(units), len(pvs)
    NSEC = 3 * PT
    with Stage(nc, "pa") as s:
        e = s.sb("e", [P, 6, 512])
        w = s.sb("w", [P, 2, 512])
        wT = s.sb("wT", [P, 2, 4, P])
        nm = s.sb("nm", [P, NU])
        l = s.sb("l", [P, NU])
        r = s.sb("r", [P, NU])
        o = s.sb("o", [P, 2, 512])
        scores = [s.ps(f"scores{i}", [P, 512]) for i in range(3)]
        tp = [s.ps(f"tp{i}", [P, 4, P]) for i in range(2)]
        po = [s.ps(f"po{i}", [P, 4, HEAD]) for i in range(3)]
        scored = s.sem("scored")
        maxed = s.sem("maxed")
        exped = s.sem("exped")
        inverted = s.sem("inverted")
        divisors = s.sem("divisors")
        weighted = s.sem("weighted")
        scaled = s.sem("scaled")
        turned = s.sem("turned")
        copied = s.sem("copied")
        summed = s.sem("summed")
        finished = s.sem("finished")
        stored = s.sems("stored", 2)
        NA = [sum(1 for v in pvs[:i] if v[2] == 0) for i in range(NV + 1)]

        with nc.Block() as block:
            @block.sync
            def _(sp):
                for c in range(NSEC):
                    t, sec = c // 3, c % 3
                    sp.wait_ge(finished, c + 1)
                    sp.dma_start(d.o_att[P * t:P * t + P, 512 * sec:512 * sec + 512],
                                 o[:, c % 2, :]).then_inc(stored[c % 2], 16)
                for b in range(2):
                    sp.wait_ge(stored[b], 8 * NSEC)

            @block.tensor
            def _(pe):
                def score(u):
                    t, sec, kc, qc, p0, _ = units[u]
                    kn = DC if sec == 0 else P
                    n = P * (t + 1)
                    if u >= 3:
                        pe.wait_ge(exped, u - 2)
                    pe.matmul(scores[u % 3][:, 0:n], k.attT[p0:p0 + kn, qc, P * t:P * t + P],
                              k.attT[p0:p0 + kn, kc, 0:n], start=True, stop=False)
                    pe.matmul(scores[u % 3][:, n - P:n], k.ident[:], k.causal[:], start=False,
                              stop=True).then_inc(scored, 1)

                def turn(i):
                    u, t, sec, h, _ = pvs[i]
                    if sec == 0:
                        pe.wait_ge(weighted, NA[i] + 1)
                        src = w[:, NA[i] % 2, :]
                    else:
                        pe.wait_ge(exped, u + 1)
                        src = e[:, u % 6, :]
                    if i >= 2:
                        pe.wait_ge(copied, i - 1)
                    for b in range(t + 1):
                        last = pe.transpose(tp[i % 2][:, b, :], src[:, P * b:P * b + P], k.ident[:])
                    last.then_inc(turned, 1)

                def attend(i):
                    u, t, sec, h, vcol = pvs[i]
                    c = 3 * t + sec
                    if h == 0 and c >= 3:
                        pe.wait_ge(finished, c - 2)
                    pe.wait_ge(copied, i + 1)
                    for b in range(t + 1):
                        last = pe.matmul(po[c % 3][:, h, :], wT[:, i % 2, b, :],
                                         k.rows_p[:, b, vcol:vcol + HEAD], start=(b == 0), stop=(b == t))
                    last.then_inc(summed, 1)

                done = 0
                for i in range(NV + 2):
                    if i < NV:
                        while done <= min(pvs[i][0] + 1, NU - 1):
                            score(done)
                            done += 1
                    if 1 <= i <= NV:
                        turn(i - 1)
                    if i >= 2:
                        attend(i - 2)

            @block.scalar
            def _(act):
                for u in range(NU):
                    t = units[u][0]
                    n = P * (t + 1)
                    act.wait_ge(maxed, u + 1)
                    if u >= 6:
                        act.wait_ge(turned, sum(1 for v in pvs if v[0] <= u - 6))
                        act.wait_ge(weighted, sum(1 for v in pvs if v[2] == 0 and v[0] <= u - 5))
                    act.activation(e[:, u % 6, 0:n], scores[u % 3][:, 0:n], ACT.Exp, bias=nm[:, u:u + 1],
                                   accum_out=l[:, u:u + 1]).then_inc(exped, 1)

            @block.vector
            def _(dve):
                def row_max(u):
                    n = P * (units[u][0] + 1)
                    dve.wait_ge(scored, u + 1)
                    dve.tensor_reduce(nm[:, u:u + 1], scores[u % 3][:, 0:n], AX_X, ALU.max,
                                      negate=True).then_inc(maxed, 1)

                def weigh(i):
                    u, t, _, _, _ = pvs[i]
                    n = P * (t + 1)
                    a = NA[i]
                    dve.wait_ge(exped, u + 1)
                    dve.reciprocal(r[:, u - 1:u + 1], l[:, u - 1:u + 1]).then_inc(inverted, 1)
                    dve.wait_ge(inverted, 2 * a + 1)
                    if i >= 2 and a >= 2:
                        j = next(x for x in range(NV) if NA[x] == a - 2 and pvs[x][2] == 0)
                        dve.wait_ge(turned, j + 1)
                    dve.tensor_scalar(w[:, a % 2, 0:n], e[:, (u - 1) % 6, 0:n], r[:, u - 1:u], None,
                                      ALU.mult).then_inc(scaled, 1)
                    dve.tensor_scalar(r[:, u:u + 1], r[:, u:u + 1], k.neglam[:, 0:1], None,
                                      ALU.mult).then_inc(inverted, 1)
                    dve.wait_ge(scaled, a + 1)
                    dve.wait_ge(inverted, 2 * a + 2)
                    dve.scalar_tensor_tensor(w[:, a % 2, 0:n], e[:, u % 6, 0:n], r[:, u:u + 1],
                                             w[:, a % 2, 0:n], ALU.mult, ALU.add).then_inc(weighted, 1)

                def copy(i):
                    t = pvs[i][1]
                    dve.wait_ge(turned, i + 1)
                    if i >= 2:
                        dve.wait_ge(summed, i - 1)
                    dve.tensor_copy(wT[:, i % 2, 0:t + 1, :], tp[i % 2][:, 0:t + 1, :]).then_inc(copied, 1)

                def finish(i):
                    u, t, sec, h, _ = pvs[i]
                    c = 3 * t + sec
                    dve.wait_ge(summed, i + 1)
                    if c >= 2:
                        dve.wait_ge(stored[c % 2], 16 * (c // 2))
                    out = o[:, c % 2, :].rearrange("p (h w) -> p h w", h=4)
                    if sec == 0:
                        dve.tensor_copy(out, po[c % 3][:]).then_inc(finished, 1)
                        return
                    dve.wait_ge(exped, u + 1)
                    dve.reciprocal(r[:, u - 3:u + 1], l[:, u - 3:u + 1]).then_inc(divisors, 1)
                    dve.wait_ge(divisors, 2 * t + sec)
                    dve.tensor_tensor(out, po[c % 3][:], r[:, u - 3:u + 1].unsqueeze(2).broadcast_to(
                        [P, 4, HEAD]), ALU.mult).then_inc(finished, 1)

                done = 0
                for i in range(NV + 3):
                    if i < NV:
                        while done <= min(pvs[i][0] + 1, NU - 1):
                            row_max(done)
                            done += 1
                        if pvs[i][2] == 0:
                            weigh(i)
                    if 1 <= i <= NV:
                        copy(i - 1)
                    if i >= 3 and pvs[i - 3][3] == 3:
                        finish(i - 3)


def compress(nc, d, k):
    NG = PAGES // 4
    with Stage(nc, "cm") as s:
        pages = s.sb("pages", [P, 4, 4, 2 * HEAD])
        table = s.sb("table", [1, DB * PAGES], I32)
        z = s.sb("z", [P, 3 * NBLK - 2])
        kc = s.sb("kc", [NBLK, DB + 1, HEAD])
        vc = s.sb("vc", [NBLK, DB + 1, HEAD])
        sq = s.sb("sq", [NBLK, DB + 1, HEAD])
        ss = s.sb("ss", [NBLK, 3, DB + 1])
        g = s.sb("g", [NBLK, HEAD])
        kcT = s.sb("kcT", [P, DB + 1, NBLK])
        qpad = s.sb("qpad", [P, DB * 144])
        same = s.sb("same", [P, P])
        shift = s.sb("shift", [P, 176])
        mul = s.sb("mul", [P, PT, 8])
        bias = s.sb("bias", [P, PT, 8])
        st = s.sb("st", [P, 8, 16])
        pc = s.sb("pc", [P, PT * HB, 8])
        pcT = s.sb("pcT", [8, PT, HB, P])
        pd = s.sb("pd", [P, NBLK])
        imp = s.sb("imp", [P, 3, NBLK])
        top = s.sb("top", [P, 2, 8])
        pdT = s.sb("pdT", [NBLK, HB, 288])
        o = s.sb("o", [P, 2, 512])
        acc = s.ps("acc", [P, 2 * HEAD])
        tp = [s.ps(f"tp{i}", [P, 512]) for i in range(2)]
        sc = s.ps("sc", [P, 512])
        sd = s.ps("sd", [P, 512])
        po = [s.ps(f"po{i}", [P, HB, HEAD]) for i in range(2)]

        table_loaded = s.sem("table_loaded")
        loaded = s.sems("loaded", 4)
        used = s.sems("used", 4)
        pooled = s.sem("pooled")
        drained = s.sem("drained")
        g_loaded = s.sem("g_loaded")
        zeroed = s.sem("zeroed")
        z_ready = s.sem("z_ready")
        masks_ready = s.sem("masks_ready")
        dve_step = s.sem("dve_step")
        summed = s.sem("summed")
        rooted = s.sem("rooted")
        normed = s.sem("normed")
        turned = s.sem("turned")
        copied = s.sem("copied")
        qpad_ready = s.sem("qpad_ready")
        p_scored, p_centred, p_exped, p_ready = (s.sem(n) for n in ("p_scored", "p_centred", "p_exped", "p_ready"))
        p_turned, p_copied, p_summed, p_out = (s.sem(n) for n in ("p_turned", "p_copied", "p_summed", "p_out"))
        p_stored = s.sems("p_stored", 2)
        d_scored, d_maxed, d_exped, d_ready = (s.sem(n) for n in ("d_scored", "d_maxed", "d_exped", "d_ready"))
        imp_ready, d_turned, d_copied, d_summed, d_out = (
            s.sem(n) for n in ("imp_ready", "d_turned", "d_copied", "d_summed", "d_out"))
        d_stored = s.sem("d_stored")
        chosen, moved, bias_out = (s.sem(n) for n in ("chosen", "moved", "bias_out"))

        with nc.Block() as block:
            @block.sync
            def _(sp):
                sp.dma_start(table[:], d.page_table.rearrange("(a b) n -> a (b n)", a=1)).then_inc(table_loaded, 16)
                for i in range(4):
                    sp.sem_inc(used[i], 1)
                sp.wait_ge(table_loaded, 16)
                with sp.Fori(0, DB) as b:
                    for q in range(NG):
                        sp.wait_ge(used[q % 4], b * 2 + q // 4 + 1)
                        for i in range(4):
                            page = sp.value_load(table[0:1, bass.ds(b * PAGES + 4 * q + i, 1)],
                                                 min_val=0, max_val=d.cache_b.shape[0] - 1)
                            sp.dma_start(pages[:, q % 4, i, :], d.cache_b[bass.ds(page, 1), :, 0:2 * HEAD]
                                         .rearrange("a p n -> p (a n)")).then_inc(loaded[q % 4], 16)
                sp.wait_ge(d_out, 1)
                sp.dma_start(d.o_att[SEQ:ROWS, 1536:2048], o[0:NS, 0, :]).then_inc(d_stored, 16)
                for t in range(PT):
                    sp.wait_ge(p_out, t + 1)
                    sp.dma_start(d.o_att[P * t:P * t + P, 1536:2048], o[:, t % 2, :]).then_inc(p_stored[t % 2], 16)
                for i in range(2):
                    sp.wait_ge(p_stored[i], 16 * PT // 2)
                sp.wait_ge(d_stored, 16)

            @block.gpsimd
            def _(pool):
                pool.dma_start(g[:], d.b_qk_g[1, :].partition_broadcast(NBLK)).then_inc(g_loaded, 16)
                pool.memset(z[:], 0.0).then_inc(zeroed, 1)
                pool.memset(qpad[:], 0.0).then_inc(zeroed, 1)
                pool.memset(pdT[:], 0.0).then_inc(zeroed, 1)
                pool.memset(same[:], 0.0).then_inc(zeroed, 1)
                pool.memset(shift[:], 0.0).then_inc(zeroed, 1)
                pool.memset(mul[:], 1.0).then_inc(zeroed, 1)
                pool.wait_ge(zeroed, 6)
                for a in range(2):
                    pool.tensor_copy(z[:, NBLK * (a + 1) - 2:NBLK * (a + 1)], k.poolw[:, a, :]).then_inc(z_ready, 1)
                pool.affine_select(out=shift[:], in_=shift[:], compare_op=ALU.not_equal, fill=1.0,
                                   base=32, pattern=[[-1, 176]], channel_multiplier=1).then_inc(masks_ready, 1)
                pool.affine_select(out=mul[:], in_=mul[:], compare_op=ALU.is_ge, fill=0.0, base=-CMP,
                                   pattern=[[P, PT], [-CMP, 8]], channel_multiplier=1).then_inc(masks_ready, 1)
                n = 2
                for h in range(1 - HB, HB):
                    pool.affine_select(out=same[:], in_=same[:], compare_op=ALU.not_equal, fill=1.0,
                                       base=DT * h, pattern=[[-1, P]], channel_multiplier=1).then_inc(masks_ready, 1)
                    n += 1
                    pool.wait_ge(masks_ready, n)
                v = same[:].rearrange("p (b r) -> p b r", b=DB)
                pool.affine_select(out=v, in_=v, compare_op=ALU.is_ge, fill=0.0, base=0,
                                   pattern=[[-16, DB], [0, 16]], channel_multiplier=1).then_inc(masks_ready, 1)
                pool.wait_ge(masks_ready, n + 1)
                pool.affine_select(out=v, in_=v, compare_op=ALU.is_ge, fill=0.0, base=15,
                                   pattern=[[16, DB], [0, 16]], channel_multiplier=-1).then_inc(masks_ready, 1)

            @block.tensor
            def _(pe):
                pe.wait_ge(z_ready, 2)
                with pe.Fori(0, DB) as b:
                    pe.wait_ge(drained, b * 2 + 2)
                    for q in range(NG):
                        pe.wait_ge(loaded[q % 4], b * 128 + 64 * (q // 4) + 64)
                        for i in range(4):
                            p = 4 * q + i
                            last = pe.matmul(acc[:], z[:, NBLK - 2 - 2 * p:3 * NBLK - 2 - 2 * p],
                                             pages[:, q % 4, i, :], start=(p == 0), stop=(p == PAGES - 1))
                        last.then_inc(used[q % 4], 1)
                    pe.wait_ge(used[3], b * 2 + 3)
                    pe.sem_inc(pooled, 1)
                pe.wait_ge(drained, 2 * DB + 2)
                for p in range(PT):
                    last = pe.matmul(acc[:], z[:, NBLK - 2 - 2 * p:3 * NBLK - 2 - 2 * p],
                                     k.rows_p[:, p, T_KC:T_KC + 2 * HEAD], start=(p == 0), stop=(p == PT - 1))
                last.then_inc(pooled, 1)
                pe.wait_ge(normed, 1)
                for b in range(DB + 1):
                    i = b // 8
                    last = pe.transpose(tp[i][:, NBLK * (b % 8):NBLK * (b % 8) + NBLK], kc[:, b, :],
                                        k.ident[0:NBLK, 0:NBLK])
                last.then_inc(turned, 1)
                pe.wait_ge(copied, 1)
                for t in range(PT):
                    for h in range(HB):
                        c = 8 * (HB * t + h)
                        last = pe.matmul(sc[:, c:c + 8], k.attT[:, X_BQ + h, P * t:P * t + P],
                                         kcT[:, DB, 0:8], start=True, stop=True)
                last.then_inc(p_scored, 1)
                pe.wait_ge(qpad_ready, 1)
                for b in range(DB):
                    last = pe.matmul(sd[:, 0:NBLK], qpad[:, P * b:P * b + P], kcT[:, b, :],
                                     start=(b == 0), stop=(b == DB - 1))
                last.then_inc(d_scored, 1)
                pe.wait_ge(masks_ready, 11)
                pe.wait_ge(d_ready, 1)
                pe.matmul(sd[:, 128:128 + NBLK], same[:], pd[:], start=True, stop=True).then_inc(imp_ready, 1)
                pe.transpose(tp[0][0:NBLK, 0:P], pd[:], k.ident[:]).then_inc(d_turned, 1)
                pe.wait_ge(d_copied, 1)
                for h in range(HB):
                    for b in range(DB):
                        last = pe.matmul(po[0][0:NS, h, :], pdT[:, h, NS * b:NS * b + NS], vc[:, b, :],
                                         start=(b == 0), stop=(b == DB - 1))
                last.then_inc(d_summed, 1)
                pe.wait_ge(chosen, 1)
                for b in range(DB):
                    last = pe.matmul(tp[1][0:NBLK, NBLK * b:NBLK * b + NBLK], shift[:, 16 * b:16 * b + 64],
                                     imp[:, 2, :], start=True, stop=True)
                last.then_inc(moved, 1)
                pe.wait_ge(p_ready, 1)
                for t in range(PT):
                    if t == 0:
                        pe.wait_ge(d_copied, 1)
                    else:
                        pe.wait_ge(p_copied, t)
                    for h in range(HB):
                        last = pe.transpose(tp[0][0:8, P * h:P * h + P], pc[:, HB * t + h, :], k.ident[:])
                    last.then_inc(p_turned, 1)
                    pe.wait_ge(p_copied, t + 1)
                    pe.wait_ge(p_out, t) if t >= 1 else pe.wait_ge(d_out, 1)
                    for h in range(HB):
                        last = pe.matmul(po[t % 2][:, h, :], pcT[:, t, h, :], vc[0:8, DB, :], start=True, stop=True)
                    last.then_inc(p_summed, 1)

            @block.scalar
            def _(act):
                act.sem_inc(drained, 1)
                with act.Fori(0, DB) as b:
                    act.wait_ge(pooled, b + 1)
                    act.activation(kc[:, bass.ds(b, 1), :], acc[0:NBLK, 0:HEAD].unsqueeze(1), ACT.Copy).then_inc(drained, 1)
                    act.activation(vc[:, bass.ds(b, 1), :], acc[NBLK:P, HEAD:2 * HEAD].unsqueeze(1),
                                   ACT.Copy).then_inc(drained, 1)
                act.wait_ge(pooled, DB + 1)
                act.activation(kc[:, DB, :], acc[0:NBLK, 0:HEAD], ACT.Copy).then_inc(drained, 1)
                act.activation(vc[:, DB, :], acc[NBLK:P, HEAD:2 * HEAD], ACT.Copy).then_inc(drained, 1)
                act.wait_ge(summed, 1)
                act.activation(ss[:, 1, :], ss[:, 0, :], ACT.Sqrt, bias=k.eps[0:NBLK, :],
                               scale=1.0 / HEAD).then_inc(rooted, 1)
                act.wait_ge(p_centred, 1)
                act.activation(pc[:], pc[:], ACT.Exp).then_inc(p_exped, 1)
                act.wait_ge(d_maxed, 1)
                act.activation(pd[:], sd[:, 0:NBLK], ACT.Exp, bias=st[:, 4, 0:1],
                               accum_out=st[:, 5, 0:1]).then_inc(d_exped, 1)

            @block.vector
            def _(dve):
                step = Chain(dve, dve_step)
                dve.sem_inc(drained, 1)
                step(dve.memset(k.selb[0:32, :, :], 0.0))
                step(dve.memset(k.selb[32:64, :, :], NEG))
                dve.wait_ge(zeroed, 6)
                dve.tensor_copy(qpad[:].rearrange("p (b x) -> p b x", x=144)[:, :, 0:16].rearrange(
                    "p b (h t) -> p b h t", h=HB),
                    k.attT[:, X_BQ:X_BQ + HB, SEQ:ROWS].rearrange("p h (b t) -> p b h t", b=DB)).then_inc(qpad_ready, 1)
                dve.wait_ge(masks_ready, 2)
                step(dve.tensor_scalar(bias[:], mul[:], -1.0, -NEG, ALU.add, ALU.mult))
                dve.wait_ge(g_loaded, 16)
                dve.wait_ge(drained, 2 * DB + 4)
                step(dve.tensor_tensor(sq[:], kc[:], kc[:], ALU.mult))
                dve.tensor_reduce(ss[:, 0, :], sq[:], AX_X, ALU.add).then_inc(summed, 1)
                dve.wait_ge(rooted, 1)
                step(dve.reciprocal(ss[:, 2, :], ss[:, 1, :]))
                step(dve.tensor_tensor(kc[:], kc[:], ss[:, 2, :].unsqueeze(2).broadcast_to(
                    [NBLK, DB + 1, HEAD]), ALU.mult))
                dve.tensor_tensor(kc[:], kc[:], g[:].unsqueeze(1).broadcast_to([NBLK, DB + 1, HEAD]),
                                  ALU.mult).then_inc(normed, 1)
                dve.wait_ge(turned, 1)
                step(dve.tensor_copy(kcT[:, 0:8, :], tp[0][:].rearrange("p (b n) -> p b n", b=8)))
                dve.tensor_copy(kcT[:, 8, :], tp[1][:, 0:NBLK]).then_inc(copied, 1)
                dve.wait_ge(p_scored, 1)
                step(dve.tensor_tensor(pc[:].rearrange("p (t h) n -> p t h n", t=PT),
                                       sc[:, 0:128].rearrange("p (t h n) -> p t h n", t=PT, h=HB),
                                       bias[:].unsqueeze(2).broadcast_to([P, PT, HB, 8]), ALU.add))
                step(dve.tensor_reduce(st[:, 0, :], pc[:], AX_X, ALU.max))
                dve.tensor_tensor(pc[:], pc[:], st[:, 0, :].unsqueeze(2).broadcast_to([P, 16, 8]),
                                  ALU.subtract).then_inc(p_centred, 1)
                dve.wait_ge(d_scored, 1)
                dve.tensor_reduce(st[:, 4, 0:1], sd[:, 0:NBLK], AX_X, ALU.max, negate=True).then_inc(d_maxed, 1)
                dve.wait_ge(p_exped, 1)
                step(dve.tensor_tensor(pc[:].rearrange("p (t h) n -> p t h n", t=PT),
                                       pc[:].rearrange("p (t h) n -> p t h n", t=PT),
                                       mul[:].unsqueeze(2).broadcast_to([P, PT, HB, 8]), ALU.mult))
                step(dve.tensor_reduce(st[:, 1, :], pc[:], AX_X, ALU.add))
                step(dve.tensor_scalar(st[:, 2, :], st[:, 1, :], 1e-30, None, ALU.max))
                step(dve.reciprocal(st[:, 3, :], st[:, 2, :]))
                dve.tensor_tensor(pc[:], pc[:], st[:, 3, :].unsqueeze(2).broadcast_to([P, 16, 8]),
                                  ALU.mult).then_inc(p_ready, 1)
                dve.wait_ge(d_exped, 1)
                step(dve.reciprocal(st[:, 6, 0:1], st[:, 5, 0:1]))
                dve.tensor_scalar(pd[:], pd[:], st[:, 6, 0:1], None, ALU.mult).then_inc(d_ready, 1)
                dve.wait_ge(imp_ready, 1)
                dve.wait_ge(d_turned, 1)
                step(dve.tensor_copy(imp[:, 0, :], sd[:, 128:128 + NBLK]))
                dve.tensor_copy(pdT[:, :, :].rearrange("p h (b x) -> p h b x", x=36)[:, :, :, 0:DT],
                                tp[0][0:NBLK, 0:P].rearrange("p (b h t) -> p h b t", b=DB, h=HB)).then_inc(d_copied, 1)
                step(dve.max(top[:, 0, :], imp[:, 0, :]))
                step(dve.match_replace(imp[:, 1, :], top[:, 0, :], imp[:, 0, :], -1.0))
                step(dve.max(top[:, 1, :], imp[:, 1, :]))
                step(dve.match_replace(imp[:, 0, :], top[:, 1, :], imp[:, 1, :], -1.0))
                dve.tensor_scalar(imp[:, 2, :], imp[:, 0, :], 0.0, NEG, ALU.is_ge, ALU.mult).then_inc(chosen, 1)
                dve.wait_ge(d_summed, 1)
                dve.tensor_copy(o[0:NS, 0, :].rearrange("p (h w) -> p h w", h=HB), po[0][0:NS, :, :]).then_inc(d_out, 1)
                dve.wait_ge(moved, 1)
                dve.tensor_copy(k.selb[32:48, :, :], tp[1][32:48, 0:512].rearrange("p (b n) -> p b n", b=DB)) \
                    .then_inc(bias_out, 1)
                dve.wait_ge(bias_out, 1)
                for t in range(PT):
                    dve.wait_ge(p_turned, t + 1)
                    dve.tensor_copy(pcT[:, t, :, :], tp[0][0:8, :].rearrange("p (h r) -> p h r", h=HB)).then_inc(p_copied, 1)
                    dve.wait_ge(p_summed, t + 1)
                    if t == 0:
                        dve.wait_ge(d_stored, 16)
                    elif t >= 2:
                        dve.wait_ge(p_stored[t % 2], 16)
                    dve.tensor_copy(o[:, t % 2, :].rearrange("p (h w) -> p h w", h=HB), po[t % 2][:]).then_inc(p_out, 1)


def decode_attend(nc, d, k):
    NG = PAGES // 4
    WING, NEWG, G = NG, NG + 1, NG + 2
    R = 64
    HEADS = HA + 2
    batches = [(g, j) for g in range(NG) for j in range(HA + 1)] + [(WING, HA + 1)]
    NT = len(batches)
    uses = [len(range(r, NT, 3)) for r in range(3)]
    first_row = [8 * h for h in range(HA)] + [32 + 4 * h for h in range(HB)] + [48 + 4 * h for h in range(HB)]
    with Stage(nc, "da") as s:
        table = s.sb("table", [1, DB * PAGES], I32)
        pa = s.sb("pa", [P, 4, 4, 1024])
        pb = s.sb("pb", [P, 4, 4, 256])
        pw = s.sb("pw", [P, 4, 256])
        kT = s.sb("kT", [P, 3, 512])
        q = s.sb("q", [P, HEADS * R])
        sb_ = s.sb("scores", [R, 2, 512])
        e = s.sb("e", [R, 2, 512])
        pT = s.sb("pT", [P, 2, 4, HEADS * R])
        winb = s.sb("winb", [R, 512])
        newb = s.sb("newb", [R, DB, NS])
        nm = s.sb("nm", [R, G])
        l = s.sb("l", [R, G])
        wt = s.sb("wt", [R, 4, G])
        st = s.sb("st", [R, 8])
        ob = s.sb("ob", [R, G, HEAD])
        oall = s.sb("oall", [R, DB, HEAD])
        coef = s.sb("coef", [R, 2])
        hot = s.sb("hot", [8, 2, R])
        late = s.sb("late", [8, DB * NS + 8])
        sel = s.sb("sel", [R, 12, 60])
        o = s.sb("o", [NS, 3, 512])
        tp = [s.ps(f"tp{i}", [P, 4, P]) for i in range(3)]
        ps = [s.ps(f"ps{i}", [R, 512]) for i in range(2)]
        pt = s.ps("pt", [P, 4, R])
        po = [s.ps(f"po{i}", [R, HEAD]) for i in range(2)]

        table_loaded = s.sem("table_loaded")
        loaded = s.sems("loaded", 4)
        win_loaded = s.sem("win_loaded")
        win_used = s.sem("win_used")
        zeroed = s.sem("zeroed")
        made = s.sem("made")
        spread = s.sem("spread")
        dve_step = s.sem("dve_step")
        consts_ready = s.sem("consts_ready")
        q_ready = s.sem("q_ready")
        turned = s.sem("turned")
        copied = s.sems("copied", 3)
        multiplied = s.sem("multiplied")
        scored = s.sem("scored")
        added = s.sem("added")
        maxed = s.sem("maxed")
        exped = s.sem("exped")
        turning = s.sem("turning")
        p_turned = s.sem("p_turned")
        p_copied = s.sem("p_copied")
        summed = s.sem("summed")
        o_copied = s.sem("o_copied")
        minned = s.sem("minned")
        weighed = s.sem("weighed")
        combined = s.sem("combined")
        gathered = s.sem("gathered")
        out_ready = s.sem("out_ready")
        stored = s.sem("stored")

        with nc.Block() as block:
            @block.sync
            def _(sp):
                sp.dma_start(table[:], d.page_table.rearrange("(a b) n -> a (b n)", a=1)).then_inc(table_loaded, 16)
                sp.sem_inc(win_used, 1)
                sp.wait_ge(table_loaded, 16)
                with sp.Fori(0, DB) as b:
                    for g in range(NG):
                        sp.wait_ge(summed, b * G + g + (3 if g >= 4 else 1))
                        for i in range(4):
                            page = sp.value_load(table[0:1, bass.ds(b * PAGES + 4 * g + i, 1)],
                                                 min_val=0, max_val=d.cache_b.shape[0] - 1)
                            sp.dma_start(pa[:, g % 4, i, :], d.cache_a[bass.ds(page, 1), :, :]
                                         .rearrange("a p n -> p (a n)")).then_inc(loaded[g % 4], 16)
                            sp.dma_start(pb[:, g % 4, i, :], d.cache_b[bass.ds(page, 1), :, 256:512]
                                         .rearrange("a p n -> p (a n)")).then_inc(loaded[g % 4], 16)
                        if g == 4:
                            sp.wait_ge(win_used, b + 1)
                            sp.dma_start(pw[:], d.b_win[bass.ds(b, 1), :, :].rearrange(
                                "a (i p) n -> p (a i) n", p=P)).then_inc(win_loaded, 16)
                sp.wait_ge(out_ready, 1)
                sp.dma_start(d.o_att[SEQ:ROWS, 0:1536], o[:].rearrange("p a n -> p (a n)")).then_inc(stored, 16)
                sp.wait_ge(stored, 16)

            @block.gpsimd
            def _(pool):
                for v in (q, pT, winb, hot, late, sel):
                    pool.memset(v[:], 0.0).then_inc(zeroed, 1)
                pool.wait_ge(zeroed, 6)
                pool.affine_select(out=winb[:], in_=winb[:], compare_op=ALU.is_ge, fill=NEG, base=-48,
                                   pattern=[[0, 512]], channel_multiplier=1).then_inc(made, 1)
                pool.affine_select(out=hot[0:4, 0, :].rearrange("p (a t) -> p a t", t=4),
                                   in_=hot[0:4, 0, :].rearrange("p (a t) -> p a t", t=4),
                                   compare_op=ALU.not_equal, fill=1.0, base=0, pattern=[[0, 16], [-1, 4]],
                                   channel_multiplier=1).then_inc(made, 1)
                pool.affine_select(out=hot[:, 1, 0:32].rearrange("p (a t) -> p a t", t=8),
                                   in_=hot[:, 1, 0:32].rearrange("p (a t) -> p a t", t=8),
                                   compare_op=ALU.not_equal, fill=1.0, base=0, pattern=[[0, 4], [-1, 8]],
                                   channel_multiplier=1).then_inc(made, 1)
                v = late[0:4, 0:DB * NS].rearrange("p (b n) -> p b n", b=DB)
                pool.affine_select(out=v, in_=v, compare_op=ALU.is_ge, fill=NEG, base=0,
                                   pattern=[[4, DB], [-1, NS]], channel_multiplier=1).then_inc(made, 1)
                pool.wait_ge(made, 4)
                pool.affine_select(out=v, in_=v, compare_op=ALU.is_ge, fill=NEG, base=0,
                                   pattern=[[-4, DB], [1, NS]], channel_multiplier=0).then_inc(made, 1)
                v = late[0:4, DB * NS:DB * NS + 4]
                pool.affine_select(out=v, in_=v, compare_op=ALU.is_gt, fill=NEG, base=0,
                                   pattern=[[1, 4]], channel_multiplier=-1).then_inc(made, 1)
                v = late[:, DB * NS + 4:DB * NS + 5]
                pool.affine_select(out=v, in_=v, compare_op=ALU.is_gt, fill=1.0, base=4,
                                   pattern=[[0, 1]], channel_multiplier=-1).then_inc(made, 1)
                n = 7
                for j, r0 in enumerate(first_row):
                    for c in range(2 if j < HA else 1):
                        v = sel[:, j, 28:32]
                        pool.affine_select(out=v, in_=v, compare_op=ALU.not_equal, fill=1.0, base=-r0 - 4 * c,
                                           pattern=[[-1, 4]], channel_multiplier=1).then_inc(made, 1)
                        n += 1
                        pool.wait_ge(made, n)

            @block.tensor
            def _(pe):
                def turn(b, i):
                    g, j = batches[i]
                    if j == 0:
                        pe.wait_ge(loaded[g % 4], b * 256 + 128 * (g // 4) + 128)
                    if g == WING:
                        pe.wait_ge(win_loaded, b * 16 + 16)
                    if i < 3:
                        for r in range(3):
                            pe.wait_ge(copied[r], b * uses[r] + 1)
                    else:
                        pe.wait_ge(copied[i % 3], b * uses[i % 3] + i // 3 + 1)
                    for c in range(4):
                        src = (pa[:, g % 4, c, HEAD * j:HEAD * j + HEAD] if j < HA else
                               pb[:, g % 4, c, 0:HEAD] if g < NG else pw[:, c, 0:HEAD])
                        last = pe.transpose(tp[i % 3][:, c, :], src, k.ident[:])
                    last.then_inc(turned, 1)

                def multiply(b, i):
                    g, j = batches[i]
                    first = j == 0 or g == WING
                    if first:
                        pe.wait_ge(added, b * G + g + 1)
                    pe.wait_ge(copied[i % 3], b * uses[i % 3] + i // 3 + 2)
                    last = pe.matmul(ps[g % 2][:], q[:, R * j:R * j + R], kT[:, i % 3, :], start=first,
                                     stop=j == HA or g == WING)
                    last.then_inc(multiplied, 1)
                    if j == HA or g == WING:
                        pe.wait_ge(multiplied, b * NT + i + 4)
                        pe.sem_inc(scored, 1)

                def attend(b, g):
                    n = NS if g == NEWG else P
                    pe.wait_ge(exped, b * G + g + 3)
                    pe.wait_ge(p_copied, b * G + g + 1)
                    pe.sem_inc(turning, 1)
                    for c in range(1 if g == NEWG else 4):
                        last = pe.transpose(pt[0:n, c, :], e[:, g % 2, P * c:P * c + n], k.ident[0:R, 0:R])
                    last.then_inc(p_turned, 1)
                    return n

                def values(b, g, n):
                    pe.wait_ge(p_copied, b * G + g + 2)
                    pe.wait_ge(o_copied, b * G + g + 1)
                    new = [k.rows_s[:, T_AV + HEAD * j:T_AV + HEAD * j + HEAD] for j in range(HA)] \
                        + [k.rows_s[:, T_VS:T_VS + HEAD], k.rows_s[:, T_VW:T_VW + HEAD]]
                    todo = []
                    if g < NG:
                        for c in range(4):
                            todo += [(c, j, pa[:, g % 4, c, 512 + HEAD * j:512 + HEAD * j + HEAD]) for j in range(HA)]
                            todo.append((c, HA, pb[:, g % 4, c, HEAD:2 * HEAD]))
                    elif g == WING:
                        todo = [(c, HA + 1, pw[:, c, HEAD:2 * HEAD]) for c in range(4)]
                    else:
                        todo = [(0, j, new[j]) for j in range(HEADS)]
                    for x, (c, j, v) in enumerate(todo):
                        last = pe.matmul(po[g % 2][:], pT[0:n, g % 2, c, R * j:R * j + R], v, start=(x == 0),
                                         stop=(x == len(todo) - 1))
                    last.then_inc(summed, 1)
                    if g == WING:
                        pe.wait_ge(summed, b * G + g + 7)
                        pe.sem_inc(win_used, 1)

                pe.wait_ge(made, 23)
                pe.matmul(ps[0][:, 0:DB * NS + 4], hot[0:4, 0, :], late[0:4, 0:DB * NS + 4], start=True, stop=True)
                pe.matmul(ps[1][:, 0:1], hot[:, 1, :], late[:, DB * NS + 4:DB * NS + 5], start=True,
                          stop=True).then_inc(spread, 1)
                pe.wait_ge(consts_ready, 1)
                pe.sem_inc(multiplied, 3)
                pe.sem_inc(scored, 1)
                pe.sem_inc(p_turned, 2)
                pe.sem_inc(summed, 6)
                new_keys = [X_AK + j for j in range(HA)] + [X_KS, X_KW]
                with pe.Fori(0, DB) as b:
                    pe.wait_ge(q_ready, b + 1)
                    for i in range(NT + 2):
                        if i < NT:
                            turn(b, i)
                        if i >= 2:
                            multiply(b, i - 2)
                            g, j = batches[i - 2]
                            if g >= 1 and (j == 0 or g == WING):
                                n = attend(b, g - 1)
                            if g >= 1 and (j == 2 or g == WING):
                                values(b, g - 1, P)
                    pe.wait_ge(added, b * G + NEWG + 1)
                    for j in range(HEADS):
                        last = pe.matmul(ps[NEWG % 2][:, 0:NS], q[:, R * j:R * j + R],
                                         k.attT[:, new_keys[j], SEQ:ROWS], start=(j == 0), stop=(j == HEADS - 1))
                    last.then_inc(scored, 1)
                    for g in (WING, NEWG):
                        values(b, g, attend(b, g))
                pe.wait_ge(combined, DB + 1)
                for j in range(12):
                    for b in range(DB):
                        last = pe.matmul(tp[j // 4][0:NS, j % 4, :], sel[:, j, 28 - 4 * b:60 - 4 * b], oall[:, b, :],
                                         start=(b == 0), stop=(b == DB - 1))
                    if j % 4 == 3:
                        last.then_inc(gathered, 1)

            @block.scalar
            def _(act):
                act.wait_ge(consts_ready, 1)
                act.sem_inc(exped, 2)
                act.sem_inc(o_copied, 2)

                def copy(b, i):
                    act.wait_ge(turned, b * NT + i + 1)
                    act.wait_ge(multiplied, b * NT + max(i, 2) + 1)
                    act.activation(kT[:, i % 3, :].rearrange("p (c n) -> p c n", c=4), tp[i % 3][:],
                                   ACT.Copy).then_inc(copied[i % 3], 1)

                def softmax(b, g):
                    n = NS if g == NEWG else 512
                    act.wait_ge(maxed, b * G + g + 1)
                    act.wait_ge(p_turned, b * G + g + 1)
                    if g == 0:
                        act.wait_ge(combined, b + 1)
                    act.activation(e[:, g % 2, 0:n], sb_[:, g % 2, 0:n], ACT.Exp, bias=nm[:, g:g + 1],
                                   accum_out=l[:, g:g + 1]).then_inc(exped, 1)

                def out(b, g):
                    act.wait_ge(summed, b * G + g + 7)
                    act.activation(ob[:, g, :], po[g % 2][:], ACT.Copy).then_inc(o_copied, 1)

                with act.Fori(0, DB) as b:
                    for i, (g, j) in enumerate(batches):
                        if j % 2 == 0 or g == WING:
                            copy(b, i)
                        if g >= 1 and (j == 0 or g == WING):
                            softmax(b, g - 1)
                        if g >= 1 and j == 4:
                            out(b, g - 1)
                        if g == WING:
                            out(b, g - 1)
                    softmax(b, WING)
                    softmax(b, NEWG)
                    out(b, WING)
                    out(b, NEWG)
                    act.wait_ge(minned, b + 1)
                    act.activation(wt[:, 0, :], nm[:], ACT.Exp, bias=st[:, 0:1], scale=-1.0).then_inc(weighed, 1)

            @block.vector
            def _(dve):
                step = Chain(dve, dve_step)
                dve.wait_ge(spread, 1)
                dve.wait_ge(made, 23)
                step(dve.tensor_copy(newb[:].rearrange("p b n -> p (b n)"), ps[0][:, 0:DB * NS]))
                step(dve.tensor_tensor(winb[:, 0:4], winb[:, 0:4], ps[0][:, DB * NS:DB * NS + 4], ALU.add))
                step(dve.tensor_copy(coef[:, 1:2], ps[1][:, 0:1]))
                step(dve.tensor_scalar(coef[:, 0:1], k.neglam[0:R, :], -1.0, None, ALU.add))
                step(dve.tensor_tensor(coef[:, 0:1], coef[:, 0:1], coef[:, 1:2], ALU.mult))
                step(dve.tensor_scalar(coef[:, 0:1], coef[:, 0:1], 1.0, None, ALU.add))
                for r in range(3):
                    dve.sem_inc(copied[r], 1)
                dve.sem_inc(added, 2)
                dve.sem_inc(p_copied, 1)
                dve.sem_inc(combined, 1)
                dve.sem_inc(consts_ready, 1)
                own = step.n

                def queries(b):
                    dve.wait_ge(scored, b * G + 1)
                    A = q[:, 0:288].rearrange("p (h x) -> p h x", x=72)
                    for c in range(2):
                        dve.tensor_copy(A[DC * c:DC * c + DC, :, 4 * c:4 * c + 4],
                                        k.attT[DC * c:DC * c + DC, X_AQ:X_AQ + HA, bass.ds(b * DT + SEQ, DT)])
                    for x in (288, 368):
                        last = dve.tensor_copy(q[:, x:x + 16].rearrange("p (h t) -> p h t", h=HB),
                                               k.attT[:, X_BQ:X_BQ + HB, bass.ds(b * DT + SEQ, DT)])
                    last.then_inc(q_ready, 1)

                def copy(b, i):
                    dve.wait_ge(turned, b * NT + i + 1)
                    dve.wait_ge(multiplied, b * NT + max(i, 2) + 1)
                    dve.tensor_copy(kT[:, i % 3, :].rearrange("p (c n) -> p c n", c=4),
                                    tp[i % 3][:]).then_inc(copied[i % 3], 1)

                def row_max(b, g):
                    dve.wait_ge(scored, b * G + g + 2)
                    dve.wait_ge(exped, b * G + g + 1)
                    if g < NG:
                        dve.tensor_tensor(sb_[:, g % 2, :].rearrange("p (n r) -> p n r", n=8),
                                          ps[g % 2][:].rearrange("p (n r) -> p n r", n=8),
                                          k.selb[:, bass.ds(b, 1), 8 * g:8 * g + 8].rearrange(
                                              "p a n -> p (a n)").unsqueeze(2).broadcast_to([R, 8, CMP]),
                                          ALU.add).then_inc(added, 1)
                    elif g == WING:
                        dve.tensor_tensor(sb_[:, g % 2, :], ps[g % 2][:], winb[:], ALU.add).then_inc(added, 1)
                    else:
                        dve.tensor_tensor(sb_[:, g % 2, 0:NS], ps[g % 2][:, 0:NS],
                                          newb[:, bass.ds(b, 1), :].rearrange("p a n -> p (a n)"),
                                          ALU.add).then_inc(added, 1)
                    n = NS if g == NEWG else 512
                    dve.wait_ge(added, b * G + g + 3)
                    dve.tensor_reduce(nm[:, g:g + 1], sb_[:, g % 2, 0:n], AX_X, ALU.max,
                                      negate=True).then_inc(maxed, 1)

                def weights(b, g):
                    dve.wait_ge(p_turned, b * G + g + 3)
                    dve.wait_ge(summed, b * G + g + 5)
                    n, c = (NS, 1) if g == NEWG else (P, 4)
                    if g != WING:
                        dve.tensor_copy(pT[0:n, g % 2, 0:c, 0:288].rearrange("p c (h x) -> p c h x", x=72)[:, :, :, 0:8],
                                        pt[0:n, 0:c, 0:32].rearrange("p c (h x) -> p c h x", h=HA))
                        last = dve.tensor_copy(pT[0:n, g % 2, 0:c, 288:304], pt[0:n, 0:c, 32:48])
                    if g >= NG:
                        last = dve.tensor_copy(pT[0:n, g % 2, 0:c, 368:384], pt[0:n, 0:c, 48:64])
                    last.then_inc(p_copied, 1)

                with dve.Fori(0, DB) as b:
                    queries(b)
                    for i, (g, j) in enumerate(batches):
                        if g >= 1 and (j == 0 or g == WING):
                            row_max(b, g - 1)
                        if j % 2 == 1 and g != WING:
                            copy(b, i)
                        if g >= 1 and (j == 1 or g == WING):
                            weights(b, g - 1)
                    row_max(b, WING)
                    row_max(b, NEWG)
                    weights(b, WING)
                    weights(b, NEWG)
                    dve.wait_ge(maxed, b * G + G)
                    dve.tensor_reduce(st[:, 0:1], nm[:], AX_X, ALU.min).then_inc(minned, 1)
                    dve.wait_ge(weighed, b + 1)
                    dve.wait_ge(exped, b * G + G + 2)
                    dve.wait_ge(o_copied, b * G + G + 2)

                    n = [0]

                    def then(ins):
                        n[0] += 1
                        ins.then_inc(dve_step, 1)
                        dve.wait_ge(dve_step, b * 6 + own + n[0])

                    then(dve.tensor_tensor(wt[:, 1, :], wt[:, 0, :], l[:], ALU.mult))
                    then(dve.tensor_reduce(st[:, 1:2], wt[:, 1, :], AX_X, ALU.add))
                    then(dve.reciprocal(st[:, 2:3], st[:, 1:2]))
                    then(dve.tensor_scalar(wt[:, 2, :], wt[:, 0, :], st[:, 2:3], coef[:, 0:1], ALU.mult, ALU.mult))
                    then(dve.tensor_tensor(ob[:], ob[:], wt[:, 2, :].unsqueeze(2).broadcast_to([R, G, HEAD]), ALU.mult))
                    then(dve.tensor_reduce(oall[:, bass.ds(b, 1), :].rearrange("p a n -> p (a n)"),
                                           ob[:].rearrange("p g n -> p n g"), AX_X, ALU.add))
                    dve.sem_inc(combined, 1)
                dve.wait_ge(gathered, 3)
                for a in range(3):
                    last = dve.tensor_copy(o[:, a, :].rearrange("p (h n) -> p h n", h=4), tp[a][0:NS, :, :])
                last.then_inc(out_ready, 1)


def convolve(nc, d, k):
    with Stage(nc, "cv") as s:
        x = s.sb("x", [P, 5, QKC])
        w = s.sb("w", [5, QKC])
        old = s.sb("old", [3 * DB, QKC])
        wT = s.sb("wT", [P, 8, 5])
        xp = s.sb("xp", [P, 8, SEQ + 3])
        xs = s.sb("xs", [P, 8, DB, DT + 3])
        sig = s.sb("sig", [P, 8, ROWS])
        gin = s.sb("gin", [P, 5, 2 * HC])
        gbias = s.sb("gbias", [HC, 2])
        t0 = s.sb("t0", [HC, ROWS])
        t1 = s.sb("t1", [HC, ROWS])
        tp = [s.ps(f"tp{i}", [P, 4, P]) for i in range(4)]
        gi = [s.ps(f"gi{i}", [HC, 512]) for i in range(4)]
        x_loaded = s.sems("x_loaded", 5)
        w_loaded = s.sem("w_loaded")
        g_loaded = s.sem("g_loaded")
        zeroed = s.sem("zeroed")
        turned = s.sem("turned")
        copied = s.sem("copied")
        g_turned = s.sem("g_turned")
        conv_done = s.sem("conv_done")
        sig_done = s.sem("sig_done")
        silu_done = s.sem("silu_done")
        f_ready = s.sem("f_ready")
        f_exped = s.sem("f_exped")
        f_logged = s.sem("f_logged")
        k_turned = s.sem("k_turned")
        k_copied = s.sem("k_copied")
        dve_step = s.sem("dve_step")
        stored = s.sem("stored")
        CQ = C_CQK
        jobs = [("w", 0, h) for h in range(2)] + [("old", 0, h) for h in range(2)] \
            + [("x", t, h) for t in range(5) for h in range(2)]

        with nc.Block() as block:
            @block.sync
            def _(sp):
                sp.dma_start(w[0:4, :], d.c_conv_w).then_inc(w_loaded, 16)
                sp.dma_start(w[4:5, :], d.c_conv_b.unsqueeze(0)).then_inc(w_loaded, 16)
                sp.dma_start(old[:], d.c_conv.rearrange("b t n -> (b t) n")).then_inc(w_loaded, 16)
                for t, (r0, rows) in enumerate(TILES):
                    sp.dma_start(x[0:rows, t, :], d.proj[r0:r0 + rows, CQ:CQ + QKC]).then_inc(x_loaded[t], 16)
                for t, (r0, rows) in enumerate(TILES):
                    sp.dma_start(gin[0:rows, t, :], d.proj[r0:r0 + rows, C_CIF:C_CIF + 2 * HC]).then_inc(g_loaded, 16)
                sp.dma_start(gbias[:], d.c_gate_b.rearrange("a h -> h a"), allow_slow_non_contiguous=True).then_inc(g_loaded, 16)
                sp.dma_start(d.conv_p, d.proj[SEQ - 3:SEQ, CQ:CQ + QKC]).then_inc(stored, 16)
                for b in range(DB):
                    r = SEQ + DT * b
                    sp.dma_start(d.conv_s[b], d.proj[r + 1:r + DT, CQ:CQ + QKC]).then_inc(stored, 16)
                sp.wait_ge(stored, 16 * (DB + 1))

            @block.tensor
            def _(pe):
                for n, (what, t, h) in enumerate(jobs):
                    if what == "w":
                        pe.wait_ge(w_loaded, 48)
                        src, rows = w, 5
                    elif what == "old":
                        src, rows = old, 3 * DB
                    else:
                        pe.wait_ge(x_loaded[t], 16)
                        src, rows = x[:, t, :], TILES[t][1]
                    if n >= 2:
                        pe.wait_ge(copied, n - 1)
                    for c in range(4):
                        col = P * (4 * h + c)
                        last = pe.transpose(tp[n % 2][:, c, 0:rows], src[0:rows, col:col + P], k.ident[0:rows, 0:rows])
                    last.then_inc(turned, 1)
                pe.wait_ge(g_loaded, 96)
                for t, (r0, rows) in enumerate(TILES):
                    for a in range(2):
                        out = gi[a][:, r0:r0 + rows] if t < PT else gi[2 + a][:, 0:rows]
                        last = pe.transpose(out, gin[0:rows, t, HC * a:HC * a + HC], k.ident[0:rows, 0:rows])
                last.then_inc(g_turned, 1)
                pe.wait_ge(silu_done, 1)
                for t, (r0, rows) in enumerate(TILES):
                    if t >= 2:
                        pe.wait_ge(k_copied, t - 1)
                    for c in range(4):
                        last = pe.transpose(tp[2 + t % 2][0:rows, c, :], k.qkT[:, 4 + c, r0:r0 + rows], k.ident[:])
                    last.then_inc(k_turned, 1)

            @block.scalar
            def _(act):
                act.wait_ge(f_ready, 1)
                act.activation(t1[:], t0[:], ACT.Exp).then_inc(f_exped, 1)
                act.wait_ge(f_exped, 1)
                act.activation(t1[:], t1[:], ACT.Ln, bias=1.0).then_inc(f_logged, 1)
                act.wait_ge(conv_done, 1)
                act.activation(sig[:], k.qkT[:], ACT.Sigmoid).then_inc(sig_done, 1)

            @block.vector
            def _(dve):
                step = Chain(dve, dve_step)
                step(dve.memset(xp[:, :, 0:3], 0.0))
                for n, (what, t, h) in enumerate(jobs):
                    dve.wait_ge(turned, n + 1)
                    c = slice(4 * h, 4 * h + 4)
                    if what == "w":
                        last = dve.tensor_copy(wT[:, c, :], tp[n % 2][:, :, 0:5])
                    elif what == "old":
                        last = dve.tensor_copy(xs[:, c, :, 0:3], tp[n % 2][:, :, 0:3 * DB].rearrange(
                            "p c (b t) -> p c b t", b=DB))
                    elif t < PT:
                        last = dve.tensor_copy(xp[:, c, 3 + P * t:3 + P * t + P], tp[n % 2][:])
                    else:
                        last = dve.tensor_copy(xs[:, c, :, 3:3 + DT], tp[n % 2][:, :, 0:NS].rearrange(
                            "p c (b t) -> p c b t", b=DB))
                    last.then_inc(copied, 1)
                dve.wait_ge(g_turned, 1)
                for a, dst in ((0, k.gate_i), (1, k.gate_f)):
                    for src, r0, n in ((gi[a], 0, SEQ), (gi[2 + a], SEQ, NS)):
                        step(dve.tensor_scalar(dst[:, r0:r0 + n], src[:, 0:n], gbias[:, a:a + 1], None, ALU.add))
                dve.scalar_tensor_tensor(t0[:], k.gate_f[:], -1.0, k.gate_f[:], ALU.mult, ALU.min).then_inc(f_ready, 1)
                dve.wait_ge(f_logged, 1)
                step(dve.tensor_scalar(k.gate_f[:], k.gate_f[:], 0.0, None, ALU.min))
                step(dve.tensor_tensor(k.gate_f[:], k.gate_f[:], t1[:], ALU.subtract))
                dve.wait_ge(copied, len(jobs))
                for j in range(4):
                    for c in range(8):
                        outs = ((k.qkT[:, c, 0:SEQ], xp[:, c, j:j + SEQ]),
                                (k.qkT[:, c, SEQ:ROWS].rearrange("p (b t) -> p b t", b=DB), xs[:, c, :, j:j + DT]))
                        for out, src in outs:
                            if j == 0:
                                last = dve.tensor_scalar(out, src, wT[:, c, 0:1], wT[:, c, 4:5], ALU.mult, ALU.add)
                            else:
                                last = dve.scalar_tensor_tensor(out, src, wT[:, c, j:j + 1], out, ALU.mult, ALU.add)
                    if j < 3:
                        step(last)
                last.then_inc(conv_done, 1)
                dve.wait_ge(sig_done, 1)
                step(dve.tensor_tensor(k.qkT[:], k.qkT[:], sig[:], ALU.mult))
                dve.tensor_scalar(k.qkT[:, 0:4, :], k.qkT[:, 0:4, :], DC ** -0.5, None, ALU.mult).then_inc(silu_done, 1)
                for t, (r0, rows) in enumerate(TILES):
                    dve.wait_ge(k_turned, t + 1)
                    dve.tensor_copy(k.k_rows[0:rows, t, :].rearrange("p (c n) -> p c n", c=4),
                                    tp[2 + t % 2][0:rows, :, :]).then_inc(k_copied, 1)
                dve.wait_ge(k_copied, 5)


def mlstm(nc, d, k, decode):
    NC, n, tile0 = (1, NS, PT) if decode else (PT, P, 0)
    NB, L = (DB, DT) if decode else (1, P)
    V = HEAD + 1
    with Stage(nc, "md" if decode else "mp") as s:
        v = s.sb("v", [P, NC, HC, V])
        ones = s.sb("ones8", [HC, P])
        m = s.sb("m", [HC, NB])
        b = s.sb("b", [HC, NC, n])
        row = s.sb("row", [HC, NC, 4, n])
        nca = s.sb("nca", [HC, NC, n])
        mt = s.sb("mt", [HC, NC, n])
        cs = s.sb("cs", [HC, NC, NB])
        diag = s.sb("diag", [HC, NC, HC, NB])
        pick = s.sb("pick", [HC, HC, P])
        mask = s.sb("mask", [n, n])
        col = s.sb("col", [P, NC, 4, HC])
        w = s.sb("w", [P, 4, n])
        qk = s.sb("qk", [P, 4, n])
        kw = s.sb("kw", [P, NC, HC, DC])
        inter = s.sb("inter", [P, 4, V])
        num = s.sb("num", [P, 4, V])
        den = s.sb("den", [P, 4, 4])
        h_out = s.sb("h_out", [P, 2, HC, HEAD])
        S = s.sb("S", [P, DB if decode else 1, 4, V])
        csb = s.sb("csb", [P, NC, HC, NB])
        sc = [s.ps(f"sc{i}", [P, 2, P]) for i in range(2)]
        small = sc[1][:, 0, 0:4 * HC].rearrange("p (x h) -> p x h", x=4)
        dd = s.ps("dd", [P, 4, n])
        pn = [s.ps(f"pn{i}", [P, 2, V]) for i in range(2)]
        pi = [s.ps(f"pi{i}", [P, 2, V]) for i in range(2)]
        pu = s.ps("pu", [P, 512])

        loaded = s.sem("loaded")
        st_loaded = s.sem("st_loaded")
        zeroed = s.sem("zeroed")
        made = s.sem("made")
        dve_step = s.sem("dve_step")
        rows_ready = s.sem("rows_ready")
        cs_exped = s.sem("cs_exped")
        diag_ready = s.sem("diag_ready")
        r_turned = s.sem("r_turned")
        r_copied = s.sem("r_copied")
        col_exped = s.sem("col_exped")
        cs_spread = s.sem("cs_spread")
        csb_ready = s.sem("csb_ready")
        kw_ready = s.sem("kw_ready")
        scored = s.sem("scored")
        exped = s.sem("exped")
        weighed = s.sem("weighed")
        summed = s.sem("summed")
        in_copied = s.sem("in_copied")
        state_ready = s.sem("state_ready")
        taken = s.sem("taken")
        h_ready = s.sem("h_ready")
        h_stored = s.sems("h_stored", 2)
        turned = s.sem("turned")
        copied = s.sem("copied")
        fin = s.sem("fin")
        out_stored = s.sem("out_stored")
        extra = [s.sem(f"extra{i}") for i in range(6)]
        if decode:
            c0 = s.sb("c0", [P, DB, HC, DC])
            c1 = s.sb("c1", [P, DB, HC, DC])
            n0 = s.sb("n0", [NS, P])
            n0b = s.sb("n0b", [DB, HC, DC])
            qpad = s.sb("qpad", [P, 4, 288])
            blk = s.sb("blk", [NS, DB])
            kwb = s.sb("kwb", [NS, 2, DB, DC])
            bh = s.sb("bh", [DB, 2, HC])
        else:
            cT = s.sb("cT", [P, 4, P])

        units = [(c, hf) for c in range(NC) for hf in range(2)]

        def q_of(h, c):
            r0 = TILES[tile0 + c][0]
            return k.qkT[DC * (h % 2):DC * (h % 2) + DC, h // 2, r0:r0 + n]

        def k_of(h, c):
            r0 = TILES[tile0 + c][0]
            return k.qkT[DC * (h % 2):DC * (h % 2) + DC, 4 + h // 2, r0:r0 + n]

        with nc.Block() as block:
            @block.sync
            def _(sp):
                for c in range(NC):
                    r0, rows = TILES[tile0 + c]
                    sp.dma_start(v[0:rows, c, :, 0:HEAD], d.proj[r0:r0 + rows, C_CV:C_CV + HC * HEAD].rearrange(
                        "r (h n) -> r h n", h=HC)).then_inc(loaded, 16)
                if decode:
                    sp.dma_start(m[:], d.c_m.rearrange("b h -> h b"), allow_slow_non_contiguous=True).then_inc(st_loaded, 16)
                    sp.dma_start(n0[:], d.c_n.rearrange("b (x y) n -> (b x) (y n)", y=2)).then_inc(st_loaded, 16)
                    sp.dma_start(n0b[:], d.c_n).then_inc(st_loaded, 16)
                    for i in range(DB):
                        sp.dma_start(c0[:, i, :, :], d.c_C[i].rearrange("h v n -> v h n")).then_inc(st_loaded, 16)
                for c in range(NC):
                    r0, rows = TILES[tile0 + c]
                    sp.wait_ge(h_ready, 2 * c + 2)
                    sp.dma_start(d.h_c[r0:r0 + rows, :], h_out[0:rows, c % 2, :, :].rearrange(
                        "p h n -> p (h n)")).then_inc(h_stored[c % 2], 16)
                sp.wait_ge(fin, 1)
                n_out = 0
                if decode:
                    for i in range(DB):
                        sp.dma_start(d.C_s[i].rearrange("h v n -> v h n"), c1[:, i, :, :]).then_inc(out_stored, 16)
                    sp.dma_start(d.n_s, n0b[:]).then_inc(out_stored, 16)
                    sp.dma_start(d.m_s, bh[:, 1, :]).then_inc(out_stored, 16)
                    n_out = DB + 2
                else:
                    for x in range(4):
                        sp.dma_start(d.C_p[2 * x:2 * x + 2].rearrange("y v n -> v y n"),
                                     cT[:, x, :].rearrange("p (y n) -> p y n", y=2)).then_inc(out_stored, 16)
                    for y in range(2):
                        sp.dma_start(d.n_p[y:HC:2, :].rearrange("x n -> n x").unsqueeze(2),
                                     S[DC * y:DC * y + DC, 0, :, HEAD:V],
                                     allow_slow_non_contiguous=True).then_inc(out_stored, 16)
                    sp.dma_start(d.m_p.unsqueeze(1), m[:]).then_inc(out_stored, 16)
                    n_out = 7
                sp.wait_ge(out_stored, 16 * n_out)
                for i in range(min(2, NC)):
                    sp.wait_ge(h_stored[i], 16 * max(1, NC // 2))

            @block.gpsimd
            def _(pool):
                pool.memset(ones[:], 1.0).then_inc(made, 1)
                pool.memset(v[:, :, :, HEAD:V], 1.0).then_inc(made, 1)
                z = [mask, pick, S] + ([qpad] if decode else [m])
                for x in z:
                    pool.memset(x[:], 0.0).then_inc(zeroed, 1)
                pool.wait_ge(zeroed, 4)
                pool.affine_select(out=mask[:], in_=mask[:], compare_op=ALU.is_ge, fill=NEG, base=0,
                                   pattern=[[1, n]], channel_multiplier=-1).then_inc(made, 1)
                pool.affine_select(out=pick[:], in_=pick[:], compare_op=ALU.not_equal, fill=1.0, base=0,
                                   pattern=[[-1, HC], [0, P]], channel_multiplier=1).then_inc(made, 1)
                if decode:
                    pool.wait_ge(made, 4)
                    mv = mask[:].rearrange("p (b t) -> p b t", b=DB)
                    pool.affine_select(out=mv, in_=mv, compare_op=ALU.is_ge, fill=NEG, base=0,
                                       pattern=[[-DT, DB], [0, DT]], channel_multiplier=1).then_inc(made, 1)
                    pool.memset(blk[:], 1.0).then_inc(made, 1)
                    pool.wait_ge(made, 6)
                    pool.affine_select(out=blk[:], in_=blk[:], compare_op=ALU.is_ge, fill=0.0, base=0,
                                       pattern=[[-DT, DB]], channel_multiplier=1).then_inc(made, 1)
                    pool.wait_ge(made, 7)
                    pool.affine_select(out=blk[:], in_=blk[:], compare_op=ALU.is_ge, fill=0.0, base=DT - 1,
                                       pattern=[[DT, DB]], channel_multiplier=-1).then_inc(made, 1)

            @block.tensor
            def _(pe):
                pe.wait_ge(made, 8 if decode else 4)
                if decode:
                    pe.wait_ge(st_loaded, 16 * (DB + 3))
                    for i in range(DB):
                        if i >= 2:
                            pe.wait_ge(copied, i - 1)
                        bank = (pn[0], pn[1])[i % 2]
                        for x in range(2):
                            last = pe.transpose(bank[:, x, 0:P], c0[:, i, 2 * x:2 * x + 2, :].rearrange("p y n -> p (y n)"), k.ident[:])
                        bank = (pi[0], pi[1])[i % 2]
                        for x in range(2, 4):
                            last = pe.transpose(bank[:, x - 2, 0:P], c0[:, i, 2 * x:2 * x + 2, :].rearrange("p y n -> p (y n)"), k.ident[:])
                        last.then_inc(turned, 1)
                    pe.transpose(pu[:, 0:NS], n0[:], k.ident[0:NS, 0:NS]).then_inc(extra[0], 1)
                for c in range(NC):
                    pe.wait_ge(rows_ready, c + 1)
                    if c:
                        pe.wait_ge(r_copied, c)
                    for x in range(4):
                        last = pe.transpose(small[0:n, x, :], row[:, c, x, :], k.ident[0:HC, 0:HC])
                    last.then_inc(r_turned, 1)
                pe.wait_ge(r_copied, NC)
                pe.wait_ge(diag_ready, 1)
                if decode:
                    pe.wait_ge(copied, DB + 1)
                pe.matmul(pu[:, 64:64 + NC * HC * NB], ones[:], diag[:].rearrange("p c h b -> p (c h b)"),
                          start=True, stop=True).then_inc(cs_spread, 1)
                pe.wait_ge(csb_ready, 1)
                pe.wait_ge(loaded, 16 * NC)
                pe.wait_ge(kw_ready, 1)
                if decode:
                    pe.wait_ge(copied, DB + 2)
                for u, (c, hf) in enumerate(units):
                    if u:
                        pe.wait_ge(weighed, u)
                        pe.wait_ge(exped, u)
                    for x in range(4):
                        h = 4 * hf + x
                        pe.matmul(dd[0:n, x, :], pick[:, h, 0:n], nca[:, c, :], start=True, stop=False)
                        pe.matmul(dd[0:n, x, :], k.ident[0:n, 0:n], mask[:], start=False, stop=True)
                        last = pe.matmul(sc[x % 2][0:n, x // 2, 0:n], k_of(h, c), q_of(h, c), start=True, stop=True)
                    last.then_inc(scored, 1)
                    if u:
                        pe.wait_ge(taken, u)
                    if not decode and c:
                        pe.wait_ge(state_ready, u - 1)
                    for x in range(4):
                        h = 4 * hf + x
                        rows = slice(DC * (h % 2), DC * (h % 2) + DC)
                        if decode:
                            for i in range(DB):
                                pe.matmul(pi[x % 2][0:n, x // 2, :], qpad[rows, h // 2, NS * i:NS * i + NS],
                                          S[rows, i, h // 2, :], start=(i == 0), stop=(i == DB - 1))
                        else:
                            pe.matmul(pi[x % 2][:, x // 2, :], q_of(h, c), S[rows, 0, h // 2, :], start=True, stop=True)
                    if not decode:
                        for x in range(4):
                            h = 4 * hf + x
                            rows = slice(DC * (h % 2), DC * (h % 2) + DC)
                            pe.matmul(pu[rows, V * (x // 2):V * (x // 2) + V], kw[:, c, h, :], v[:, c, h, :],
                                      start=True, stop=True)
                    pe.wait_ge(weighed, u + 1)
                    for x in range(4):
                        h = 4 * hf + x
                        last = pe.matmul(pn[x // 2][0:n, x % 2, :], qk[0:n, x, :], v[0:n, c, h, :], start=True, stop=True)
                    last.then_inc(summed, 1)
                if decode:
                    for h in range(HC):
                        pe.wait_ge(extra[1], h + 1)
                        if h:
                            pe.wait_ge(extra[3], h)
                        pe.matmul(pu[:], v[0:NS, 0, h, 0:HEAD], kwb[:, h % 2, :, :].rearrange("p b n -> p (b n)"),
                                  start=True, stop=True).then_inc(extra[2], 1)
                    pe.wait_ge(extra[3], HC)
                    pe.matmul(pu[0:DB, :], blk[:], kw[0:NS, 0, :, :].rearrange("p h n -> p (h n)"), start=True, stop=True)
                    pe.transpose(small[0:DB, 0, :], cs[:, 0, :], k.ident[0:HC, 0:HC])
                    pe.transpose(small[0:DB, 1, :], mt[:, 0, :].rearrange("p (b t) -> p b t", b=DB)[:, :, DT - 1],
                                 k.ident[0:HC, 0:HC]).then_inc(extra[4], 1)
                else:
                    pe.wait_ge(state_ready, 2 * NC)
                    for x in range(4):
                        last = pe.transpose(dd[:, x, :], S[:, 0, x, 0:HEAD], k.ident[:])
                    last.then_inc(turned, 1)

            @block.scalar
            def _(act):
                act.wait_ge(extra[5], 1)
                act.activation(cs[:], cs[:], ACT.Exp).then_inc(cs_exped, 1)
                for c in range(NC):
                    act.wait_ge(r_turned, c + 1)
                    act.activation(col[0:n, c, 0, :], small[0:n, 0, :], ACT.Copy)
                    act.activation(col[0:n, c, 1:4, :], small[0:n, 1:4, :], ACT.Exp).then_inc(r_copied, 1)
                act.wait_ge(r_copied, NC)
                for u, (c, hf) in enumerate(units):
                    act.wait_ge(scored, u + 1)
                    if u:
                        act.wait_ge(weighed, u)
                    for x in range(4):
                        h = 4 * hf + x
                        last = act.activation(w[0:n, x, :], dd[0:n, x, :], ACT.Exp, bias=col[0:n, c, 0, h:h + 1])
                    last.then_inc(exped, 1)
                    act.wait_ge(summed, u + 1)
                    if u:
                        act.wait_ge(taken, u)
                    for x in range(4):
                        h = 4 * hf + x
                        last = act.activation(inter[0:n, x, :], pi[x % 2][0:n, x // 2, :], ACT.Copy,
                                              scale=col[0:n, c, 1, h:h + 1])
                    last.then_inc(in_copied, 1)

            @block.vector
            def _(dve):
                step = Chain(dve, dve_step)
                if decode:
                    dve.wait_ge(st_loaded, 16 * (DB + 3))
                dve.wait_ge(zeroed, 4)
                dve.wait_ge(made, 4)
                for c in range(NC):
                    g0 = TILES[tile0 + c][0]
                    for i in range(NB):
                        r = slice(L * i, L * i + L)
                        gr = slice(g0 + L * i, g0 + L * i + L)
                        init = m[:, i:i + 1]
                        step(dve.tensor_tensor_scan(b[:, c, r], ones[:, 0:L], k.gate_f[:, gr], 0.0, ALU.mult, ALU.add))
                        step(dve.tensor_tensor(row[:, c, 0, r], k.gate_i[:, gr], b[:, c, r], ALU.subtract))
                        step(dve.tensor_tensor_scan(nca[:, c, r], row[:, c, 0, r], row[:, c, 0, r], init, ALU.max, ALU.max))
                    ca = nca[:, c, :].rearrange("p (b t) -> p b t", b=NB)
                    last_ca = ca[:, :, L - 1:L]
                    step(dve.tensor_tensor(row[:, c, 1, :].rearrange("p (b t) -> p b t", b=NB),
                                           m[:].unsqueeze(2).broadcast_to([HC, NB, L]), ca, ALU.subtract))
                    step(dve.tensor_tensor(mt[:, c, :], b[:, c, :], nca[:, c, :], ALU.add))
                    step(dve.tensor_scalar(row[:, c, 2, :], mt[:, c, :], -1.0, None, ALU.mult))
                    step(dve.tensor_tensor(row[:, c, 3, :].rearrange("p (b t) -> p b t", b=NB),
                                           row[:, c, 0, :].rearrange("p (b t) -> p b t", b=NB),
                                           last_ca.broadcast_to([HC, NB, L]), ALU.subtract))
                    step(dve.tensor_tensor(cs[:, c, :].unsqueeze(2), m[:].unsqueeze(2), last_ca, ALU.subtract))
                    if not decode:
                        step(dve.tensor_copy(m[:], mt[:, c, L - 1:L]))
                    dve.tensor_scalar(nca[:, c, :], nca[:, c, :], -1.0, None, ALU.mult).then_inc(rows_ready, 1)
                dve.sem_inc(extra[5], 1)
                dve.wait_ge(cs_exped, 1)
                for c in range(NC):
                    last = dve.tensor_tensor(diag[:, c, :, :], k.ident[0:HC, 0:HC].unsqueeze(2).broadcast_to([HC, HC, NB]),
                                             cs[:, c, :].unsqueeze(1).broadcast_to([HC, HC, NB]), ALU.mult)
                last.then_inc(diag_ready, 1)
                if decode:
                    for i in range(DB):
                        dve.wait_ge(turned, i + 1)
                        dve.tensor_copy(S[:, i, 0:2, 0:HEAD], pn[i % 2][:, :, 0:HEAD])
                        dve.tensor_copy(S[:, i, 2:4, 0:HEAD], pi[i % 2][:, :, 0:HEAD]).then_inc(copied, 1)
                    dve.wait_ge(extra[0], 1)
                    dve.tensor_copy(S[:, :, :, HEAD:V], pu[:, 0:NS].rearrange("p (b x) -> p b x", b=DB).unsqueeze(3)) \
                        .then_inc(copied, 1)
                    dve.tensor_copy(qpad[:].rearrange("p x (b y) -> p x b y", y=36)[:, :, :, 0:DT],
                                    k.qkT[:, 0:4, SEQ:ROWS].rearrange("p x (b t) -> p x b t", b=DB)).then_inc(copied, 1)
                dve.wait_ge(cs_spread, 1)
                dve.tensor_copy(csb[:].rearrange("p c h b -> p (c h b)"), pu[:, 64:64 + NC * HC * NB]).then_inc(csb_ready, 1)
                dve.wait_ge(csb_ready, 1)
                dve.wait_ge(r_copied, NC)
                for c in range(NC):
                    last = dve.tensor_tensor(kw[0:n, c, :, :], k.k_rows[0:n, tile0 + c, :].rearrange(
                        "p (h n) -> p h n", h=HC), col[0:n, c, 3, :].unsqueeze(2).broadcast_to([n, HC, DC]), ALU.mult)
                last.then_inc(kw_ready, 1)
                for u, (c, hf) in enumerate(units):
                    dve.wait_ge(exped, u + 1)
                    if u:
                        dve.wait_ge(summed, u)
                    for y in range(2):
                        last = dve.tensor_tensor(qk[0:n, y:4:2, :], sc[y][0:n, :, 0:n], w[0:n, y:4:2, :], ALU.mult)
                    last.then_inc(weighed, 1)
                    dve.wait_ge(summed, u + 1)
                    dve.wait_ge(in_copied, u + 1)
                    for x in range(2):
                        last = dve.tensor_tensor(num[0:n, 2 * x:2 * x + 2, :], inter[0:n, 2 * x:2 * x + 2, :],
                                                 pn[x][0:n, :, :], ALU.add)
                    step(last)
                    if not decode:
                        st = S[:, 0, 2 * hf:2 * hf + 2, :]
                        for y in range(2):
                            rows = slice(DC * y, DC * y + DC)
                            sy = S[rows, 0, 2 * hf:2 * hf + 2, :]
                            step(dve.tensor_tensor(sy, sy, csb[rows, c, 4 * hf + y:4 * hf + 4:2, :].broadcast_to(
                                [DC, 2, V]), ALU.mult))
                        dve.tensor_tensor(st, st, pu[:, 0:2 * V].rearrange("p (x n) -> p x n", x=2),
                                          ALU.add).then_inc(state_ready, 1)
                        dve.wait_ge(state_ready, u + 1)
                    dve.sem_inc(taken, 1)
                    dn = num[0:n, :, HEAD:V].rearrange("p x a -> p (x a)")
                    step(dve.scalar_tensor_tensor(den[0:n, 0, :], dn, -1.0, dn, ALU.mult, ALU.max))
                    step(dve.tensor_tensor(den[0:n, 1, :], den[0:n, 0, :], col[0:n, c, 2, 4 * hf:4 * hf + 4], ALU.max))
                    step(dve.reciprocal(den[0:n, 2, :], den[0:n, 1, :]))
                    if c >= 2:
                        dve.wait_ge(h_stored[c % 2], 16 * (c // 2))
                    dve.tensor_tensor(h_out[0:n, c % 2, 4 * hf:4 * hf + 4, :], num[0:n, :, 0:HEAD],
                                      den[0:n, 2, :].unsqueeze(2).broadcast_to([n, 4, HEAD]), ALU.mult).then_inc(h_ready, 1)
                if decode:
                    for h in range(HC):
                        if h >= 2:
                            dve.wait_ge(extra[2], h - 1)
                        dve.tensor_tensor(kwb[:, h % 2, :, :], kw[0:NS, 0, h, :].unsqueeze(1).broadcast_to([NS, DB, DC]),
                                          blk[:].unsqueeze(2).broadcast_to([NS, DB, DC]), ALU.mult).then_inc(extra[1], 1)
                        step(dve.tensor_tensor(c1[:, :, h, :], c0[:, :, h, :], csb[:, 0, h, :].unsqueeze(2).broadcast_to(
                            [P, DB, DC]), ALU.mult))
                        dve.wait_ge(extra[2], h + 1)
                        dve.tensor_tensor(c1[:, :, h, :], c1[:, :, h, :], pu[:].rearrange("p (b n) -> p b n", b=DB),
                                          ALU.add).then_inc(extra[3], 1)
                    dve.wait_ge(extra[4], 1)
                    step(dve.tensor_copy(bh[:], small[0:DB, 0:2, :]))
                    step(dve.tensor_tensor(n0b[:], n0b[:], bh[:, 0, :].unsqueeze(2).broadcast_to([DB, HC, DC]), ALU.mult))
                    dve.tensor_tensor(n0b[:], n0b[:], pu[0:DB, :].rearrange("p (h n) -> p h n", h=HC),
                                      ALU.add).then_inc(fin, 1)
                else:
                    dve.wait_ge(turned, 1)
                    dve.tensor_copy(cT[:], dd[:]).then_inc(fin, 1)


def output(nc, d, k):
    GW = 1036
    CW = 2 * HC * HEAD
    NSL = D // SLAB
    with Stage(nc, "ou") as s:
        att = s.sb("att", [P, 2, 2048])
        hc = s.sb("hc", [P, 2, HC * HEAD])
        g = s.sb("g", [P, 2, GW + CW])
        sg = s.sb("sg", [P, GW + CW])
        sq = s.sb("sq", [P, 1536])
        st = s.sb("st", [P, 5, 3, 12])
        ga = s.sb("ga", [P, HEAD])
        gc = s.sb("gc", [P, HEAD])
        mixT = s.sb("mixT", [P, KC, ROWS])
        w = s.sb("w", [P, 2, KC, SLAB])
        out = s.sb("out", [P, 2, 5, SLAB])
        tp = [s.ps(f"tp{i}", [P, 4, P]) for i in range(3)]
        ps = [s.ps(f"ps{i}", [P, SLAB]) for i in range(5)]
        loaded = s.sems("loaded", 2)
        gains_loaded = s.sem("gains_loaded")
        w_loaded = s.sems("w_loaded", 2)
        x_loaded = s.sems("x_loaded", 2)
        gains_ready = s.sem("gains_ready")
        squashed = s.sem("squashed")
        gated = s.sem("gated")
        summed = s.sem("summed")
        rooted = s.sem("rooted")
        dve_step = s.sem("dve_step")
        pool_step = s.sem("pool_step")
        mixed = s.sem("mixed")
        turned = s.sem("turned")
        copied = s.sem("copied")
        product_ready = s.sem("product_ready")
        y_ready = s.sem("y_ready")
        w_used = s.sem("w_used")
        stored = s.sems("stored", 2)
        wv = d.w_out.rearrange("(c p) n -> p c n", p=P)

        with nc.Block() as block:
            @block.sync
            def _(sp):
                def load_tile(t):
                    r0, rows = TILES[t]
                    i = t % 2
                    if t >= 2:
                        sp.wait_ge(turned, 4 * (t - 1))
                        sp.wait_ge(gated, t - 1)
                    for dst, src in ((att[0:rows, i, :], d.o_att[r0:r0 + rows, :]),
                                     (hc[0:rows, i, :], d.h_c[r0:r0 + rows, :]),
                                     (g[0:rows, i, 0:512], d.proj[r0:r0 + rows, C_AZ:C_BQ]),
                                     (g[0:rows, i, 512:GW], d.proj[r0:r0 + rows, C_BG:C_CQK]),
                                     (g[0:rows, i, GW:GW + CW], d.proj[r0:r0 + rows, C_CO:N_IN])):
                        sp.dma_start(dst, src).then_inc(loaded[i], 16)

                def load_slab(n):
                    i = n % 2
                    sp.dma_start(w[:, i, :, :], wv[:, :, SLAB * n:SLAB * n + SLAB]).then_inc(w_loaded[i], 16)
                    for t, (r0, rows) in enumerate(TILES):
                        src = d.x_prompt[r0:r0 + rows, :] if t < PT else d.x_sample
                        sp.dma_start(out[0:rows, i, t, :], src[:, SLAB * n:SLAB * n + SLAB]).then_inc(x_loaded[i], 16)

                load_tile(0)
                load_tile(1)
                load_slab(0)
                for t in range(2, 5):
                    load_tile(t)
                load_slab(1)
                for n in range(NSL):
                    for t, (r0, rows) in enumerate(TILES):
                        dst = d.y_p[r0:r0 + rows, :] if t < PT else d.y_s
                        sp.wait_ge(y_ready, 5 * n + t + 1)
                        sp.dma_start(dst[:, SLAB * n:SLAB * n + SLAB], out[0:rows, n % 2, t, :]).then_inc(stored[n % 2], 16)
                    if n + 2 < NSL:
                        sp.wait_ge(w_used, n + 1)
                        sp.wait_ge(stored[n % 2], 80 * (n // 2 + 1))
                        load_slab(n + 2)
                for i in range(2):
                    sp.wait_ge(stored[i], 40 * NSL)

            @block.gpsimd
            def _(pool):
                pool.dma_start(ga[:], d.a_out_g.partition_broadcast(P)).then_inc(gains_loaded, 16)
                pool.dma_start(gc[:], d.c_out_g.partition_broadcast(P)).then_inc(gains_loaded, 16)
                n = 0
                for t, (r0, rows) in enumerate(TILES):
                    i = t % 2
                    pool.wait_ge(squashed, t + 1)
                    for a, b in ((0, 512), (GW - 512, GW), (GW + 1024, GW + CW)):
                        pool.tensor_tensor(g[0:rows, i, a:b], g[0:rows, i, a:b], sg[0:rows, a:b],
                                           ALU.mult).then_inc(pool_step, 1)
                    n += 3
                    pool.wait_ge(pool_step, n)
                    pool.tensor_tensor(g[0:rows, i, GW:GW + 1024], g[0:rows, i, GW + 1024:GW + CW],
                                       sg[0:rows, GW:GW + 1024], ALU.mult).then_inc(gated, 1)

            @block.scalar
            def _(act):
                def copy_out(t):
                    r0, rows = TILES[t]
                    for q in range(4):
                        act.wait_ge(turned, 4 * t + q + 1)
                        act.activation(mixT[:, 4 * q:4 * q + 4, r0:r0 + rows], tp[(4 * t + q) % 3][:, :, 0:rows],
                                       ACT.Copy).then_inc(copied, 1)

                for t, (r0, rows) in enumerate(TILES):
                    act.wait_ge(loaded[t % 2], 80 * (t // 2 + 1))
                    if t:
                        act.wait_ge(mixed, t)
                        act.wait_ge(gated, t)
                    act.activation(sg[0:rows, :], g[0:rows, t % 2, :], ACT.Sigmoid).then_inc(squashed, 1)
                    act.wait_ge(summed, t + 1)
                    act.activation(st[0:rows, t, 1, :], st[0:rows, t, 0, :], ACT.Sqrt, bias=k.eps[0:rows, :],
                                   scale=1.0 / HEAD).then_inc(rooted, 1)
                    if t:
                        copy_out(t - 1)
                copy_out(4)

            @block.vector
            def _(dve):
                step = Chain(dve, dve_step)
                dve.wait_ge(gains_loaded, 32)
                step(dve.tensor_scalar(ga[:], ga[:], 1.0 - LAM0, None, ALU.mult))
                for t, (r0, rows) in enumerate(TILES):
                    i = t % 2
                    heads = lambda v: v.rearrange("p (h n) -> p h n", n=HEAD)
                    A, C = heads(att[0:rows, i, 0:512]), heads(hc[0:rows, i, :])
                    dve.wait_ge(loaded[i], 80 * (t // 2 + 1))
                    dve.tensor_tensor(heads(sq[0:rows, 0:512]), A, A, ALU.mult)
                    step(dve.tensor_tensor(heads(sq[0:rows, 512:1536]), C, C, ALU.mult))
                    dve.wait_ge(dve_step, step.n)
                    dve.tensor_reduce(st[0:rows, t, 0, :], heads(sq[0:rows, :]), AX_X, ALU.add).then_inc(summed, 1)
                    dve.wait_ge(squashed, t + 1)
                    gates = sg[0:rows, 512:524].rearrange("p (h n) -> p h n", n=3)
                    br = [heads(att[0:rows, i, 512 * (x + 1):512 * (x + 2)]) for x in range(3)]
                    for x, gate in ((0, 1), (1, 2), (2, 0)):
                        last = dve.tensor_tensor(br[x], br[x], gates[:, :, gate:gate + 1].broadcast_to(
                            [rows, HB, HEAD]), ALU.mult)
                    step(last)
                    step(dve.tensor_tensor(br[0], br[0], br[1], ALU.add))
                    step(dve.tensor_tensor(br[0], br[0], br[2], ALU.add))
                    dve.wait_ge(rooted, t + 1)
                    step(dve.reciprocal(st[0:rows, t, 2, :], st[0:rows, t, 1, :]))
                    dve.tensor_tensor(A, A, st[0:rows, t, 2, 0:HA].unsqueeze(2).broadcast_to([rows, HA, HEAD]), ALU.mult)
                    step(dve.tensor_tensor(C, C, st[0:rows, t, 2, HA:12].unsqueeze(2).broadcast_to([rows, HC, HEAD]),
                                           ALU.mult))
                    dve.tensor_tensor(A, A, ga[0:rows, :].unsqueeze(1).broadcast_to([rows, HA, HEAD]), ALU.mult)
                    step(dve.tensor_tensor(C, C, gc[0:rows, :].unsqueeze(1).broadcast_to([rows, HC, HEAD]), ALU.mult))
                    dve.wait_ge(gated, t + 1)
                    dve.tensor_tensor(A, A, heads(g[0:rows, i, 0:512]), ALU.mult)
                    dve.tensor_tensor(br[0], br[0], heads(g[0:rows, i, GW - 512:GW]), ALU.mult)
                    dve.tensor_tensor(C, C, heads(g[0:rows, i, GW:GW + 1024]), ALU.mult).then_inc(mixed, 1)
                for n in range(NSL):
                    dve.wait_ge(x_loaded[n % 2], 80 * (n // 2 + 1))
                    for t, (r0, rows) in enumerate(TILES):
                        dve.wait_ge(product_ready, 5 * n + t + 1)
                        dve.tensor_tensor(out[0:rows, n % 2, t, :], out[0:rows, n % 2, t, :], ps[t][0:rows, :],
                                          ALU.add).then_inc(y_ready, 1)

            @block.tensor
            def _(pe):
                def turn(t):
                    rows = TILES[t][1]
                    pe.wait_ge(mixed, t + 1)
                    for q in range(4):
                        m = 4 * t + q
                        if m >= 3:
                            pe.wait_ge(copied, m - 2)
                        src = (att, hc)[q // 2][:, t % 2, 512 * (q % 2):512 * (q % 2) + 512]
                        for c in range(4):
                            last = pe.transpose(tp[m % 3][:, c, 0:rows], src[0:rows, P * c:P * c + P],
                                                k.ident[0:rows, 0:rows])
                        last.then_inc(turned, 1)

                def multiply(n, t):
                    r0, rows = TILES[t]
                    if n == 0:
                        pe.wait_ge(copied, 4 * t + 4)
                    else:
                        pe.wait_ge(y_ready, 5 * n + t - 4)
                    for c in range(KC):
                        last = pe.matmul(ps[t][0:rows, :], mixT[:, c, r0:r0 + rows], w[:, n % 2, c, :],
                                         start=(c == 0), stop=(c == KC - 1))
                    last.then_inc(product_ready, 1)

                turn(0)
                for n in range(NSL):
                    pe.wait_ge(w_loaded[n % 2], 16 * (n // 2 + 1))
                    for t in range(5):
                        if n == 0 and t + 1 < 5:
                            turn(t + 1)
                        multiply(n, t)
                    pe.wait_ge(product_ready, 5 * n + 5)
                    pe.sem_inc(w_used, 1)


def stages(nc, d, k, s):
    k.eps = s.sb("eps", [P, 1])
    k.ones = s.sb("ones", [P, P])
    k.causal = s.sb("causal", [P, P])
    k.poolw = s.sb("poolw", [P, 2, 2])
    k.g_kc = s.sb("g_kc", [P, 1])
    k.neglam = s.sb("neglam", [P, 1])
    project(nc, d, k)
    constants(nc, d, k)
    with Stage(nc, "at") as a:
        k.rows_s = a.sb("rows_s", [NS, TW])
        k.attT = a.sb("attT", [P, XCH, ROWS])
        k.selb = a.sb("selb", [NBLK, DB, NBLK])
        with Stage(nc, "ap") as p:
            k.rows_p = p.sb("rows_p", [P, PT, TW])
            prepare(nc, d, k)
            prompt_attend(nc, d, k)
            compress(nc, d, k)
        decode_attend(nc, d, k)
    with Stage(nc, "ml") as c:
        k.qkT = c.sb("qkT", [P, 8, ROWS])
        k.k_rows = c.sb("k_rows", [P, 5, HC * DC])
        k.gate_i = c.sb("gate_i", [HC, ROWS])
        k.gate_f = c.sb("gate_f", [HC, ROWS])
        convolve(nc, d, k)
        mlstm(nc, d, k, False)
        mlstm(nc, d, k, True)
    output(nc, d, k)


class Names:
    pass


INPUTS = ["x_prompt", "x_sample", "cache_a_kv", "cache_b_kv", "state_b_win", "state_c_conv", "state_c_C",
          "state_c_n", "state_c_m", "page_table", "norm_g", "w_in", "w_out", "a_qk_g", "a_lambda", "a_out_g",
          "b_qk_g", "b_cmp_w", "c_conv_w", "c_conv_b", "c_gate_b", "c_out_g"]
QKC = 2 * HC * DC
OUTPUTS = [(1, SEQ, D), (DB, DT, D), (1, 1, SEQ, 2, HA, HEAD), (1, DB, DT, 2, HA, HEAD),
           (1, 1, SEQ, 4, HEAD), (1, DB, DT, 4, HEAD), (1, 1, WIN, 2, HEAD), (1, DB, WIN, 2, HEAD),
           (1, 1, 3, QKC), (1, DB, 3, QKC), (1, 1, HC, HEAD, DC), (1, DB, HC, HEAD, DC),
           (1, 1, HC, DC), (1, DB, HC, DC), (1, 1, HC), (1, DB, HC)]


def build(nc, a, o):
    d, k = Names(), Names()
    d.x_prompt = a["x_prompt"][0]
    d.x_sample = a["x_sample"].rearrange("b t d -> (b t) d")
    d.cache_a = a["cache_a_kv"][0].rearrange("n p a h d -> n p (a h d)")
    d.cache_b = a["cache_b_kv"][0].rearrange("n p a d -> n p (a d)")
    d.b_win = a["state_b_win"][0].rearrange("b w a d -> b w (a d)")
    d.c_conv = a["state_c_conv"][0]
    d.c_C, d.c_n, d.c_m = a["state_c_C"][0], a["state_c_n"][0], a["state_c_m"][0]
    d.page_table = a["page_table"]
    d.norm_g, d.w_in, d.w_out = a["norm_g"][0], a["w_in"][0], a["w_out"][0]
    d.a_qk_g, d.a_lambda, d.a_out_g = a["a_qk_g"][0], a["a_lambda"][0], a["a_out_g"][0]
    d.b_qk_g, d.b_cmp_w, d.c_conv_w = a["b_qk_g"][0], a["b_cmp_w"][0], a["c_conv_w"][0]
    d.c_conv_b, d.c_gate_b, d.c_out_g = a["c_conv_b"][0], a["c_gate_b"][0], a["c_out_g"][0]
    d.y_p, d.y_s = o[0][0], o[1].rearrange("b t d -> (b t) d")
    d.a_kv_p = o[2][0, 0].rearrange("t a h d -> t (a h d)")
    d.a_kv_s = o[3][0].rearrange("b t a h d -> (b t) (a h d)")
    d.b_kv_p = o[4][0, 0].rearrange("t a d -> t (a d)")
    d.b_kv_s = o[5][0].rearrange("b t a d -> (b t) (a d)")
    d.win_p = o[6][0, 0].rearrange("t a d -> t (a d)")
    d.win_s = o[7][0].rearrange("b t a d -> b t (a d)")
    d.conv_p, d.conv_s = o[8][0, 0], o[9][0]
    d.C_p, d.C_s, d.n_p, d.n_s = o[10][0, 0], o[11][0], o[12][0, 0], o[13][0]
    d.m_p, d.m_s = o[14][0, 0], o[15][0]
    d.proj = nc.dram_tensor("proj", [ROWS, N_IN], F32).ap()
    d.o_att = nc.dram_tensor("o_att", [ROWS, 4 * 512], F32).ap()
    d.h_c = nc.dram_tensor("h_c", [ROWS, HC * HEAD], F32).ap()
    with Stage(nc, "all") as s:
        k.ident = s.sb("ident", [P, P])
        stages(nc, d, k, s)


def kernel(**inputs):
    import numpy as np
    import concourse.bacc as bacc
    from concourse.bass_utils import run_bass_kernel_spmd

    nc = bacc.Bacc("TRN2", target_bir_lowering=False, num_devices=1)
    arrays, a = {}, {}
    for name in INPUTS:
        v = np.ascontiguousarray(inputs[name])
        arrays[f"in_{name}"] = v
        a[name] = nc.dram_tensor(f"in_{name}", v.shape, mybir.dt.from_np(v.dtype), kind="ExternalInput").ap()
    o = [nc.dram_tensor(f"out_{i}", shape, F32, kind="ExternalOutput").ap() for i, shape in enumerate(OUTPUTS)]
    build(nc, a, o)
    r = run_bass_kernel_spmd(nc, [arrays], core_ids=[0])
    return tuple(r.results[0][f"out_{i}"] for i in range(len(OUTPUTS)))
```

```python
from contextlib import ExitStack

import concourse.bass as bass
from concourse import mybir

F32 = mybir.dt.float32
I32 = mybir.dt.int32
F32R = mybir.dt.float32r
ACT = mybir.ActivationFunctionType
ALU = mybir.AluOpType
AX_X = mybir.AxisListType.X

P = 128
D = 2048
KC = D // P
SEQ = 512
DB, DT = 8, 4
NS = DB * DT
ROWS = SEQ + NS
PT = SEQ // P
TILES = [(P * t, P) for t in range(PT)] + [(SEQ, NS)]
N_IN = 7964
HEAD = 128
HA, HB, HC = 4, 4, 8
DC = 64
PAGE = 128
PAGES = 32
PAST = PAGE * PAGES
CMP = 64
NBLK = PAST // CMP
WIN = 512
EPS = 1e-6
LAM0 = 0.8 - 0.6
NEG = -1.0e30
A_SCALE = DC ** -0.5
B_SCALE = HEAD ** -0.5

C_AQ, C_AZ, C_BQ, C_BG, C_BZ = 0, 1536, 2048, 3328, 3340
C_CQK, C_CV, C_CIF, C_CO, C_CZ = 3852, 4876, 5900, 5916, 6940
T_AQ, T_AK, T_AV, T_BQ, T_KC = 0, 512, 1024, 1536, 2048
T_VC, T_KS, T_VS, T_KW, T_VW = 2176, 2304, 2432, 2560, 2688
TW = 2816
X_AQ, X_AK, X_BQ, X_KS, X_KW = 0, 4, 8, 12, 13
XCH = 14
X_COL = [T_AQ + HEAD * h for h in range(HA)] + [T_AK + HEAD * h for h in range(HA)] \
    + [T_BQ + HEAD * h for h in range(HB)] + [T_KS, T_KW]
SLAB = 512


class Stage:

    def __init__(self, nc, name):
        self.nc, self.name, self.stack, self.used = nc, name, ExitStack(), []

    def __enter__(self):
        self.stack.__enter__()
        return self

    def __exit__(self, *e):
        if self.used and e[0] is None:
            self.nc.clear_and_free_semaphores(self.used)
            self.nc.all_engine_barrier()
        return self.stack.__exit__(*e)

    def sb(self, name, shape, dt=F32):
        return self.stack.enter_context(self.nc.sbuf_tensor(f"{self.name}_{name}", shape, dt))

    def ps(self, name, shape, dt=F32):
        return self.stack.enter_context(self.nc.psum_tensor(f"{self.name}_{name}", shape, dt))

    def sem(self, name):
        self.used.append(self.nc.alloc_semaphore(f"{self.name}_{name}"))
        return self.used[-1]

    def sems(self, name, n):
        return [self.sem(f"{name}{i}") for i in range(n)]


class Chain:

    def __init__(self, eng, sem):
        self.eng, self.sem, self.n = eng, sem, 0

    def __call__(self, ins):
        self.n += 1
        ins.then_inc(self.sem, 1)
        self.eng.wait_ge(self.sem, self.n)


def project(nc, d, k):
    NSLAB = -(-N_IN // SLAB)
    LAST = N_IN - (NSLAB - 1) * SLAB
    PC, RING = 2, 4
    NP = KC // PC
    HALF = DB * PAGES // NSLAB
    assert HALF * 2 == PAGES and HALF == 16
    with Stage(nc, "pj") as s:
        x = s.sb("x", [P, 2, D])
        ssq = s.sb("ssq", [P, 8])
        rms = s.sb("rms", [P, 8])
        rstd = s.sb("rstd", [P, 8])
        gain = s.sb("gain", [P, KC])
        eps = s.sb("eps", [P, 1])
        w = s.sb("w", [P, 2, PC, SLAB])
        whi = s.sb("whi", [P, RING, PC, SLAB], F32R)
        wlo = s.sb("wlo", [P, RING, PC, SLAB], F32R)
        table = s.sb("table", [1, DB * PAGES], I32)
        pages = s.sb("pages", [P, 2, 4, 2 * HEAD])
        out = s.sb("out", [P, 5, SLAB])
        low = s.sb("low", [NS, SLAB])
        ps = [s.ps(f"ps{i}", [P, SLAB]) for i in range(8)]
        xg = s.sb("xg", [P, 2, 4, P])
        sq = out[:, 0:4, :].rearrange("p a n -> p (a n)")
        xhi = s.sb("xhi", [P, KC, SEQ], F32R)
        xlo = s.sb("xlo", [P, KC, SEQ], F32R)
        xs = s.sb("xs", [P, KC, 2 * NS], F32R)

        x_loaded = s.sems("x_loaded", 2)
        gain_loaded = s.sem("gain_loaded")
        ident_ready = s.sem("ident_ready")
        squared = s.sem("squared")
        rooted = s.sem("rooted")
        inverted = s.sem("inverted")
        scaled = s.sem("scaled")
        turned = s.sem("turned")
        xg_ready = s.sem("xg_ready")
        xhi_ready = s.sem("xhi_ready")
        xlo_ready = s.sem("xlo_ready")
        w_loaded = s.sems("w_loaded", 2)
        whi_ready = s.sem("whi_ready")
        wlo_ready = s.sem("wlo_ready")
        w_used = s.sem("w_used")
        store_turn = s.sem("store_turn")
        table_loaded = s.sem("table_loaded")
        z_zeroed = s.sem("z_zeroed")
        z_loaded = s.sem("z_loaded")
        pages_loaded = s.sems("pages_loaded", 2)
        pages_used = s.sem("pages_used")
        pool_out = s.sem("pool_out")
        product_ready = s.sems("product_ready", 5)
        low_out = s.sem("low_out")
        evacuated = s.sems("evacuated", 5)
        stored = s.sems("stored", 5)
        wv = d.w_in.rearrange("(c p) n -> p c n", p=P)

        def high(t):
            return xhi[:, :, P * t:P * t + P] if t < PT else xs[:, :, 0:NS]

        def low_part(t):
            return xlo[:, :, P * t:P * t + P] if t < PT else xs[:, :, NS:2 * NS]

        with nc.Block() as block:
            @block.sync
            def _(sp):
                def load_x(t):
                    r0, rows = TILES[t]
                    src = d.x_prompt[r0:r0 + rows, :] if t < PT else d.x_sample
                    if t >= 2:
                        sp.wait_ge(turned, 4 * (t - 1))
                    sp.dma_start(x[0:rows, t % 2, :], src).then_inc(x_loaded[t % 2], 16)

                def load_w(j, c, n):
                    sp.dma_start(w[:, c % 2, :, 0:n],
                                 wv[:, PC * c:PC * c + PC, bass.ds(j * SLAB, n)]).then_inc(w_loaded[c % 2], 16)

                def store(j, t, n):
                    r0, rows = TILES[t]
                    sp.wait_ge(evacuated[t], j + 2)
                    sp.sem_inc(store_turn, 1)
                    sp.dma_start(d.proj[r0:r0 + rows, bass.ds(j * SLAB, n)],
                                 out[0:rows, t, 0:n]).then_inc(stored[t], 16)

                def load_next(j, c, n):
                    sp.wait_ge(wlo_ready, j * NP + c + 1)
                    load_w(j + (c + 2) // NP, (c + 2) % NP, n)

                def step(j, here, after):
                    for c in range(RING, NP):
                        if c + 2 < NP or after:
                            load_next(j, c, here if c + 2 < NP else after)
                    for c in range(RING - 1):
                        if after:
                            load_next(j + 1, c, after)
                    for t in range(5):
                        store(j, t, here)
                    if after:
                        load_next(j + 1, RING - 1, after)

                for t in range(5):
                    sp.sem_inc(stored[t], 16)
                load_x(0)
                load_x(1)
                load_w(0, 0, SLAB)
                load_w(0, 1, SLAB)
                for t in range(2, 5):
                    load_x(t)
                for c in range(RING):
                    load_next(0, c, SLAB)
                with sp.Fori(0, NSLAB - 2) as j:
                    step(j, SLAB, SLAB)
                step(NSLAB - 2, SLAB, LAST)
                step(NSLAB - 1, LAST, None)
                for t in range(5):
                    sp.wait_ge(stored[t], 16 + 16 * NSLAB)

            @block.gpsimd
            def _(pool):
                pool.dma_start(gain[:], d.norm_g.rearrange("(c p) -> p c", p=P),
                               allow_slow_non_contiguous=True).then_inc(gain_loaded, 16)
                pool.memset(k.z[:], 0.0).then_inc(z_zeroed, 1)
                pool.wait_ge(z_zeroed, 1)
                for a in range(2):
                    for j in range(2):
                        pool.dma_start(k.z[CMP * j:CMP * (j + 1), 30 + 32 * a + j:31 + 32 * a + j],
                                       d.b_cmp_w[a, :].unsqueeze(1)).then_inc(z_loaded, 16)
                pool.memset(eps[:], EPS).then_inc(ident_ready, 1)
                pool.memset(k.ident[:], 0.0).then_inc(ident_ready, 1)
                pool.wait_ge(ident_ready, 2)
                pool.affine_select(out=k.ident[:], in_=k.ident[:], compare_op=ALU.not_equal, fill=1.0,
                                   base=0, pattern=[[-1, P]], channel_multiplier=1).then_inc(ident_ready, 1)

            @block.scalar
            def _(act):
                def split_x(t):
                    for q in range(4):
                        n = 4 * t + q
                        act.wait_ge(xg_ready, n + 1)
                        act.activation(high(t)[:, 4 * q:4 * q + 4, :], xg[:, n % 2, :, 0:TILES[t][1]],
                                       ACT.Copy).then_inc(xhi_ready, 1)

                def split_w(j, c, n):
                    act.wait_ge(w_loaded[c % 2], j * (8 * NP) + 16 * (c // 2) + 16)
                    act.wait_ge(w_used, j * NP + c + 1)
                    act.activation(whi[:, c % RING, :, 0:n], w[:, c % 2, :, 0:n], ACT.Copy).then_inc(whi_ready, 1)

                def load_pages(j, q):
                    act.wait_ge(pages_used, j * 4 + q + 1)
                    for i in range(4):
                        page = act.value_load(table[0:1, bass.ds(j * HALF + 4 * q + i, 1)],
                                              min_val=0, max_val=d.cache_b.shape[0] - 1)
                        act.dma_start(pages[:, q % 2, i, :], d.cache_b[bass.ds(page, 1), :, 0:2 * HEAD]
                                      .rearrange("a p n -> p (a n)")).then_inc(pages_loaded[q % 2], 16)

                act.dma_start(table[:], d.page_table.rearrange("(a b) n -> a (b n)", a=1)).then_inc(table_loaded, 16)
                act.sem_inc(pages_used, 2)
                act.sem_inc(pool_out, 1)
                act.wait_ge(ident_ready, 1)
                for t, (_, rows) in enumerate(TILES):
                    act.wait_ge(x_loaded[t % 2], 16 * (t // 2 + 1))
                    act.activation(sq[0:rows, :], x[0:rows, t % 2, :], ACT.Square,
                                   accum_out=ssq[0:rows, t:t + 1]).then_inc(squared, 1)
                    act.wait_ge(squared, t + 1)
                    act.activation(rms[0:rows, t:t + 1], ssq[0:rows, t:t + 1], ACT.Sqrt,
                                   bias=eps[0:rows, :], scale=1.0 / D).then_inc(rooted, 1)
                    if t:
                        split_x(t - 1)
                        split_w(0, t - 1, SLAB)
                split_x(4)
                act.wait_ge(table_loaded, 16)
                load_pages(0, 0)
                load_pages(0, 1)

                def step(j, width, after):
                    split_w(j, 4, width)
                    load_pages(j, 2)
                    split_w(j, 5, width)
                    split_w(j, 6, width)
                    load_pages(j, 3)
                    split_w(j, 7, width)
                    if after:
                        split_w(j + 1, 0, after)
                        load_pages(j + 1, 0)
                        split_w(j + 1, 1, after)
                        split_w(j + 1, 2, after)
                        load_pages(j + 1, 1)
                    act.wait_ge(pages_used, j * 4 + 6)
                    for a in range(2):
                        last = act.activation(k.pkv[:, bass.ds(j, 1), HEAD * a:HEAD * a + HEAD],
                                              ps[7][32 * a:32 * a + 32, HEAD * a:HEAD * a + HEAD].unsqueeze(1),
                                              ACT.Copy)
                    last.then_inc(pool_out, 1)
                    for t in (1, 3):
                        act.wait_ge(product_ready[t], j + 1)
                        act.wait_ge(stored[t], j * 16 + 16)
                        act.activation(out[:, t, 0:width], ps[t][:, 0:width], ACT.Copy).then_inc(evacuated[t], 1)
                    act.wait_ge(product_ready[4], j + 1)
                    act.wait_ge(evacuated[4], j + 1)
                    act.activation(low[:, 0:width], ps[4][NS:2 * NS, 0:width], ACT.Copy).then_inc(low_out, 1)
                    if after:
                        split_w(j + 1, 3, after)

                with act.Fori(0, NSLAB - 2) as j:
                    step(j, SLAB, SLAB)
                step(NSLAB - 2, SLAB, LAST)
                step(NSLAB - 1, LAST, None)

            @block.vector
            def _(dve):
                def split_x(n):
                    t, q = n // 4, n % 4
                    dve.wait_ge(xhi_ready, n + 1)
                    dve.tensor_tensor(low_part(t)[:, 4 * q:4 * q + 4, :], xg[:, n % 2, :, 0:TILES[t][1]],
                                      high(t)[:, 4 * q:4 * q + 4, :], ALU.subtract).then_inc(xlo_ready, 1)

                def split_w(j, c, n):
                    dve.wait_ge(whi_ready, j * NP + c + 1)
                    dve.tensor_tensor(wlo[:, c % RING, :, 0:n], w[:, c % 2, :, 0:n], whi[:, c % RING, :, 0:n],
                                      ALU.subtract).then_inc(wlo_ready, 1)

                for t in range(5):
                    dve.sem_inc(evacuated[t], 1)
                dve.sem_inc(w_used, RING)
                dve.wait_ge(gain_loaded, 16)
                for t, (r0, rows) in enumerate(TILES):
                    dve.wait_ge(rooted, t + 1)
                    dve.reciprocal(rstd[0:rows, t:t + 1], rms[0:rows, t:t + 1]).then_inc(inverted, 1)
                    dve.wait_ge(inverted, t + 1)
                    dve.tensor_scalar(x[0:rows, t % 2, :], x[0:rows, t % 2, :], rstd[0:rows, t:t + 1],
                                      None, ALU.mult).then_inc(scaled, 1)
                    for q in range(4):
                        n = 4 * t + q
                        dve.wait_ge(turned, n + 1)
                        if n >= 2:
                            dve.wait_ge(xlo_ready, n - 1)
                        dve.tensor_tensor(
                            xg[:, n % 2, :, 0:rows],
                            ps[n % 2 + 5][:, :].rearrange("p (c r) -> p c r", c=4)[:, :, 0:rows],
                            gain[:, 4 * q:4 * q + 4].unsqueeze(2).broadcast_to([P, 4, rows]),
                            ALU.mult).then_inc(xg_ready, 1)
                        if q:
                            split_x(n - 1)
                    split_x(4 * t + 3)
                    if t >= 2:
                        split_w(0, t - 2, SLAB)
                split_w(0, 3, SLAB)

                def step(j, width, after):
                    for c in range(RING, NP):
                        split_w(j, c, width)
                    if after:
                        for c in range(3):
                            split_w(j + 1, c, after)
                    for t in (0, 2):
                        dve.wait_ge(product_ready[t], j + 1)
                        dve.wait_ge(stored[t], j * 16 + 16)
                        dve.tensor_copy(out[:, t, 0:width], ps[t][:, 0:width]).then_inc(evacuated[t], 1)
                    dve.wait_ge(low_out, j + 1)
                    dve.wait_ge(stored[4], j * 16 + 16)
                    dve.tensor_tensor(out[0:NS, 4, 0:width], ps[4][0:NS, 0:width], low[:, 0:width],
                                      ALU.add).then_inc(evacuated[4], 1)
                    if after:
                        split_w(j + 1, 3, after)

                with dve.Fori(0, NSLAB - 2) as j:
                    step(j, SLAB, SLAB)
                step(NSLAB - 2, SLAB, LAST)
                step(NSLAB - 1, LAST, None)

            @block.tensor
            def _(pe):
                pe.wait_ge(ident_ready, 3)
                for t, (r0, rows) in enumerate(TILES):
                    pe.wait_ge(scaled, t + 1)
                    for q in range(4):
                        n = 4 * t + q
                        if n >= 2:
                            pe.wait_ge(xg_ready, n - 1)
                        for c in range(4):
                            col = (4 * q + c) * P
                            last = pe.transpose(ps[n % 2 + 5][:, c * P:c * P + rows],
                                                x[0:rows, t % 2, col:col + P], k.ident[0:rows, 0:rows])
                        last.then_inc(turned, 1)

                def pool_pages(j, q):
                    if q == 0:
                        pe.wait_ge(pool_out, j + 1)
                    pe.wait_ge(pages_loaded[q % 2], j * 128 + 64 * (q // 2) + 64)
                    for i in range(4):
                        p = 4 * q + i
                        last = pe.matmul(ps[7][0:64, 0:2 * HEAD], k.z[:, 30 - 2 * p:94 - 2 * p],
                                         pages[:, q % 2, i, :], start=(p == 0), stop=(p == HALF - 1))
                    last.then_inc(pages_used, 1)

                def multiply(j, width):
                    for c in range(NP):
                        pe.wait_ge(wlo_ready, j * NP + c + 1)
                        for t in range(5):
                            if c == 0:
                                pe.wait_ge(evacuated[t], j + 1)
                            for i in range(PC):
                                kc = PC * c + i
                                first, end = kc == 0, kc == KC - 1
                                high, low = whi[:, c % RING, i, 0:width], wlo[:, c % RING, i, 0:width]
                                if t < PT:
                                    acc = ps[t][:, 0:width]
                                    hi, lo = (v[:, kc, P * t:P * t + P] for v in (xhi, xlo))
                                    pe.matmul(acc, hi, high, start=first, stop=False)
                                    pe.matmul(acc, hi, low, start=False, stop=False)
                                    last = pe.matmul(acc, lo, high, start=False, stop=end)
                                else:
                                    acc = ps[t][0:2 * NS, 0:width]
                                    pe.matmul(acc, xs[:, kc, :], high, start=first, stop=False)
                                    last = pe.matmul(acc, xs[:, kc, :], low, start=False, stop=end)
                            if c == NP - 1:
                                last.then_inc(product_ready[t], 1)
                        if c < NP - 1:
                            last.then_inc(w_used, 1)
                        if c % 2 == 0:
                            pool_pages(j, c // 2)
                    pe.wait_ge(product_ready[4], j + 1)
                    pe.sem_inc(w_used, 1)

                pe.wait_ge(z_loaded, 64)
                pe.wait_ge(xlo_ready, 20)
                with pe.Fori(0, NSLAB - 1) as j:
                    multiply(j, SLAB)
                multiply(NSLAB - 1, LAST)


def prepare(nc, d, k):
    with Stage(nc, "pr") as s:
        sq = s.sb("sq", [P, 1792])
        ss = s.sb("ss", [P, 5, 32])
        rms = s.sb("rms", [P, 5, 32])
        rstd = s.sb("rstd", [P, 5, 32])
        eps = s.sb("eps", [P, 1])
        ga = s.sb("ga", [P, 2, DC])
        gb = s.sb("gb", [P, 4, HEAD])
        ps = [s.ps(f"ps{i}", [P, 512]) for i in range(4)]
        tiles_loaded = s.sems("tiles_loaded", 5)
        gains_loaded = s.sem("gains_loaded")
        dve_step = s.sem("dve_step")
        eps_ready = s.sem("eps_ready")
        summed = s.sem("summed")
        rooted = s.sem("rooted")
        normed = s.sem("normed")
        turned = s.sem("turned")
        copied = s.sem("copied")
        stored = s.sem("stored")
        NQ = -(-XCH // 4)

        def tile(t):
            return k.rows_p[:, t, :] if t < PT else k.rows_s[:, :]

        with nc.Block() as block:
            @block.sync
            def _(sp):
                for t, (r0, rows) in enumerate(TILES):
                    sp.dma_start(tile(t)[0:rows, 0:T_BQ], d.proj[r0:r0 + rows, 0:C_AZ]).then_inc(tiles_loaded[t], 16)
                    sp.dma_start(tile(t)[0:rows, T_BQ:TW],
                                 d.proj[r0:r0 + rows, C_BQ:C_BG]).then_inc(tiles_loaded[t], 16)
                n = 0
                for b in range(DB):
                    sp.dma_start(d.win_s[b, 0:WIN - DT, :], d.b_win[b, DT:WIN, :]).then_inc(stored, 16)
                    n += 16
                for t, (r0, rows) in enumerate(TILES):
                    a, b, win = ((d.a_kv_p, d.b_kv_p, d.win_p) if t < PT else (d.a_kv_s, d.b_kv_s, None))
                    q0 = r0 if t < PT else 0
                    sp.wait_ge(normed, t + 1)
                    sp.dma_start(a[q0:q0 + rows, :], tile(t)[0:rows, T_AK:T_BQ]).then_inc(stored, 16)
                    sp.dma_start(b[q0:q0 + rows, :], tile(t)[0:rows, T_KC:T_KW]).then_inc(stored, 16)
                    n += 32
                    if win is not None:
                        sp.dma_start(win[q0:q0 + rows, :], tile(t)[0:rows, T_KW:TW]).then_inc(stored, 16)
                        n += 16
                for b in range(DB):
                    sp.dma_start(d.win_s[b, WIN - DT:WIN, :],
                                 tile(4)[DT * b:DT * b + DT, T_KW:TW]).then_inc(stored, 16)
                    n += 16
                sp.wait_ge(stored, n)

            @block.gpsimd
            def _(pool):
                pool.memset(eps[:], EPS).then_inc(eps_ready, 1)
                pool.dma_start(ga[:], d.a_qk_g.partition_broadcast(P)).then_inc(gains_loaded, 16)
                pool.dma_start(gb[:], d.b_qk_g.partition_broadcast(P)).then_inc(gains_loaded, 16)

            @block.scalar
            def _(act):
                act.wait_ge(eps_ready, 1)
                for t, (r0, rows) in enumerate(TILES):
                    act.wait_ge(summed, t + 1)
                    act.activation(rms[0:rows, t, 0:22], ss[0:rows, t, 0:22], ACT.Sqrt,
                                   bias=eps[0:rows, :]).then_inc(rooted, 1)
                n = 0
                for t, (r0, rows) in enumerate(TILES):
                    for q in range(NQ):
                        m = min(4, XCH - 4 * q)
                        n += 1
                        act.wait_ge(turned, n)
                        act.activation(k.attT[:, 4 * q:4 * q + m, r0:r0 + rows],
                                       ps[n % 4][:, :].rearrange("p (c r) -> p c r", c=4)[:, 0:m, 0:rows],
                                       ACT.Copy).then_inc(copied, 1)

            @block.vector
            def _(dve):
                step = Chain(dve, dve_step)
                dve.wait_ge(gains_loaded, 32)
                step(dve.tensor_scalar(ga[:, 0, :], ga[:, 0, :], A_SCALE, None, ALU.mult))
                step(dve.tensor_scalar(gb[:, 0, :], gb[:, 0, :], B_SCALE, None, ALU.mult))

                def heads(t, rows):
                    T = tile(t)
                    v = lambda c0, n, w: T[0:rows, c0:c0 + n * w].rearrange("p (h w) -> p h w", w=w)
                    return [(v(T_AQ, 8, DC), 0, ga[0:rows, 0, :]), (v(T_AK, 8, DC), 8, ga[0:rows, 1, :]),
                            (v(T_BQ, HB, HEAD), 16, gb[0:rows, 0, :]), (v(T_KS, 1, HEAD), 20, gb[0:rows, 2, :]),
                            (v(T_KW, 1, HEAD), 21, gb[0:rows, 3, :])]

                for t, (r0, rows) in enumerate(TILES):
                    dve.wait_ge(tiles_loaded[t], 32)
                    if t:
                        dve.wait_ge(dve_step, step.n)
                    at = 0
                    for v, c, _ in heads(t, rows):
                        n, w = v.shape[1], v.shape[2]
                        last = dve.tensor_tensor(sq[0:rows, at:at + n * w].rearrange("p (h w) -> p h w", w=w),
                                                 v, v, ALU.mult)
                        at += n * w
                        step(last)
                    step(dve.tensor_reduce(ss[0:rows, t, 0:16], sq[0:rows, 0:1024].rearrange(
                        "p (h w) -> p h w", w=DC), AX_X, ALU.add))
                    step(dve.tensor_reduce(ss[0:rows, t, 16:22], sq[0:rows, 1024:1792].rearrange(
                        "p (h w) -> p h w", w=HEAD), AX_X, ALU.add))
                    step(dve.tensor_scalar(ss[0:rows, t, 0:16], ss[0:rows, t, 0:16], 1.0 / DC, None, ALU.mult))
                    dve.tensor_scalar(ss[0:rows, t, 16:22], ss[0:rows, t, 16:22], 1.0 / HEAD, None,
                                      ALU.mult).then_inc(summed, 1)
                for t, (r0, rows) in enumerate(TILES):
                    dve.wait_ge(rooted, t + 1)
                    step(dve.reciprocal(rstd[0:rows, t, 0:22], rms[0:rows, t, 0:22]))
                    parts = heads(t, rows)
                    for v, c, _ in parts:
                        n, w = v.shape[1], v.shape[2]
                        step(dve.tensor_tensor(v, v, rstd[0:rows, t, c:c + n].unsqueeze(2).broadcast_to(
                            [rows, n, w]), ALU.mult))
                    for i, (v, c, g) in enumerate(parts):
                        n, w = v.shape[1], v.shape[2]
                        last = dve.tensor_tensor(v, v, g.unsqueeze(1).broadcast_to([rows, n, w]), ALU.mult)
                        if i < len(parts) - 1:
                            step(last)
                    last.then_inc(normed, 1)

            @block.tensor
            def _(pe):
                n = 0
                for t, (r0, rows) in enumerate(TILES):
                    pe.wait_ge(normed, t + 1)
                    for q in range(NQ):
                        n += 1
                        if n > 4:
                            pe.wait_ge(copied, n - 4)
                        for c in range(4 * q, min(4 * q + 4, XCH)):
                            last = pe.transpose(ps[n % 4][:, (c % 4) * P:(c % 4) * P + rows],
                                                tile(t)[0:rows, X_COL[c]:X_COL[c] + P],
                                                k.ident[0:rows, 0:rows])
                        last.then_inc(turned, 1)


def constants(nc, d, k):
    with Stage(nc, "ct") as s:
        lp = s.sb("lp", [P, 4, DC])
        prod = s.sb("prod", [P, 2, DC])
        dots = s.sb("dots", [P, 2])
        exps = s.sb("exps", [P, 2])
        loaded = s.sem("loaded")
        zeroed = s.sem("zeroed")
        made = s.sem("made")
        dve_step = s.sem("dve_step")
        dotted = s.sem("dotted")
        exped = s.sem("exped")
        with nc.Block() as block:
            @block.gpsimd
            def _(pool):
                pool.memset(k.eps[:], EPS).then_inc(made, 1)
                pool.memset(k.ones[:], 1.0).then_inc(made, 1)
                pool.memset(k.causal[:], 0.0).then_inc(zeroed, 1)
                pool.wait_ge(zeroed, 1)
                pool.affine_select(out=k.causal[:], in_=k.causal[:], compare_op=ALU.is_ge, fill=NEG,
                                   base=0, pattern=[[-1, P]], channel_multiplier=1).then_inc(made, 1)
                pool.dma_start(lp[:], d.a_lambda.partition_broadcast(P)).then_inc(loaded, 16)
                pool.wait_ge(made, 3)
                pool.wait_ge(loaded, 16)

            @block.vector
            def _(dve):
                step = Chain(dve, dve_step)
                dve.wait_ge(loaded, 16)
                step(dve.tensor_tensor(prod[:], lp[:, 0:4:2, :], lp[:, 1:4:2, :], ALU.mult))
                dve.tensor_reduce(dots[:], prod[:], AX_X, ALU.add).then_inc(dotted, 1)
                dve.wait_ge(exped, 1)
                step(dve.tensor_tensor(k.neglam[:], exps[:, 1:2], exps[:, 0:1], ALU.subtract))
                step(dve.tensor_scalar(k.neglam[:], k.neglam[:], -LAM0, None, ALU.add))

            @block.scalar
            def _(act):
                act.wait_ge(dotted, 1)
                act.activation(exps[:], dots[:], ACT.Exp).then_inc(exped, 1)


def prompt_attend(nc, d, k):
    units = []
    for t in range(PT):
        for h in range(HA):
            units += [(t, 0, X_AK + h, X_AQ + h, DC * c, T_AV + HEAD * h) for c in range(2)]
        units += [(t, 1, X_KS, X_BQ + h, 0, T_VS) for h in range(HB)]
        units += [(t, 2, X_KW, X_BQ + h, 0, T_VW) for h in range(HB)]
    pvs = []
    for u, (t, sec, _, _, p0, vcol) in enumerate(units):
        if sec == 0 and p0 == 0:
            continue
        head = (u % 16) // 2 if sec == 0 else (u % 16) % 4
        pvs.append((u, t, sec, head, vcol))
    NU, NV = len(units), len(pvs)
    NSEC = 3 * PT
    with Stage(nc, "pa") as s:
        e = s.sb("e", [P, 6, 512])
        w = s.sb("w", [P, 2, 512])
        wT = s.sb("wT", [P, 2, 4, P])
        nm = s.sb("nm", [P, NU])
        l = s.sb("l", [P, NU])
        r = s.sb("r", [P, NU])
        o = s.sb("o", [P, 2, 512])
        scores = [s.ps(f"scores{i}", [P, 512]) for i in range(3)]
        tp = [s.ps(f"tp{i}", [P, 4, P]) for i in range(2)]
        po = [s.ps(f"po{i}", [P, 4, HEAD]) for i in range(3)]
        scored = s.sem("scored")
        maxed = s.sem("maxed")
        exped = s.sem("exped")
        inverted = s.sem("inverted")
        divisors = s.sem("divisors")
        weighted = s.sem("weighted")
        scaled = s.sem("scaled")
        turned = s.sem("turned")
        copied = s.sem("copied")
        summed = s.sem("summed")
        finished = s.sem("finished")
        stored = s.sems("stored", 2)
        NA = [sum(1 for v in pvs[:i] if v[2] == 0) for i in range(NV + 1)]

        with nc.Block() as block:
            @block.sync
            def _(sp):
                for c in range(NSEC):
                    t, sec = c // 3, c % 3
                    sp.wait_ge(finished, c + 1)
                    sp.dma_start(d.o_att[P * t:P * t + P, 512 * sec:512 * sec + 512],
                                 o[:, c % 2, :]).then_inc(stored[c % 2], 16)
                for b in range(2):
                    sp.wait_ge(stored[b], 8 * NSEC)

            @block.tensor
            def _(pe):
                def score(u):
                    t, sec, kc, qc, p0, _ = units[u]
                    kn = DC if sec == 0 else P
                    n = P * (t + 1)
                    if u >= 3:
                        pe.wait_ge(exped, u - 2)
                    pe.matmul(scores[u % 3][:, 0:n], k.attT[p0:p0 + kn, qc, P * t:P * t + P],
                              k.attT[p0:p0 + kn, kc, 0:n], start=True, stop=False)
                    pe.matmul(scores[u % 3][:, n - P:n], k.ident[:], k.causal[:], start=False,
                              stop=True).then_inc(scored, 1)

                def turn(i):
                    u, t, sec, h, _ = pvs[i]
                    if sec == 0:
                        pe.wait_ge(weighted, NA[i] + 1)
                        src = w[:, NA[i] % 2, :]
                    else:
                        pe.wait_ge(exped, u + 1)
                        src = e[:, u % 6, :]
                    if i >= 2:
                        pe.wait_ge(copied, i - 1)
                    for b in range(t + 1):
                        last = pe.transpose(tp[i % 2][:, b, :], src[:, P * b:P * b + P], k.ident[:])
                    last.then_inc(turned, 1)

                def attend(i):
                    u, t, sec, h, vcol = pvs[i]
                    c = 3 * t + sec
                    if h == 0 and c >= 3:
                        pe.wait_ge(finished, c - 2)
                    pe.wait_ge(copied, i + 1)
                    for b in range(t + 1):
                        last = pe.matmul(po[c % 3][:, h, :], wT[:, i % 2, b, :],
                                         k.rows_p[:, b, vcol:vcol + HEAD], start=(b == 0), stop=(b == t))
                    last.then_inc(summed, 1)

                done = 0
                for i in range(NV + 2):
                    if i < NV:
                        while done <= min(pvs[i][0] + 1, NU - 1):
                            score(done)
                            done += 1
                    if 1 <= i <= NV:
                        turn(i - 1)
                    if i >= 2:
                        attend(i - 2)

            @block.scalar
            def _(act):
                for u in range(NU):
                    t = units[u][0]
                    n = P * (t + 1)
                    act.wait_ge(maxed, u + 1)
                    if u >= 6:
                        act.wait_ge(turned, sum(1 for v in pvs if v[0] <= u - 6))
                        act.wait_ge(weighted, sum(1 for v in pvs if v[2] == 0 and v[0] <= u - 5))
                    act.activation(e[:, u % 6, 0:n], scores[u % 3][:, 0:n], ACT.Exp, bias=nm[:, u:u + 1],
                                   accum_out=l[:, u:u + 1]).then_inc(exped, 1)

            @block.vector
            def _(dve):
                def row_max(u):
                    n = P * (units[u][0] + 1)
                    dve.wait_ge(scored, u + 1)
                    dve.tensor_reduce(nm[:, u:u + 1], scores[u % 3][:, 0:n], AX_X, ALU.max,
                                      negate=True).then_inc(maxed, 1)

                def weigh(i):
                    u, t, _, _, _ = pvs[i]
                    n = P * (t + 1)
                    a = NA[i]
                    dve.wait_ge(exped, u + 1)
                    dve.reciprocal(r[:, u - 1:u + 1], l[:, u - 1:u + 1]).then_inc(inverted, 1)
                    dve.wait_ge(inverted, 2 * a + 1)
                    if i >= 2 and a >= 2:
                        j = next(x for x in range(NV) if NA[x] == a - 2 and pvs[x][2] == 0)
                        dve.wait_ge(turned, j + 1)
                    dve.tensor_scalar(w[:, a % 2, 0:n], e[:, (u - 1) % 6, 0:n], r[:, u - 1:u], None,
                                      ALU.mult).then_inc(scaled, 1)
                    dve.tensor_scalar(r[:, u:u + 1], r[:, u:u + 1], k.neglam[:, 0:1], None,
                                      ALU.mult).then_inc(inverted, 1)
                    dve.wait_ge(scaled, a + 1)
                    dve.wait_ge(inverted, 2 * a + 2)
                    dve.scalar_tensor_tensor(w[:, a % 2, 0:n], e[:, u % 6, 0:n], r[:, u:u + 1],
                                             w[:, a % 2, 0:n], ALU.mult, ALU.add).then_inc(weighted, 1)

                def copy(i):
                    t = pvs[i][1]
                    dve.wait_ge(turned, i + 1)
                    if i >= 2:
                        dve.wait_ge(summed, i - 1)
                    dve.tensor_copy(wT[:, i % 2, 0:t + 1, :], tp[i % 2][:, 0:t + 1, :]).then_inc(copied, 1)

                def finish(i):
                    u, t, sec, h, _ = pvs[i]
                    c = 3 * t + sec
                    dve.wait_ge(summed, i + 1)
                    if c >= 2:
                        dve.wait_ge(stored[c % 2], 16 * (c // 2))
                    out = o[:, c % 2, :].rearrange("p (h w) -> p h w", h=4)
                    if sec == 0:
                        dve.tensor_copy(out, po[c % 3][:]).then_inc(finished, 1)
                        return
                    dve.wait_ge(exped, u + 1)
                    dve.reciprocal(r[:, u - 3:u + 1], l[:, u - 3:u + 1]).then_inc(divisors, 1)
                    dve.wait_ge(divisors, 2 * t + sec)
                    dve.tensor_tensor(out, po[c % 3][:], r[:, u - 3:u + 1].unsqueeze(2).broadcast_to(
                        [P, 4, HEAD]), ALU.mult).then_inc(finished, 1)

                done = 0
                for i in range(NV + 3):
                    if i < NV:
                        while done <= min(pvs[i][0] + 1, NU - 1):
                            row_max(done)
                            done += 1
                        if pvs[i][2] == 0:
                            weigh(i)
                    if 1 <= i <= NV:
                        copy(i - 1)
                    if i >= 3 and pvs[i - 3][3] == 3:
                        finish(i - 3)


def compress(nc, d, k):
    with Stage(nc, "cm") as s:
        kc = s.sb("kc", [NBLK, DB + 1, HEAD])
        vc = s.sb("vc", [NBLK, DB + 1, HEAD])
        sq = s.sb("sq", [NBLK, DB + 1, HEAD])
        ss = s.sb("ss", [NBLK, 3, DB + 1])
        g = s.sb("g", [NBLK, HEAD])
        kcT = s.sb("kcT", [P, DB + 1, NBLK])
        qpad = s.sb("qpad", [P, DB * 144])
        same = s.sb("same", [P, P])
        shift = s.sb("shift", [P, 176])
        mul = s.sb("mul", [P, PT, 8])
        bias = s.sb("bias", [P, PT, 8])
        st = s.sb("st", [P, 8, 16])
        pc = s.sb("pc", [P, PT * HB, 8])
        pcT = s.sb("pcT", [8, PT, HB, P])
        pd = s.sb("pd", [P, NBLK])
        imp = s.sb("imp", [P, 3, NBLK])
        top = s.sb("top", [P, 2, 8])
        pdT = s.sb("pdT", [NBLK, HB, 288])
        o = s.sb("o", [P, 2, 512])
        acc = s.ps("acc", [NBLK, 2 * HEAD])
        tp = [s.ps(f"tp{i}", [P, 512]) for i in range(2)]
        sc = s.ps("sc", [P, 512])
        sd = s.ps("sd", [P, 512])
        po = [s.ps(f"po{i}", [P, HB, HEAD]) for i in range(2)]

        pooled = s.sem("pooled")
        drained = s.sem("drained")
        g_loaded = s.sem("g_loaded")
        zeroed = s.sem("zeroed")
        masks_ready = s.sem("masks_ready")
        dve_step = s.sem("dve_step")
        summed = s.sem("summed")
        rooted = s.sem("rooted")
        normed = s.sem("normed")
        turned = s.sem("turned")
        copied = s.sem("copied")
        qpad_ready = s.sem("qpad_ready")
        p_scored, p_centred, p_exped, p_ready = (s.sem(n) for n in ("p_scored", "p_centred", "p_exped", "p_ready"))
        p_turned, p_copied, p_summed, p_out = (s.sem(n) for n in ("p_turned", "p_copied", "p_summed", "p_out"))
        p_stored = s.sems("p_stored", 2)
        d_scored, d_maxed, d_exped, d_ready = (s.sem(n) for n in ("d_scored", "d_maxed", "d_exped", "d_ready"))
        imp_ready, d_turned, d_copied, d_summed, d_out = (
            s.sem(n) for n in ("imp_ready", "d_turned", "d_copied", "d_summed", "d_out"))
        d_stored = s.sem("d_stored")
        chosen, moved, bias_out = (s.sem(n) for n in ("chosen", "moved", "bias_out"))

        with nc.Block() as block:
            @block.sync
            def _(sp):
                sp.wait_ge(d_out, 1)
                sp.dma_start(d.o_att[SEQ:ROWS, 1536:2048], o[0:NS, 0, :]).then_inc(d_stored, 16)
                for t in range(PT):
                    sp.wait_ge(p_out, t + 1)
                    sp.dma_start(d.o_att[P * t:P * t + P, 1536:2048], o[:, t % 2, :]).then_inc(p_stored[t % 2], 16)
                for i in range(2):
                    sp.wait_ge(p_stored[i], 16 * PT // 2)
                sp.wait_ge(d_stored, 16)

            @block.gpsimd
            def _(pool):
                pool.dma_start(g[:], d.b_qk_g[1, :].partition_broadcast(NBLK)).then_inc(g_loaded, 16)
                pool.memset(qpad[:], 0.0).then_inc(zeroed, 1)
                pool.memset(pdT[:], 0.0).then_inc(zeroed, 1)
                pool.memset(same[:], 0.0).then_inc(zeroed, 1)
                pool.memset(shift[:], 0.0).then_inc(zeroed, 1)
                pool.memset(mul[:], 1.0).then_inc(zeroed, 1)
                pool.wait_ge(zeroed, 5)
                pool.affine_select(out=shift[:], in_=shift[:], compare_op=ALU.not_equal, fill=1.0,
                                   base=32, pattern=[[-1, 176]], channel_multiplier=1).then_inc(masks_ready, 1)
                pool.affine_select(out=mul[:], in_=mul[:], compare_op=ALU.is_ge, fill=0.0, base=-CMP,
                                   pattern=[[P, PT], [-CMP, 8]], channel_multiplier=1).then_inc(masks_ready, 1)
                n = 2
                for h in range(1 - HB, HB):
                    pool.affine_select(out=same[:], in_=same[:], compare_op=ALU.not_equal, fill=1.0,
                                       base=DT * h, pattern=[[-1, P]], channel_multiplier=1).then_inc(masks_ready, 1)
                    n += 1
                    pool.wait_ge(masks_ready, n)
                v = same[:].rearrange("p (b r) -> p b r", b=DB)
                pool.affine_select(out=v, in_=v, compare_op=ALU.is_ge, fill=0.0, base=0,
                                   pattern=[[-16, DB], [0, 16]], channel_multiplier=1).then_inc(masks_ready, 1)
                pool.wait_ge(masks_ready, n + 1)
                pool.affine_select(out=v, in_=v, compare_op=ALU.is_ge, fill=0.0, base=15,
                                   pattern=[[16, DB], [0, 16]], channel_multiplier=-1).then_inc(masks_ready, 1)

            @block.tensor
            def _(pe):
                for p in range(PT):
                    last = pe.matmul(acc[:], k.z[:, 30 - 2 * p:94 - 2 * p], k.rows_p[:, p, T_KC:T_KC + 2 * HEAD],
                                     start=(p == 0), stop=(p == PT - 1))
                last.then_inc(pooled, 1)
                pe.wait_ge(normed, 1)
                for b in range(DB + 1):
                    i = b // 8
                    last = pe.transpose(tp[i][:, NBLK * (b % 8):NBLK * (b % 8) + NBLK], kc[:, b, :],
                                        k.ident[0:NBLK, 0:NBLK])
                last.then_inc(turned, 1)
                pe.wait_ge(copied, 1)
                for t in range(PT):
                    for h in range(HB):
                        c = 8 * (HB * t + h)
                        last = pe.matmul(sc[:, c:c + 8], k.attT[:, X_BQ + h, P * t:P * t + P],
                                         kcT[:, DB, 0:8], start=True, stop=True)
                last.then_inc(p_scored, 1)
                pe.wait_ge(qpad_ready, 1)
                for b in range(DB):
                    last = pe.matmul(sd[:, 0:NBLK], qpad[:, P * b:P * b + P], kcT[:, b, :],
                                     start=(b == 0), stop=(b == DB - 1))
                last.then_inc(d_scored, 1)
                pe.wait_ge(masks_ready, 11)
                pe.wait_ge(d_ready, 1)
                pe.matmul(sd[:, 128:128 + NBLK], same[:], pd[:], start=True, stop=True).then_inc(imp_ready, 1)
                pe.transpose(tp[0][0:NBLK, 0:P], pd[:], k.ident[:]).then_inc(d_turned, 1)
                pe.wait_ge(d_copied, 1)
                for h in range(HB):
                    for b in range(DB):
                        last = pe.matmul(po[0][0:NS, h, :], pdT[:, h, NS * b:NS * b + NS], vc[:, b, :],
                                         start=(b == 0), stop=(b == DB - 1))
                last.then_inc(d_summed, 1)
                pe.wait_ge(chosen, 1)
                for b in range(DB):
                    last = pe.matmul(tp[1][0:NBLK, NBLK * b:NBLK * b + NBLK], shift[:, 16 * b:16 * b + 64],
                                     imp[:, 2, :], start=True, stop=True)
                last.then_inc(moved, 1)
                pe.wait_ge(p_ready, 1)
                for t in range(PT):
                    if t == 0:
                        pe.wait_ge(d_copied, 1)
                    else:
                        pe.wait_ge(p_copied, t)
                    for h in range(HB):
                        last = pe.transpose(tp[0][0:8, P * h:P * h + P], pc[:, HB * t + h, :], k.ident[:])
                    last.then_inc(p_turned, 1)
                    pe.wait_ge(p_copied, t + 1)
                    pe.wait_ge(p_out, t) if t >= 1 else pe.wait_ge(d_out, 1)
                    for h in range(HB):
                        last = pe.matmul(po[t % 2][:, h, :], pcT[:, t, h, :], vc[0:8, DB, :], start=True, stop=True)
                    last.then_inc(p_summed, 1)

            @block.scalar
            def _(act):
                for h in range(2):
                    for a, v in ((0, kc), (1, vc)):
                        act.activation(v[32 * h:32 * h + 32, 0:DB, :], k.pkv[:, h:2 * DB:2, HEAD * a:HEAD * a + HEAD],
                                       ACT.Copy).then_inc(drained, 1)
                act.wait_ge(pooled, 1)
                act.activation(kc[0:32, DB, :], acc[0:32, 0:HEAD], ACT.Copy).then_inc(drained, 1)
                act.activation(vc[0:32, DB, :], acc[32:64, HEAD:2 * HEAD], ACT.Copy).then_inc(drained, 1)
                act.wait_ge(summed, 1)
                act.activation(ss[:, 1, :], ss[:, 0, :], ACT.Sqrt, bias=k.eps[0:NBLK, :],
                               scale=1.0 / HEAD).then_inc(rooted, 1)
                act.wait_ge(p_centred, 1)
                act.activation(pc[:], pc[:], ACT.Exp).then_inc(p_exped, 1)
                act.wait_ge(d_maxed, 1)
                act.activation(pd[:], sd[:, 0:NBLK], ACT.Exp, bias=st[:, 4, 0:1],
                               accum_out=st[:, 5, 0:1]).then_inc(d_exped, 1)

            @block.vector
            def _(dve):
                step = Chain(dve, dve_step)
                step(dve.memset(kc[32:64, DB, :], 0.0))
                step(dve.memset(k.selb[0:32, :, :], 0.0))
                step(dve.memset(k.selb[32:64, :, :], NEG))
                dve.wait_ge(zeroed, 5)
                dve.tensor_copy(qpad[:].rearrange("p (b x) -> p b x", x=144)[:, :, 0:16].rearrange(
                    "p b (h t) -> p b h t", h=HB),
                    k.attT[:, X_BQ:X_BQ + HB, SEQ:ROWS].rearrange("p h (b t) -> p b h t", b=DB)).then_inc(qpad_ready, 1)
                dve.wait_ge(masks_ready, 2)
                step(dve.tensor_scalar(bias[:], mul[:], -1.0, -NEG, ALU.add, ALU.mult))
                dve.wait_ge(g_loaded, 16)
                dve.wait_ge(drained, 6)
                step(dve.tensor_tensor(sq[:], kc[:], kc[:], ALU.mult))
                dve.tensor_reduce(ss[:, 0, :], sq[:], AX_X, ALU.add).then_inc(summed, 1)
                dve.wait_ge(rooted, 1)
                step(dve.reciprocal(ss[:, 2, :], ss[:, 1, :]))
                step(dve.tensor_tensor(kc[:], kc[:], ss[:, 2, :].unsqueeze(2).broadcast_to(
                    [NBLK, DB + 1, HEAD]), ALU.mult))
                dve.tensor_tensor(kc[:], kc[:], g[:].unsqueeze(1).broadcast_to([NBLK, DB + 1, HEAD]),
                                  ALU.mult).then_inc(normed, 1)
                dve.wait_ge(turned, 1)
                step(dve.tensor_copy(kcT[:, 0:8, :], tp[0][:].rearrange("p (b n) -> p b n", b=8)))
                dve.tensor_copy(kcT[:, 8, :], tp[1][:, 0:NBLK]).then_inc(copied, 1)
                dve.wait_ge(p_scored, 1)
                step(dve.tensor_tensor(pc[:].rearrange("p (t h) n -> p t h n", t=PT),
                                       sc[:, 0:128].rearrange("p (t h n) -> p t h n", t=PT, h=HB),
                                       bias[:].unsqueeze(2).broadcast_to([P, PT, HB, 8]), ALU.add))
                step(dve.tensor_reduce(st[:, 0, :], pc[:], AX_X, ALU.max))
                dve.tensor_tensor(pc[:], pc[:], st[:, 0, :].unsqueeze(2).broadcast_to([P, 16, 8]),
                                  ALU.subtract).then_inc(p_centred, 1)
                dve.wait_ge(d_scored, 1)
                dve.tensor_reduce(st[:, 4, 0:1], sd[:, 0:NBLK], AX_X, ALU.max, negate=True).then_inc(d_maxed, 1)
                dve.wait_ge(p_exped, 1)
                step(dve.tensor_tensor(pc[:].rearrange("p (t h) n -> p t h n", t=PT),
                                       pc[:].rearrange("p (t h) n -> p t h n", t=PT),
                                       mul[:].unsqueeze(2).broadcast_to([P, PT, HB, 8]), ALU.mult))
                step(dve.tensor_reduce(st[:, 1, :], pc[:], AX_X, ALU.add))
                step(dve.tensor_scalar(st[:, 2, :], st[:, 1, :], 1e-30, None, ALU.max))
                step(dve.reciprocal(st[:, 3, :], st[:, 2, :]))
                dve.tensor_tensor(pc[:], pc[:], st[:, 3, :].unsqueeze(2).broadcast_to([P, 16, 8]),
                                  ALU.mult).then_inc(p_ready, 1)
                dve.wait_ge(d_exped, 1)
                step(dve.reciprocal(st[:, 6, 0:1], st[:, 5, 0:1]))
                dve.tensor_scalar(pd[:], pd[:], st[:, 6, 0:1], None, ALU.mult).then_inc(d_ready, 1)
                dve.wait_ge(imp_ready, 1)
                dve.wait_ge(d_turned, 1)
                step(dve.tensor_copy(imp[:, 0, :], sd[:, 128:128 + NBLK]))
                dve.tensor_copy(pdT[:, :, :].rearrange("p h (b x) -> p h b x", x=36)[:, :, :, 0:DT],
                                tp[0][0:NBLK, 0:P].rearrange("p (b h t) -> p h b t", b=DB, h=HB)).then_inc(d_copied, 1)
                step(dve.max(top[:, 0, :], imp[:, 0, :]))
                step(dve.match_replace(imp[:, 1, :], top[:, 0, :], imp[:, 0, :], -1.0))
                step(dve.max(top[:, 1, :], imp[:, 1, :]))
                step(dve.match_replace(imp[:, 0, :], top[:, 1, :], imp[:, 1, :], -1.0))
                dve.tensor_scalar(imp[:, 2, :], imp[:, 0, :], 0.0, NEG, ALU.is_ge, ALU.mult).then_inc(chosen, 1)
                dve.wait_ge(d_summed, 1)
                dve.tensor_copy(o[0:NS, 0, :].rearrange("p (h w) -> p h w", h=HB), po[0][0:NS, :, :]).then_inc(d_out, 1)
                dve.wait_ge(moved, 1)
                dve.tensor_copy(k.selb[32:48, :, :], tp[1][32:48, 0:512].rearrange("p (b n) -> p b n", b=DB)) \
                    .then_inc(bias_out, 1)
                dve.wait_ge(bias_out, 1)
                for t in range(PT):
                    dve.wait_ge(p_turned, t + 1)
                    dve.tensor_copy(pcT[:, t, :, :], tp[0][0:8, :].rearrange("p (h r) -> p h r", h=HB)).then_inc(p_copied, 1)
                    dve.wait_ge(p_summed, t + 1)
                    if t == 0:
                        dve.wait_ge(d_stored, 16)
                    elif t >= 2:
                        dve.wait_ge(p_stored[t % 2], 16)
                    dve.tensor_copy(o[:, t % 2, :].rearrange("p (h w) -> p h w", h=HB), po[t % 2][:]).then_inc(p_out, 1)


def decode_attend(nc, d, k):
    NG = PAGES // 4
    WING, NEWG, G = NG, NG + 1, NG + 2
    R = 64
    HEADS = HA + 2
    batches = [(g, j) for g in range(NG) for j in range(HA + 1)] + [(WING, HA + 1)]
    NT = len(batches)
    uses = [len(range(r, NT, 3)) for r in range(3)]
    first_row = [8 * h for h in range(HA)] + [32 + 4 * h for h in range(HB)] + [48 + 4 * h for h in range(HB)]
    with Stage(nc, "da") as s:
        table = s.sb("table", [1, DB * PAGES], I32)
        pa = s.sb("pa", [P, 4, 4, 1024])
        pb = s.sb("pb", [P, 4, 4, 256])
        pw = s.sb("pw", [P, 4, 256])
        khi = s.sb("khi", [P, 3, 512], F32R)
        klo = s.sb("klo", [P, 3, 512], F32R)
        q = s.sb("q", [P, HEADS * R])
        qs = s.sb("qs", [P, HEADS, 2 * R], F32R)
        low = s.sb("low", [R, 2, 512])
        sb_ = s.sb("scores", [R, 2, 512])
        e = s.sb("e", [R, 2, 512])
        pT = s.sb("pT", [P, 2, 4, HEADS * R])
        winb = s.sb("winb", [R, 512])
        newb = s.sb("newb", [R, DB, NS])
        nm = s.sb("nm", [R, G])
        l = s.sb("l", [R, G])
        wt = s.sb("wt", [R, 4, G])
        st = s.sb("st", [R, 8])
        ob = s.sb("ob", [R, G, HEAD])
        oall = s.sb("oall", [R, DB, HEAD])
        coef = s.sb("coef", [R, 2])
        hot = s.sb("hot", [8, 2, R])
        late = s.sb("late", [8, DB * NS + 8])
        sel = s.sb("sel", [R, 12, 60])
        o = pT[0:NS, :, :, :].rearrange("p a c n -> p (a c n)")[:, 0:1536].rearrange("p (a n) -> p a n", a=3)
        tp = [s.ps(f"tp{i}", [P, 4, P]) for i in range(3)]
        ps = [s.ps(f"ps{i}", [2 * R, 512]) for i in range(2)]
        pt = s.ps("pt", [P, 4, R])
        po = [s.ps(f"po{i}", [R, HEAD]) for i in range(2)]

        table_loaded = s.sem("table_loaded")
        loaded = s.sems("loaded", 4)
        win_loaded = s.sem("win_loaded")
        win_used = s.sem("win_used")
        zeroed = s.sem("zeroed")
        made = s.sem("made")
        spread = s.sem("spread")
        dve_step = s.sem("dve_step")
        consts_ready = s.sem("consts_ready")
        q_placed = s.sem("q_placed")
        q_high = s.sem("q_high")
        q_ready = s.sem("q_ready")
        low_out = s.sem("low_out")
        turned = s.sem("turned")
        split = s.sem("split")
        copied = s.sems("copied", 3)
        multiplied = s.sem("multiplied")
        scored = s.sem("scored")
        joined = s.sem("joined")
        added = s.sem("added")
        maxed = s.sem("maxed")
        exped = s.sem("exped")
        turning = s.sem("turning")
        p_turned = s.sem("p_turned")
        p_copied = s.sem("p_copied")
        summed = s.sem("summed")
        o_copied = s.sem("o_copied")
        minned = s.sem("minned")
        weighed = s.sem("weighed")
        combined = s.sem("combined")
        gathered = s.sem("gathered")
        out_ready = s.sem("out_ready")
        stored = s.sem("stored")

        with nc.Block() as block:
            @block.sync
            def _(sp):
                sp.dma_start(table[:], d.page_table.rearrange("(a b) n -> a (b n)", a=1)).then_inc(table_loaded, 16)
                sp.sem_inc(win_used, 1)
                sp.wait_ge(table_loaded, 16)
                with sp.Fori(0, DB) as b:
                    for g in range(NG):
                        sp.wait_ge(summed, b * G + g + (3 if g >= 4 else 1))
                        for i in range(4):
                            page = sp.value_load(table[0:1, bass.ds(b * PAGES + 4 * g + i, 1)],
                                                 min_val=0, max_val=d.cache_b.shape[0] - 1)
                            sp.dma_start(pa[:, g % 4, i, :], d.cache_a[bass.ds(page, 1), :, :]
                                         .rearrange("a p n -> p (a n)")).then_inc(loaded[g % 4], 16)
                            sp.dma_start(pb[:, g % 4, i, :], d.cache_b[bass.ds(page, 1), :, 256:512]
                                         .rearrange("a p n -> p (a n)")).then_inc(loaded[g % 4], 16)
                        if g == 4:
                            sp.wait_ge(win_used, b + 1)
                            sp.dma_start(pw[:], d.b_win[bass.ds(b, 1), :, :].rearrange(
                                "a (i p) n -> p (a i) n", p=P)).then_inc(win_loaded, 16)
                sp.wait_ge(out_ready, 1)
                sp.dma_start(d.o_att[SEQ:ROWS, 0:1536], o.rearrange("p a n -> p (a n)")).then_inc(stored, 16)
                sp.wait_ge(stored, 16)

            @block.gpsimd
            def _(pool):
                for v in (q, pT, winb, hot, late, sel):
                    pool.memset(v[:], 0.0).then_inc(zeroed, 1)
                pool.wait_ge(zeroed, 6)
                pool.affine_select(out=winb[:], in_=winb[:], compare_op=ALU.is_ge, fill=NEG, base=-48,
                                   pattern=[[0, 512]], channel_multiplier=1).then_inc(made, 1)
                pool.affine_select(out=hot[0:4, 0, :].rearrange("p (a t) -> p a t", t=4),
                                   in_=hot[0:4, 0, :].rearrange("p (a t) -> p a t", t=4),
                                   compare_op=ALU.not_equal, fill=1.0, base=0, pattern=[[0, 16], [-1, 4]],
                                   channel_multiplier=1).then_inc(made, 1)
                pool.affine_select(out=hot[:, 1, 0:32].rearrange("p (a t) -> p a t", t=8),
                                   in_=hot[:, 1, 0:32].rearrange("p (a t) -> p a t", t=8),
                                   compare_op=ALU.not_equal, fill=1.0, base=0, pattern=[[0, 4], [-1, 8]],
                                   channel_multiplier=1).then_inc(made, 1)
                v = late[0:4, 0:DB * NS].rearrange("p (b n) -> p b n", b=DB)
                pool.affine_select(out=v, in_=v, compare_op=ALU.is_ge, fill=NEG, base=0,
                                   pattern=[[4, DB], [-1, NS]], channel_multiplier=1).then_inc(made, 1)
                pool.wait_ge(made, 4)
                pool.affine_select(out=v, in_=v, compare_op=ALU.is_ge, fill=NEG, base=0,
                                   pattern=[[-4, DB], [1, NS]], channel_multiplier=0).then_inc(made, 1)
                v = late[0:4, DB * NS:DB * NS + 4]
                pool.affine_select(out=v, in_=v, compare_op=ALU.is_gt, fill=NEG, base=0,
                                   pattern=[[1, 4]], channel_multiplier=-1).then_inc(made, 1)
                v = late[:, DB * NS + 4:DB * NS + 5]
                pool.affine_select(out=v, in_=v, compare_op=ALU.is_gt, fill=1.0, base=4,
                                   pattern=[[0, 1]], channel_multiplier=-1).then_inc(made, 1)
                n = 7
                for j, r0 in enumerate(first_row):
                    for c in range(2 if j < HA else 1):
                        v = sel[:, j, 28:32]
                        pool.affine_select(out=v, in_=v, compare_op=ALU.not_equal, fill=1.0, base=-r0 - 4 * c,
                                           pattern=[[-1, 4]], channel_multiplier=1).then_inc(made, 1)
                        n += 1
                        pool.wait_ge(made, n)

            @block.tensor
            def _(pe):
                def turn(b, i):
                    g, j = batches[i]
                    if j == 0:
                        pe.wait_ge(loaded[g % 4], b * 256 + 128 * (g // 4) + 128)
                    if g == WING:
                        pe.wait_ge(win_loaded, b * 16 + 16)
                    if i < 3:
                        for r in range(3):
                            pe.wait_ge(copied[r], b * uses[r] + 1)
                    else:
                        pe.wait_ge(copied[i % 3], b * uses[i % 3] + i // 3 + 1)
                    for c in range(4):
                        src = (pa[:, g % 4, c, HEAD * j:HEAD * j + HEAD] if j < HA else
                               pb[:, g % 4, c, 0:HEAD] if g < NG else pw[:, c, 0:HEAD])
                        last = pe.transpose(tp[i % 3][:, c, :], src, k.ident[:])
                    last.then_inc(turned, 1)

                def multiply(b, i):
                    g, j = batches[i]
                    first = j == 0 or g == WING
                    if first:
                        pe.wait_ge(added, b * G + g + 1)
                    pe.wait_ge(copied[i % 3], b * uses[i % 3] + i // 3 + 2)
                    pe.matmul(ps[g % 2][:], qs[:, j, :], khi[:, i % 3, :], start=first, stop=False)
                    last = pe.matmul(ps[g % 2][:], qs[:, j, :], klo[:, i % 3, :], start=False,
                                     stop=j == HA or g == WING)
                    last.then_inc(multiplied, 1)
                    if j == HA or g == WING:
                        pe.wait_ge(multiplied, b * NT + i + 4)
                        pe.sem_inc(scored, 1)

                def attend(b, g):
                    n = NS if g == NEWG else P
                    pe.wait_ge(exped, b * G + g + 3)
                    pe.wait_ge(p_copied, b * G + g + 1)
                    pe.sem_inc(turning, 1)
                    for c in range(1 if g == NEWG else 4):
                        last = pe.transpose(pt[0:n, c, :], e[:, g % 2, P * c:P * c + n], k.ident[0:R, 0:R])
                    last.then_inc(p_turned, 1)

                def values(b, g):
                    n = NS if g == NEWG else P
                    pe.wait_ge(p_copied, b * G + g + 2)
                    pe.wait_ge(o_copied, b * G + g + 1)
                    new = [k.rows_s[:, T_AV + HEAD * j:T_AV + HEAD * j + HEAD] for j in range(HA)] \
                        + [k.rows_s[:, T_VS:T_VS + HEAD], k.rows_s[:, T_VW:T_VW + HEAD]]
                    todo = []
                    if g < NG:
                        for c in range(4):
                            todo += [(c, j, pa[:, g % 4, c, 512 + HEAD * j:512 + HEAD * j + HEAD]) for j in range(HA)]
                            todo.append((c, HA, pb[:, g % 4, c, HEAD:2 * HEAD]))
                    elif g == WING:
                        todo = [(c, HA + 1, pw[:, c, HEAD:2 * HEAD]) for c in range(4)]
                    else:
                        todo = [(0, j, new[j]) for j in range(HEADS)]
                    for x, (c, j, v) in enumerate(todo):
                        last = pe.matmul(po[g % 2][:], pT[0:n, g % 2, c, R * j:R * j + R], v, start=(x == 0),
                                         stop=(x == len(todo) - 1))
                    last.then_inc(summed, 1)
                    if g == WING:
                        pe.wait_ge(summed, b * G + g + 7)
                        pe.sem_inc(win_used, 1)

                pe.wait_ge(made, 23)
                pe.matmul(ps[0][0:R, 0:DB * NS + 4], hot[0:4, 0, :], late[0:4, 0:DB * NS + 4], start=True, stop=True)
                pe.matmul(ps[1][0:R, 0:1], hot[:, 1, :], late[:, DB * NS + 4:DB * NS + 5], start=True,
                          stop=True).then_inc(spread, 1)
                pe.wait_ge(consts_ready, 1)
                pe.sem_inc(multiplied, 3)
                pe.sem_inc(scored, 1)
                pe.sem_inc(p_turned, 2)
                pe.sem_inc(summed, 6)
                new_keys = [X_AK + j for j in range(HA)] + [X_KS, X_KW]
                with pe.Fori(0, DB) as b:
                    pe.wait_ge(q_ready, b + 1)
                    for i in range(NT + 2):
                        if i < NT:
                            turn(b, i)
                        if i >= 2:
                            multiply(b, i - 2)
                            g, j = batches[i - 2]
                            if g >= 1 and j == 3:
                                attend(b, g - 1)
                            if g >= 2 and j == 0 or g == WING:
                                values(b, g - 2)
                    pe.wait_ge(added, b * G + NEWG + 1)
                    for j in range(HEADS):
                        last = pe.matmul(ps[NEWG % 2][0:R, 0:NS], q[:, R * j:R * j + R],
                                         k.attT[:, new_keys[j], SEQ:ROWS], start=(j == 0), stop=(j == HEADS - 1))
                    last.then_inc(scored, 1)
                    for g in (NG - 1, WING, NEWG):
                        attend(b, g)
                        values(b, g)
                pe.wait_ge(combined, DB + 1)
                for j in range(12):
                    for b in range(DB):
                        last = pe.matmul(tp[j // 4][0:NS, j % 4, :], sel[:, j, 28 - 4 * b:60 - 4 * b], oall[:, b, :],
                                         start=(b == 0), stop=(b == DB - 1))
                    if j % 4 == 3:
                        last.then_inc(gathered, 1)

            @block.scalar
            def _(act):
                act.wait_ge(consts_ready, 1)
                act.sem_inc(exped, 2)
                act.sem_inc(o_copied, 2)

                def high(b, i):
                    act.wait_ge(turned, b * NT + i + 1)
                    act.wait_ge(multiplied, b * NT + max(i, 2) + 1)
                    act.activation(khi[:, i % 3, :].rearrange("p (c n) -> p c n", c=4), tp[i % 3][:],
                                   ACT.Copy).then_inc(split, 1)

                def low_scores(b, g):
                    act.wait_ge(scored, b * G + g + 2)
                    act.wait_ge(added, b * G + g + 1)
                    act.activation(low[:, g % 2, :], ps[g % 2][R:2 * R, :], ACT.Copy).then_inc(low_out, 1)

                def softmax(b, g):
                    n = NS if g == NEWG else 512
                    act.wait_ge(maxed, b * G + g + 1)
                    act.wait_ge(p_turned, b * G + g + 1)
                    if g == 0:
                        act.wait_ge(combined, b + 1)
                    act.activation(e[:, g % 2, 0:n], sb_[:, g % 2, 0:n], ACT.Exp, bias=nm[:, g:g + 1],
                                   accum_out=l[:, g:g + 1]).then_inc(exped, 1)

                def out(b, g):
                    act.wait_ge(summed, b * G + g + 7)
                    act.activation(ob[:, g, :], po[g % 2][:], ACT.Copy).then_inc(o_copied, 1)

                with act.Fori(0, DB) as b:
                    for i, (g, j) in enumerate(batches):
                        high(b, i)
                        if g >= 1 and j == 1:
                            low_scores(b, g - 1)
                        if g >= 2 and j == 2:
                            out(b, g - 2)
                        if g >= 1 and j == 3:
                            softmax(b, g - 1)
                    low_scores(b, NG - 1)
                    out(b, NG - 2)
                    softmax(b, NG - 1)
                    low_scores(b, WING)
                    softmax(b, WING)
                    out(b, NG - 1)
                    softmax(b, NEWG)
                    out(b, WING)
                    out(b, NEWG)
                    act.wait_ge(minned, b + 1)
                    act.activation(wt[:, 0, :], nm[:], ACT.Exp, bias=st[:, 0:1], scale=-1.0).then_inc(weighed, 1)

            @block.vector
            def _(dve):
                step = Chain(dve, dve_step)
                dve.wait_ge(spread, 1)
                dve.wait_ge(made, 23)
                step(dve.tensor_copy(newb[:].rearrange("p b n -> p (b n)"), ps[0][0:R, 0:DB * NS]))
                step(dve.tensor_tensor(winb[:, 0:4], winb[:, 0:4], ps[0][0:R, DB * NS:DB * NS + 4], ALU.add))
                step(dve.tensor_copy(coef[:, 1:2], ps[1][0:R, 0:1]))
                step(dve.tensor_scalar(coef[:, 0:1], k.neglam[0:R, :], -1.0, None, ALU.add))
                step(dve.tensor_tensor(coef[:, 0:1], coef[:, 0:1], coef[:, 1:2], ALU.mult))
                step(dve.tensor_scalar(coef[:, 0:1], coef[:, 0:1], 1.0, None, ALU.add))
                for r in range(3):
                    dve.sem_inc(copied[r], 1)
                dve.sem_inc(added, 2)
                dve.sem_inc(p_copied, 1)
                dve.sem_inc(combined, 1)
                dve.sem_inc(consts_ready, 1)
                own = step.n

                def queries(b):
                    dve.wait_ge(scored, b * G + 1)
                    A = q[:, 0:288].rearrange("p (h x) -> p h x", x=72)
                    for c in range(2):
                        dve.tensor_copy(A[DC * c:DC * c + DC, :, 4 * c:4 * c + 4],
                                        k.attT[DC * c:DC * c + DC, X_AQ:X_AQ + HA, bass.ds(b * DT + SEQ, DT)])
                    for x in (288, 368):
                        last = dve.tensor_copy(q[:, x:x + 16].rearrange("p (h t) -> p h t", h=HB),
                                               k.attT[:, X_BQ:X_BQ + HB, bass.ds(b * DT + SEQ, DT)])
                    last.then_inc(q_placed, 1)
                    dve.wait_ge(q_placed, b + 1)
                    v = q[:].rearrange("p (j r) -> p j r", j=HEADS)
                    dve.tensor_copy(qs[:, :, 0:R], v).then_inc(q_high, 1)
                    dve.wait_ge(q_high, b + 1)
                    dve.tensor_tensor(qs[:, :, R:2 * R], v, qs[:, :, 0:R], ALU.subtract).then_inc(q_ready, 1)

                def low_part(b, i):
                    dve.wait_ge(split, b * NT + i + 1)
                    dve.tensor_tensor(klo[:, i % 3, :].rearrange("p (c n) -> p c n", c=4), tp[i % 3][:],
                                      khi[:, i % 3, :].rearrange("p (c n) -> p c n", c=4),
                                      ALU.subtract).then_inc(copied[i % 3], 1)

                def row_max(b, g):
                    dve.wait_ge(scored, b * G + g + 2)
                    dve.wait_ge(exped, b * G + g + 1)
                    if g < NEWG:
                        dve.wait_ge(low_out, b * (G - 1) + g + 1)
                        dve.tensor_tensor(sb_[:, g % 2, :], ps[g % 2][0:R, :], low[:, g % 2, :],
                                          ALU.add).then_inc(joined, 1)
                        dve.wait_ge(joined, b * (G - 1) + g + 1)
                    if g < NG:
                        v = sb_[:, g % 2, :].rearrange("p (n r) -> p n r", n=8)
                        dve.tensor_tensor(v, v, k.selb[:, bass.ds(b, 1), 8 * g:8 * g + 8].rearrange(
                            "p a n -> p (a n)").unsqueeze(2).broadcast_to([R, 8, CMP]), ALU.add).then_inc(added, 1)
                    elif g == WING:
                        dve.tensor_tensor(sb_[:, g % 2, :], sb_[:, g % 2, :], winb[:], ALU.add).then_inc(added, 1)
                    else:
                        dve.tensor_tensor(sb_[:, g % 2, 0:NS], ps[g % 2][0:R, 0:NS],
                                          newb[:, bass.ds(b, 1), :].rearrange("p a n -> p (a n)"),
                                          ALU.add).then_inc(added, 1)
                    n = NS if g == NEWG else 512
                    dve.wait_ge(added, b * G + g + 3)
                    dve.tensor_reduce(nm[:, g:g + 1], sb_[:, g % 2, 0:n], AX_X, ALU.max,
                                      negate=True).then_inc(maxed, 1)

                def weights(b, g):
                    dve.wait_ge(p_turned, b * G + g + 3)
                    dve.wait_ge(summed, b * G + g + 5)
                    n, c = (NS, 1) if g == NEWG else (P, 4)
                    if g != WING:
                        dve.tensor_copy(pT[0:n, g % 2, 0:c, 0:288].rearrange("p c (h x) -> p c h x", x=72)[:, :, :, 0:8],
                                        pt[0:n, 0:c, 0:32].rearrange("p c (h x) -> p c h x", h=HA))
                        last = dve.tensor_copy(pT[0:n, g % 2, 0:c, 288:304], pt[0:n, 0:c, 32:48])
                    if g >= NG:
                        last = dve.tensor_copy(pT[0:n, g % 2, 0:c, 368:384], pt[0:n, 0:c, 48:64])
                    last.then_inc(p_copied, 1)

                with dve.Fori(0, DB) as b:
                    queries(b)
                    for i, (g, j) in enumerate(batches):
                        low_part(b, i)
                        if g >= 2 and j == 0 or g == WING:
                            weights(b, g - 2)
                        if g >= 1 and j == 1:
                            row_max(b, g - 1)
                    row_max(b, NG - 1)
                    row_max(b, WING)
                    weights(b, NG - 1)
                    row_max(b, NEWG)
                    weights(b, WING)
                    weights(b, NEWG)
                    dve.wait_ge(maxed, b * G + G)
                    dve.tensor_reduce(st[:, 0:1], nm[:], AX_X, ALU.min).then_inc(minned, 1)
                    dve.wait_ge(weighed, b + 1)
                    dve.wait_ge(exped, b * G + G + 2)
                    dve.wait_ge(o_copied, b * G + G + 2)

                    n = [0]

                    def then(ins):
                        n[0] += 1
                        ins.then_inc(dve_step, 1)
                        dve.wait_ge(dve_step, b * 6 + own + n[0])

                    then(dve.tensor_tensor(wt[:, 1, :], wt[:, 0, :], l[:], ALU.mult))
                    then(dve.tensor_reduce(st[:, 1:2], wt[:, 1, :], AX_X, ALU.add))
                    then(dve.reciprocal(st[:, 2:3], st[:, 1:2]))
                    then(dve.tensor_scalar(wt[:, 2, :], wt[:, 0, :], st[:, 2:3], coef[:, 0:1], ALU.mult, ALU.mult))
                    then(dve.tensor_tensor(ob[:], ob[:], wt[:, 2, :].unsqueeze(2).broadcast_to([R, G, HEAD]), ALU.mult))
                    then(dve.tensor_reduce(oall[:, bass.ds(b, 1), :].rearrange("p a n -> p (a n)"),
                                           ob[:].rearrange("p g n -> p n g"), AX_X, ALU.add))
                    dve.sem_inc(combined, 1)
                dve.wait_ge(gathered, 3)
                for a in range(3):
                    last = dve.tensor_copy(o[:, a, :].rearrange("p (h n) -> p h n", h=4), tp[a][0:NS, :, :])
                last.then_inc(out_ready, 1)


def convolve(nc, d, k):
    with Stage(nc, "cv") as s:
        x = s.sb("x", [P, 5, QKC])
        w = s.sb("w", [5, QKC])
        old = s.sb("old", [3 * DB, QKC])
        wT = s.sb("wT", [P, 8, 5])
        xp = s.sb("xp", [P, 8, SEQ + 3])
        xs = s.sb("xs", [P, 8, DB, DT + 3])
        sig = s.sb("sig", [P, 8, ROWS])
        gin = s.sb("gin", [P, 5, 2 * HC])
        gbias = s.sb("gbias", [HC, 2])
        t0 = s.sb("t0", [HC, ROWS])
        t1 = s.sb("t1", [HC, ROWS])
        tp = [s.ps(f"tp{i}", [P, 4, P]) for i in range(4)]
        gi = [s.ps(f"gi{i}", [HC, 512]) for i in range(4)]
        x_loaded = s.sems("x_loaded", 5)
        w_loaded = s.sem("w_loaded")
        g_loaded = s.sem("g_loaded")
        zeroed = s.sem("zeroed")
        turned = s.sem("turned")
        copied = s.sem("copied")
        g_turned = s.sem("g_turned")
        conv_done = s.sem("conv_done")
        sig_done = s.sem("sig_done")
        silu_done = s.sem("silu_done")
        f_ready = s.sem("f_ready")
        f_exped = s.sem("f_exped")
        f_logged = s.sem("f_logged")
        k_turned = s.sem("k_turned")
        k_copied = s.sem("k_copied")
        dve_step = s.sem("dve_step")
        stored = s.sem("stored")
        CQ = C_CQK
        jobs = [("w", 0, h) for h in range(2)] + [("old", 0, h) for h in range(2)] \
            + [("x", t, h) for t in range(5) for h in range(2)]

        with nc.Block() as block:
            @block.sync
            def _(sp):
                sp.dma_start(w[0:4, :], d.c_conv_w).then_inc(w_loaded, 16)
                sp.dma_start(w[4:5, :], d.c_conv_b.unsqueeze(0)).then_inc(w_loaded, 16)
                sp.dma_start(old[:], d.c_conv.rearrange("b t n -> (b t) n")).then_inc(w_loaded, 16)
                for t, (r0, rows) in enumerate(TILES):
                    sp.dma_start(x[0:rows, t, :], d.proj[r0:r0 + rows, CQ:CQ + QKC]).then_inc(x_loaded[t], 16)
                for t, (r0, rows) in enumerate(TILES):
                    sp.dma_start(gin[0:rows, t, :], d.proj[r0:r0 + rows, C_CIF:C_CIF + 2 * HC]).then_inc(g_loaded, 16)
                sp.dma_start(gbias[:], d.c_gate_b.rearrange("a h -> h a"), allow_slow_non_contiguous=True).then_inc(g_loaded, 16)
                sp.dma_start(d.conv_p, d.proj[SEQ - 3:SEQ, CQ:CQ + QKC]).then_inc(stored, 16)
                for b in range(DB):
                    r = SEQ + DT * b
                    sp.dma_start(d.conv_s[b], d.proj[r + 1:r + DT, CQ:CQ + QKC]).then_inc(stored, 16)
                sp.wait_ge(stored, 16 * (DB + 1))

            @block.tensor
            def _(pe):
                for n, (what, t, h) in enumerate(jobs):
                    if what == "w":
                        pe.wait_ge(w_loaded, 48)
                        src, rows = w, 5
                    elif what == "old":
                        src, rows = old, 3 * DB
                    else:
                        pe.wait_ge(x_loaded[t], 16)
                        src, rows = x[:, t, :], TILES[t][1]
                    if n >= 2:
                        pe.wait_ge(copied, n - 1)
                    for c in range(4):
                        col = P * (4 * h + c)
                        last = pe.transpose(tp[n % 2][:, c, 0:rows], src[0:rows, col:col + P], k.ident[0:rows, 0:rows])
                    last.then_inc(turned, 1)
                pe.wait_ge(g_loaded, 96)
                for t, (r0, rows) in enumerate(TILES):
                    for a in range(2):
                        out = gi[a][:, r0:r0 + rows] if t < PT else gi[2 + a][:, 0:rows]
                        last = pe.transpose(out, gin[0:rows, t, HC * a:HC * a + HC], k.ident[0:rows, 0:rows])
                last.then_inc(g_turned, 1)
                pe.wait_ge(silu_done, 1)
                for t, (r0, rows) in enumerate(TILES):
                    if t >= 2:
                        pe.wait_ge(k_copied, t - 1)
                    for c in range(4):
                        last = pe.transpose(tp[2 + t % 2][0:rows, c, :], k.qkT[:, 4 + c, r0:r0 + rows], k.ident[:])
                    last.then_inc(k_turned, 1)

            @block.scalar
            def _(act):
                act.wait_ge(f_ready, 1)
                act.activation(t1[:], t0[:], ACT.Exp).then_inc(f_exped, 1)
                act.wait_ge(f_exped, 1)
                act.activation(t1[:], t1[:], ACT.Ln, bias=1.0).then_inc(f_logged, 1)
                act.wait_ge(conv_done, 1)
                act.activation(sig[:], k.qkT[:], ACT.Sigmoid).then_inc(sig_done, 1)

            @block.vector
            def _(dve):
                step = Chain(dve, dve_step)
                step(dve.memset(xp[:, :, 0:3], 0.0))
                for n, (what, t, h) in enumerate(jobs):
                    dve.wait_ge(turned, n + 1)
                    c = slice(4 * h, 4 * h + 4)
                    if what == "w":
                        last = dve.tensor_copy(wT[:, c, :], tp[n % 2][:, :, 0:5])
                    elif what == "old":
                        last = dve.tensor_copy(xs[:, c, :, 0:3], tp[n % 2][:, :, 0:3 * DB].rearrange(
                            "p c (b t) -> p c b t", b=DB))
                    elif t < PT:
                        last = dve.tensor_copy(xp[:, c, 3 + P * t:3 + P * t + P], tp[n % 2][:])
                    else:
                        last = dve.tensor_copy(xs[:, c, :, 3:3 + DT], tp[n % 2][:, :, 0:NS].rearrange(
                            "p c (b t) -> p c b t", b=DB))
                    last.then_inc(copied, 1)
                dve.wait_ge(g_turned, 1)
                for a, dst in ((0, k.gate_i), (1, k.gate_f)):
                    for src, r0, n in ((gi[a], 0, SEQ), (gi[2 + a], SEQ, NS)):
                        step(dve.tensor_scalar(dst[:, r0:r0 + n], src[:, 0:n], gbias[:, a:a + 1], None, ALU.add))
                dve.scalar_tensor_tensor(t0[:], k.gate_f[:], -1.0, k.gate_f[:], ALU.mult, ALU.min).then_inc(f_ready, 1)
                dve.wait_ge(f_logged, 1)
                step(dve.tensor_scalar(k.gate_f[:], k.gate_f[:], 0.0, None, ALU.min))
                step(dve.tensor_tensor(k.gate_f[:], k.gate_f[:], t1[:], ALU.subtract))
                dve.wait_ge(copied, len(jobs))
                for j in range(4):
                    for c in range(8):
                        outs = ((k.qkT[:, c, 0:SEQ], xp[:, c, j:j + SEQ]),
                                (k.qkT[:, c, SEQ:ROWS].rearrange("p (b t) -> p b t", b=DB), xs[:, c, :, j:j + DT]))
                        for out, src in outs:
                            if j == 0:
                                last = dve.tensor_scalar(out, src, wT[:, c, 0:1], wT[:, c, 4:5], ALU.mult, ALU.add)
                            else:
                                last = dve.scalar_tensor_tensor(out, src, wT[:, c, j:j + 1], out, ALU.mult, ALU.add)
                    if j < 3:
                        step(last)
                last.then_inc(conv_done, 1)
                dve.wait_ge(sig_done, 1)
                step(dve.tensor_tensor(k.qkT[:], k.qkT[:], sig[:], ALU.mult))
                dve.tensor_scalar(k.qkT[:, 0:4, :], k.qkT[:, 0:4, :], DC ** -0.5, None, ALU.mult).then_inc(silu_done, 1)
                for t, (r0, rows) in enumerate(TILES):
                    dve.wait_ge(k_turned, t + 1)
                    dve.tensor_copy(k.k_rows[0:rows, t, :].rearrange("p (c n) -> p c n", c=4),
                                    tp[2 + t % 2][0:rows, :, :]).then_inc(k_copied, 1)
                dve.wait_ge(k_copied, 5)


def mlstm(nc, d, k, decode):
    NC, n, tile0 = (1, NS, PT) if decode else (PT, P, 0)
    NB, L = (DB, DT) if decode else (1, P)
    V = HEAD + 1
    with Stage(nc, "md" if decode else "mp") as s:
        v = s.sb("v", [P, NC, HC, V])
        ones = s.sb("ones8", [HC, P])
        m = s.sb("m", [HC, NB])
        b = s.sb("b", [HC, NC, n])
        row = s.sb("row", [HC, NC, 4, n])
        nca = s.sb("nca", [HC, NC, n])
        mt = s.sb("mt", [HC, NC, n])
        cs = s.sb("cs", [HC, NC, NB])
        diag = s.sb("diag", [HC, NC, HC, NB])
        pick = s.sb("pick", [HC, HC, P])
        mask = s.sb("mask", [n, n])
        col = s.sb("col", [P, NC, 4, HC])
        w = s.sb("w", [P, 4, n])
        qk = s.sb("qk", [P, 4, n])
        kw = s.sb("kw", [P, NC, HC, DC])
        inter = s.sb("inter", [P, 4, V])
        num = s.sb("num", [P, 4, V])
        den = s.sb("den", [P, 4, 4])
        h_out = s.sb("h_out", [P, 2, HC, HEAD])
        S = s.sb("S", [P, DB if decode else 1, 4, V])
        csb = s.sb("csb", [P, NC, HC, NB])
        sc = [s.ps(f"sc{i}", [P, 2, P]) for i in range(2)]
        small = sc[1][:, 0, 0:4 * HC].rearrange("p (x h) -> p x h", x=4)
        dd = s.ps("dd", [P, 4, n])
        pn = [s.ps(f"pn{i}", [P, 2, V]) for i in range(2)]
        pi = [s.ps(f"pi{i}", [P, 2, V]) for i in range(2)]
        pu = s.ps("pu", [P, 512])

        loaded = s.sem("loaded")
        st_loaded = s.sem("st_loaded")
        zeroed = s.sem("zeroed")
        made = s.sem("made")
        dve_step = s.sem("dve_step")
        rows_ready = s.sem("rows_ready")
        cs_exped = s.sem("cs_exped")
        diag_ready = s.sem("diag_ready")
        r_turned = s.sem("r_turned")
        r_copied = s.sem("r_copied")
        col_exped = s.sem("col_exped")
        cs_spread = s.sem("cs_spread")
        csb_ready = s.sem("csb_ready")
        kw_ready = s.sem("kw_ready")
        scored = s.sem("scored")
        exped = s.sem("exped")
        weighed = s.sem("weighed")
        summed = s.sem("summed")
        in_copied = s.sem("in_copied")
        state_ready = s.sem("state_ready")
        taken = s.sem("taken")
        h_ready = s.sem("h_ready")
        h_stored = s.sems("h_stored", 2)
        turned = s.sem("turned")
        copied = s.sem("copied")
        fin = s.sem("fin")
        out_stored = s.sem("out_stored")
        extra = [s.sem(f"extra{i}") for i in range(6)]
        if decode:
            c0 = s.sb("c0", [P, DB, HC, DC])
            c1 = s.sb("c1", [P, DB, HC, DC])
            n0 = s.sb("n0", [NS, P])
            n0b = s.sb("n0b", [DB, HC, DC])
            qpad = s.sb("qpad", [P, 4, 288])
            blk = s.sb("blk", [NS, DB])
            kwb = s.sb("kwb", [NS, 2, DB, DC])
            bh = s.sb("bh", [DB, 2, HC])
        else:
            cT = s.sb("cT", [P, 4, P])

        units = [(c, hf) for c in range(NC) for hf in range(2)]

        def q_of(h, c):
            r0 = TILES[tile0 + c][0]
            return k.qkT[DC * (h % 2):DC * (h % 2) + DC, h // 2, r0:r0 + n]

        def k_of(h, c):
            r0 = TILES[tile0 + c][0]
            return k.qkT[DC * (h % 2):DC * (h % 2) + DC, 4 + h // 2, r0:r0 + n]

        with nc.Block() as block:
            @block.sync
            def _(sp):
                for c in range(NC):
                    r0, rows = TILES[tile0 + c]
                    sp.dma_start(v[0:rows, c, :, 0:HEAD], d.proj[r0:r0 + rows, C_CV:C_CV + HC * HEAD].rearrange(
                        "r (h n) -> r h n", h=HC)).then_inc(loaded, 16)
                if decode:
                    sp.dma_start(m[:], d.c_m.rearrange("b h -> h b"), allow_slow_non_contiguous=True).then_inc(st_loaded, 16)
                    sp.dma_start(n0[:], d.c_n.rearrange("b (x y) n -> (b x) (y n)", y=2)).then_inc(st_loaded, 16)
                    sp.dma_start(n0b[:], d.c_n).then_inc(st_loaded, 16)
                    for i in range(DB):
                        sp.dma_start(c0[:, i, :, :], d.c_C[i].rearrange("h v n -> v h n")).then_inc(st_loaded, 16)
                for c in range(NC):
                    r0, rows = TILES[tile0 + c]
                    sp.wait_ge(h_ready, 2 * c + 2)
                    sp.dma_start(d.h_c[r0:r0 + rows, :], h_out[0:rows, c % 2, :, :].rearrange(
                        "p h n -> p (h n)")).then_inc(h_stored[c % 2], 16)
                sp.wait_ge(fin, 1)
                n_out = 0
                if decode:
                    for i in range(DB):
                        sp.dma_start(d.C_s[i].rearrange("h v n -> v h n"), c1[:, i, :, :]).then_inc(out_stored, 16)
                    sp.dma_start(d.n_s, n0b[:]).then_inc(out_stored, 16)
                    sp.dma_start(d.m_s, bh[:, 1, :]).then_inc(out_stored, 16)
                    n_out = DB + 2
                else:
                    for x in range(4):
                        sp.dma_start(d.C_p[2 * x:2 * x + 2].rearrange("y v n -> v y n"),
                                     cT[:, x, :].rearrange("p (y n) -> p y n", y=2)).then_inc(out_stored, 16)
                    for y in range(2):
                        sp.dma_start(d.n_p[y:HC:2, :].rearrange("x n -> n x").unsqueeze(2),
                                     S[DC * y:DC * y + DC, 0, :, HEAD:V],
                                     allow_slow_non_contiguous=True).then_inc(out_stored, 16)
                    sp.dma_start(d.m_p.unsqueeze(1), m[:]).then_inc(out_stored, 16)
                    n_out = 7
                sp.wait_ge(out_stored, 16 * n_out)
                for i in range(min(2, NC)):
                    sp.wait_ge(h_stored[i], 16 * max(1, NC // 2))

            @block.gpsimd
            def _(pool):
                pool.memset(ones[:], 1.0).then_inc(made, 1)
                pool.memset(v[:, :, :, HEAD:V], 1.0).then_inc(made, 1)
                z = [mask, pick, S] + ([qpad] if decode else [m])
                for x in z:
                    pool.memset(x[:], 0.0).then_inc(zeroed, 1)
                pool.wait_ge(zeroed, 4)
                pool.affine_select(out=mask[:], in_=mask[:], compare_op=ALU.is_ge, fill=NEG, base=0,
                                   pattern=[[1, n]], channel_multiplier=-1).then_inc(made, 1)
                pool.affine_select(out=pick[:], in_=pick[:], compare_op=ALU.not_equal, fill=1.0, base=0,
                                   pattern=[[-1, HC], [0, P]], channel_multiplier=1).then_inc(made, 1)
                if decode:
                    pool.wait_ge(made, 4)
                    mv = mask[:].rearrange("p (b t) -> p b t", b=DB)
                    pool.affine_select(out=mv, in_=mv, compare_op=ALU.is_ge, fill=NEG, base=0,
                                       pattern=[[-DT, DB], [0, DT]], channel_multiplier=1).then_inc(made, 1)
                    pool.memset(blk[:], 1.0).then_inc(made, 1)
                    pool.wait_ge(made, 6)
                    pool.affine_select(out=blk[:], in_=blk[:], compare_op=ALU.is_ge, fill=0.0, base=0,
                                       pattern=[[-DT, DB]], channel_multiplier=1).then_inc(made, 1)
                    pool.wait_ge(made, 7)
                    pool.affine_select(out=blk[:], in_=blk[:], compare_op=ALU.is_ge, fill=0.0, base=DT - 1,
                                       pattern=[[DT, DB]], channel_multiplier=-1).then_inc(made, 1)

            @block.tensor
            def _(pe):
                pe.wait_ge(made, 8 if decode else 4)
                if decode:
                    pe.wait_ge(st_loaded, 16 * (DB + 3))
                    for i in range(DB):
                        if i >= 2:
                            pe.wait_ge(copied, i - 1)
                        bank = (pn[0], pn[1])[i % 2]
                        for x in range(2):
                            last = pe.transpose(bank[:, x, 0:P], c0[:, i, 2 * x:2 * x + 2, :].rearrange("p y n -> p (y n)"), k.ident[:])
                        bank = (pi[0], pi[1])[i % 2]
                        for x in range(2, 4):
                            last = pe.transpose(bank[:, x - 2, 0:P], c0[:, i, 2 * x:2 * x + 2, :].rearrange("p y n -> p (y n)"), k.ident[:])
                        last.then_inc(turned, 1)
                    pe.transpose(pu[:, 0:NS], n0[:], k.ident[0:NS, 0:NS]).then_inc(extra[0], 1)
                for c in range(NC):
                    pe.wait_ge(rows_ready, c + 1)
                    if c:
                        pe.wait_ge(r_copied, c)
                    for x in range(4):
                        last = pe.transpose(small[0:n, x, :], row[:, c, x, :], k.ident[0:HC, 0:HC])
                    last.then_inc(r_turned, 1)
                pe.wait_ge(r_copied, NC)
                pe.wait_ge(diag_ready, 1)
                if decode:
                    pe.wait_ge(copied, DB + 1)
                pe.matmul(pu[:, 64:64 + NC * HC * NB], ones[:], diag[:].rearrange("p c h b -> p (c h b)"),
                          start=True, stop=True).then_inc(cs_spread, 1)
                pe.wait_ge(csb_ready, 1)
                pe.wait_ge(loaded, 16 * NC)
                pe.wait_ge(kw_ready, 1)
                if decode:
                    pe.wait_ge(copied, DB + 2)
                for u, (c, hf) in enumerate(units):
                    if u:
                        pe.wait_ge(weighed, u)
                        pe.wait_ge(exped, u)
                    for x in range(4):
                        h = 4 * hf + x
                        pe.matmul(dd[0:n, x, :], pick[:, h, 0:n], nca[:, c, :], start=True, stop=False)
                        pe.matmul(dd[0:n, x, :], k.ident[0:n, 0:n], mask[:], start=False, stop=True)
                        last = pe.matmul(sc[x % 2][0:n, x // 2, 0:n], k_of(h, c), q_of(h, c), start=True, stop=True)
                    last.then_inc(scored, 1)
                    if u:
                        pe.wait_ge(taken, u)
                    if not decode and c:
                        pe.wait_ge(state_ready, u - 1)
                    for x in range(4):
                        h = 4 * hf + x
                        rows = slice(DC * (h % 2), DC * (h % 2) + DC)
                        if decode:
                            for i in range(DB):
                                pe.matmul(pi[x % 2][0:n, x // 2, :], qpad[rows, h // 2, NS * i:NS * i + NS],
                                          S[rows, i, h // 2, :], start=(i == 0), stop=(i == DB - 1))
                        else:
                            pe.matmul(pi[x % 2][:, x // 2, :], q_of(h, c), S[rows, 0, h // 2, :], start=True, stop=True)
                    if not decode:
                        for x in range(4):
                            h = 4 * hf + x
                            rows = slice(DC * (h % 2), DC * (h % 2) + DC)
                            pe.matmul(pu[rows, V * (x // 2):V * (x // 2) + V], kw[:, c, h, :], v[:, c, h, :],
                                      start=True, stop=True)
                    pe.wait_ge(weighed, u + 1)
                    for x in range(4):
                        h = 4 * hf + x
                        last = pe.matmul(pn[x // 2][0:n, x % 2, :], qk[0:n, x, :], v[0:n, c, h, :], start=True, stop=True)
                    last.then_inc(summed, 1)
                if decode:
                    for h in range(HC):
                        pe.wait_ge(extra[1], h + 1)
                        if h:
                            pe.wait_ge(extra[3], h)
                        pe.matmul(pu[:], v[0:NS, 0, h, 0:HEAD], kwb[:, h % 2, :, :].rearrange("p b n -> p (b n)"),
                                  start=True, stop=True).then_inc(extra[2], 1)
                    pe.wait_ge(extra[3], HC)
                    pe.matmul(pu[0:DB, :], blk[:], kw[0:NS, 0, :, :].rearrange("p h n -> p (h n)"), start=True, stop=True)
                    pe.transpose(small[0:DB, 0, :], cs[:, 0, :], k.ident[0:HC, 0:HC])
                    pe.transpose(small[0:DB, 1, :], mt[:, 0, :].rearrange("p (b t) -> p b t", b=DB)[:, :, DT - 1],
                                 k.ident[0:HC, 0:HC]).then_inc(extra[4], 1)
                else:
                    pe.wait_ge(state_ready, 2 * NC)
                    for x in range(4):
                        last = pe.transpose(dd[:, x, :], S[:, 0, x, 0:HEAD], k.ident[:])
                    last.then_inc(turned, 1)

            @block.scalar
            def _(act):
                act.wait_ge(extra[5], 1)
                act.activation(cs[:], cs[:], ACT.Exp).then_inc(cs_exped, 1)
                for c in range(NC):
                    act.wait_ge(r_turned, c + 1)
                    act.activation(col[0:n, c, 0, :], small[0:n, 0, :], ACT.Copy)
                    act.activation(col[0:n, c, 1:4, :], small[0:n, 1:4, :], ACT.Exp).then_inc(r_copied, 1)
                act.wait_ge(r_copied, NC)
                for u, (c, hf) in enumerate(units):
                    act.wait_ge(scored, u + 1)
                    if u:
                        act.wait_ge(weighed, u)
                    for x in range(4):
                        h = 4 * hf + x
                        last = act.activation(w[0:n, x, :], dd[0:n, x, :], ACT.Exp, bias=col[0:n, c, 0, h:h + 1])
                    last.then_inc(exped, 1)
                    act.wait_ge(summed, u + 1)
                    if u:
                        act.wait_ge(taken, u)
                    for x in range(4):
                        h = 4 * hf + x
                        last = act.activation(inter[0:n, x, :], pi[x % 2][0:n, x // 2, :], ACT.Copy,
                                              scale=col[0:n, c, 1, h:h + 1])
                    last.then_inc(in_copied, 1)

            @block.vector
            def _(dve):
                step = Chain(dve, dve_step)
                if decode:
                    dve.wait_ge(st_loaded, 16 * (DB + 3))
                dve.wait_ge(zeroed, 4)
                dve.wait_ge(made, 4)
                for c in range(NC):
                    g0 = TILES[tile0 + c][0]
                    for i in range(NB):
                        r = slice(L * i, L * i + L)
                        gr = slice(g0 + L * i, g0 + L * i + L)
                        init = m[:, i:i + 1]
                        step(dve.tensor_tensor_scan(b[:, c, r], ones[:, 0:L], k.gate_f[:, gr], 0.0, ALU.mult, ALU.add))
                        step(dve.tensor_tensor(row[:, c, 0, r], k.gate_i[:, gr], b[:, c, r], ALU.subtract))
                        step(dve.tensor_tensor_scan(nca[:, c, r], row[:, c, 0, r], row[:, c, 0, r], init, ALU.max, ALU.max))
                    ca = nca[:, c, :].rearrange("p (b t) -> p b t", b=NB)
                    last_ca = ca[:, :, L - 1:L]
                    step(dve.tensor_tensor(row[:, c, 1, :].rearrange("p (b t) -> p b t", b=NB),
                                           m[:].unsqueeze(2).broadcast_to([HC, NB, L]), ca, ALU.subtract))
                    step(dve.tensor_tensor(mt[:, c, :], b[:, c, :], nca[:, c, :], ALU.add))
                    step(dve.tensor_scalar(row[:, c, 2, :], mt[:, c, :], -1.0, None, ALU.mult))
                    step(dve.tensor_tensor(row[:, c, 3, :].rearrange("p (b t) -> p b t", b=NB),
                                           row[:, c, 0, :].rearrange("p (b t) -> p b t", b=NB),
                                           last_ca.broadcast_to([HC, NB, L]), ALU.subtract))
                    step(dve.tensor_tensor(cs[:, c, :].unsqueeze(2), m[:].unsqueeze(2), last_ca, ALU.subtract))
                    if not decode:
                        step(dve.tensor_copy(m[:], mt[:, c, L - 1:L]))
                    dve.tensor_scalar(nca[:, c, :], nca[:, c, :], -1.0, None, ALU.mult).then_inc(rows_ready, 1)
                dve.sem_inc(extra[5], 1)
                dve.wait_ge(cs_exped, 1)
                for c in range(NC):
                    last = dve.tensor_tensor(diag[:, c, :, :], k.ident[0:HC, 0:HC].unsqueeze(2).broadcast_to([HC, HC, NB]),
                                             cs[:, c, :].unsqueeze(1).broadcast_to([HC, HC, NB]), ALU.mult)
                last.then_inc(diag_ready, 1)
                if decode:
                    for i in range(DB):
                        dve.wait_ge(turned, i + 1)
                        dve.tensor_copy(S[:, i, 0:2, 0:HEAD], pn[i % 2][:, :, 0:HEAD])
                        dve.tensor_copy(S[:, i, 2:4, 0:HEAD], pi[i % 2][:, :, 0:HEAD]).then_inc(copied, 1)
                    dve.wait_ge(extra[0], 1)
                    dve.tensor_copy(S[:, :, :, HEAD:V], pu[:, 0:NS].rearrange("p (b x) -> p b x", b=DB).unsqueeze(3)) \
                        .then_inc(copied, 1)
                    dve.tensor_copy(qpad[:].rearrange("p x (b y) -> p x b y", y=36)[:, :, :, 0:DT],
                                    k.qkT[:, 0:4, SEQ:ROWS].rearrange("p x (b t) -> p x b t", b=DB)).then_inc(copied, 1)
                dve.wait_ge(cs_spread, 1)
                dve.tensor_copy(csb[:].rearrange("p c h b -> p (c h b)"), pu[:, 64:64 + NC * HC * NB]).then_inc(csb_ready, 1)
                dve.wait_ge(csb_ready, 1)
                dve.wait_ge(r_copied, NC)
                for c in range(NC):
                    last = dve.tensor_tensor(kw[0:n, c, :, :], k.k_rows[0:n, tile0 + c, :].rearrange(
                        "p (h n) -> p h n", h=HC), col[0:n, c, 3, :].unsqueeze(2).broadcast_to([n, HC, DC]), ALU.mult)
                last.then_inc(kw_ready, 1)
                for u, (c, hf) in enumerate(units):
                    dve.wait_ge(exped, u + 1)
                    if u:
                        dve.wait_ge(summed, u)
                    for y in range(2):
                        last = dve.tensor_tensor(qk[0:n, y:4:2, :], sc[y][0:n, :, 0:n], w[0:n, y:4:2, :], ALU.mult)
                    last.then_inc(weighed, 1)
                    dve.wait_ge(summed, u + 1)
                    dve.wait_ge(in_copied, u + 1)
                    for x in range(2):
                        last = dve.tensor_tensor(num[0:n, 2 * x:2 * x + 2, :], inter[0:n, 2 * x:2 * x + 2, :],
                                                 pn[x][0:n, :, :], ALU.add)
                    step(last)
                    if not decode:
                        st = S[:, 0, 2 * hf:2 * hf + 2, :]
                        for y in range(2):
                            rows = slice(DC * y, DC * y + DC)
                            sy = S[rows, 0, 2 * hf:2 * hf + 2, :]
                            step(dve.tensor_tensor(sy, sy, csb[rows, c, 4 * hf + y:4 * hf + 4:2, :].broadcast_to(
                                [DC, 2, V]), ALU.mult))
                        dve.tensor_tensor(st, st, pu[:, 0:2 * V].rearrange("p (x n) -> p x n", x=2),
                                          ALU.add).then_inc(state_ready, 1)
                        dve.wait_ge(state_ready, u + 1)
                    dve.sem_inc(taken, 1)
                    dn = num[0:n, :, HEAD:V].rearrange("p x a -> p (x a)")
                    step(dve.scalar_tensor_tensor(den[0:n, 0, :], dn, -1.0, dn, ALU.mult, ALU.max))
                    step(dve.tensor_tensor(den[0:n, 1, :], den[0:n, 0, :], col[0:n, c, 2, 4 * hf:4 * hf + 4], ALU.max))
                    step(dve.reciprocal(den[0:n, 2, :], den[0:n, 1, :]))
                    if c >= 2:
                        dve.wait_ge(h_stored[c % 2], 16 * (c // 2))
                    dve.tensor_tensor(h_out[0:n, c % 2, 4 * hf:4 * hf + 4, :], num[0:n, :, 0:HEAD],
                                      den[0:n, 2, :].unsqueeze(2).broadcast_to([n, 4, HEAD]), ALU.mult).then_inc(h_ready, 1)
                if decode:
                    for h in range(HC):
                        if h >= 2:
                            dve.wait_ge(extra[2], h - 1)
                        dve.tensor_tensor(kwb[:, h % 2, :, :], kw[0:NS, 0, h, :].unsqueeze(1).broadcast_to([NS, DB, DC]),
                                          blk[:].unsqueeze(2).broadcast_to([NS, DB, DC]), ALU.mult).then_inc(extra[1], 1)
                        step(dve.tensor_tensor(c1[:, :, h, :], c0[:, :, h, :], csb[:, 0, h, :].unsqueeze(2).broadcast_to(
                            [P, DB, DC]), ALU.mult))
                        dve.wait_ge(extra[2], h + 1)
                        dve.tensor_tensor(c1[:, :, h, :], c1[:, :, h, :], pu[:].rearrange("p (b n) -> p b n", b=DB),
                                          ALU.add).then_inc(extra[3], 1)
                    dve.wait_ge(extra[4], 1)
                    step(dve.tensor_copy(bh[:], small[0:DB, 0:2, :]))
                    step(dve.tensor_tensor(n0b[:], n0b[:], bh[:, 0, :].unsqueeze(2).broadcast_to([DB, HC, DC]), ALU.mult))
                    dve.tensor_tensor(n0b[:], n0b[:], pu[0:DB, :].rearrange("p (h n) -> p h n", h=HC),
                                      ALU.add).then_inc(fin, 1)
                else:
                    dve.wait_ge(turned, 1)
                    dve.tensor_copy(cT[:], dd[:]).then_inc(fin, 1)


def output(nc, d, k):
    GW = 1036
    CW = 2 * HC * HEAD
    NSL = D // SLAB
    with Stage(nc, "ou") as s:
        att = s.sb("att", [P, 2, 2048])
        hc = s.sb("hc", [P, 2, HC * HEAD])
        g = s.sb("g", [P, 2, GW + CW])
        sg = s.sb("sg", [P, GW + CW])
        sq = s.sb("sq", [P, 1536])
        st = s.sb("st", [P, 5, 3, 12])
        ga = s.sb("ga", [P, HEAD])
        gc = s.sb("gc", [P, HEAD])
        mixT = s.sb("mixT", [P, KC, ROWS])
        w = s.sb("w", [P, 2, KC, SLAB])
        out = s.sb("out", [P, 2, 5, SLAB])
        tp = [s.ps(f"tp{i}", [P, 4, P]) for i in range(3)]
        ps = [s.ps(f"ps{i}", [P, SLAB]) for i in range(5)]
        loaded = s.sems("loaded", 2)
        gains_loaded = s.sem("gains_loaded")
        w_loaded = s.sems("w_loaded", 2)
        x_loaded = s.sems("x_loaded", 2)
        gains_ready = s.sem("gains_ready")
        squashed = s.sem("squashed")
        gated = s.sem("gated")
        summed = s.sem("summed")
        rooted = s.sem("rooted")
        dve_step = s.sem("dve_step")
        pool_step = s.sem("pool_step")
        mixed = s.sem("mixed")
        turned = s.sem("turned")
        copied = s.sem("copied")
        product_ready = s.sem("product_ready")
        y_ready = s.sem("y_ready")
        w_used = s.sem("w_used")
        stored = s.sems("stored", 2)
        wv = d.w_out.rearrange("(c p) n -> p c n", p=P)

        with nc.Block() as block:
            @block.sync
            def _(sp):
                def load_tile(t):
                    r0, rows = TILES[t]
                    i = t % 2
                    if t >= 2:
                        sp.wait_ge(turned, 4 * (t - 1))
                        sp.wait_ge(gated, t - 1)
                    for dst, src in ((att[0:rows, i, :], d.o_att[r0:r0 + rows, :]),
                                     (hc[0:rows, i, :], d.h_c[r0:r0 + rows, :]),
                                     (g[0:rows, i, 0:512], d.proj[r0:r0 + rows, C_AZ:C_BQ]),
                                     (g[0:rows, i, 512:GW], d.proj[r0:r0 + rows, C_BG:C_CQK]),
                                     (g[0:rows, i, GW:GW + CW], d.proj[r0:r0 + rows, C_CO:N_IN])):
                        sp.dma_start(dst, src).then_inc(loaded[i], 16)

                def load_slab(n):
                    i = n % 2
                    sp.dma_start(w[:, i, :, :], wv[:, :, SLAB * n:SLAB * n + SLAB]).then_inc(w_loaded[i], 16)
                    for t, (r0, rows) in enumerate(TILES):
                        src = d.x_prompt[r0:r0 + rows, :] if t < PT else d.x_sample
                        sp.dma_start(out[0:rows, i, t, :], src[:, SLAB * n:SLAB * n + SLAB]).then_inc(x_loaded[i], 16)

                load_tile(0)
                load_tile(1)
                load_slab(0)
                for t in range(2, 5):
                    load_tile(t)
                load_slab(1)
                for n in range(NSL):
                    for t, (r0, rows) in enumerate(TILES):
                        dst = d.y_p[r0:r0 + rows, :] if t < PT else d.y_s
                        sp.wait_ge(y_ready, 5 * n + t + 1)
                        sp.dma_start(dst[:, SLAB * n:SLAB * n + SLAB], out[0:rows, n % 2, t, :]).then_inc(stored[n % 2], 16)
                    if n + 2 < NSL:
                        sp.wait_ge(w_used, n + 1)
                        sp.wait_ge(stored[n % 2], 80 * (n // 2 + 1))
                        load_slab(n + 2)
                for i in range(2):
                    sp.wait_ge(stored[i], 40 * NSL)

            @block.gpsimd
            def _(pool):
                pool.dma_start(ga[:], d.a_out_g.partition_broadcast(P)).then_inc(gains_loaded, 16)
                pool.dma_start(gc[:], d.c_out_g.partition_broadcast(P)).then_inc(gains_loaded, 16)
                n = 0
                for t, (r0, rows) in enumerate(TILES):
                    i = t % 2
                    pool.wait_ge(squashed, t + 1)
                    for a, b in ((0, 512), (GW - 512, GW), (GW + 1024, GW + CW)):
                        pool.tensor_tensor(g[0:rows, i, a:b], g[0:rows, i, a:b], sg[0:rows, a:b],
                                           ALU.mult).then_inc(pool_step, 1)
                    n += 3
                    pool.wait_ge(pool_step, n)
                    pool.tensor_tensor(g[0:rows, i, GW:GW + 1024], g[0:rows, i, GW + 1024:GW + CW],
                                       sg[0:rows, GW:GW + 1024], ALU.mult).then_inc(gated, 1)

            @block.scalar
            def _(act):
                def copy_out(t):
                    r0, rows = TILES[t]
                    for q in range(4):
                        act.wait_ge(turned, 4 * t + q + 1)
                        act.activation(mixT[:, 4 * q:4 * q + 4, r0:r0 + rows], tp[(4 * t + q) % 3][:, :, 0:rows],
                                       ACT.Copy).then_inc(copied, 1)

                for t, (r0, rows) in enumerate(TILES):
                    act.wait_ge(loaded[t % 2], 80 * (t // 2 + 1))
                    if t:
                        act.wait_ge(mixed, t)
                        act.wait_ge(gated, t)
                    act.activation(sg[0:rows, :], g[0:rows, t % 2, :], ACT.Sigmoid).then_inc(squashed, 1)
                    act.wait_ge(summed, t + 1)
                    act.activation(st[0:rows, t, 1, :], st[0:rows, t, 0, :], ACT.Sqrt, bias=k.eps[0:rows, :],
                                   scale=1.0 / HEAD).then_inc(rooted, 1)
                    if t:
                        copy_out(t - 1)
                copy_out(4)

            @block.vector
            def _(dve):
                step = Chain(dve, dve_step)
                dve.wait_ge(gains_loaded, 32)
                step(dve.tensor_scalar(ga[:], ga[:], 1.0 - LAM0, None, ALU.mult))
                for t, (r0, rows) in enumerate(TILES):
                    i = t % 2
                    heads = lambda v: v.rearrange("p (h n) -> p h n", n=HEAD)
                    A, C = heads(att[0:rows, i, 0:512]), heads(hc[0:rows, i, :])
                    dve.wait_ge(loaded[i], 80 * (t // 2 + 1))
                    dve.tensor_tensor(heads(sq[0:rows, 0:512]), A, A, ALU.mult)
                    step(dve.tensor_tensor(heads(sq[0:rows, 512:1536]), C, C, ALU.mult))
                    dve.wait_ge(dve_step, step.n)
                    dve.tensor_reduce(st[0:rows, t, 0, :], heads(sq[0:rows, :]), AX_X, ALU.add).then_inc(summed, 1)
                    dve.wait_ge(squashed, t + 1)
                    gates = sg[0:rows, 512:524].rearrange("p (h n) -> p h n", n=3)
                    br = [heads(att[0:rows, i, 512 * (x + 1):512 * (x + 2)]) for x in range(3)]
                    for x, gate in ((0, 1), (1, 2), (2, 0)):
                        last = dve.tensor_tensor(br[x], br[x], gates[:, :, gate:gate + 1].broadcast_to(
                            [rows, HB, HEAD]), ALU.mult)
                    step(last)
                    step(dve.tensor_tensor(br[0], br[0], br[1], ALU.add))
                    step(dve.tensor_tensor(br[0], br[0], br[2], ALU.add))
                    dve.wait_ge(rooted, t + 1)
                    step(dve.reciprocal(st[0:rows, t, 2, :], st[0:rows, t, 1, :]))
                    dve.tensor_tensor(A, A, st[0:rows, t, 2, 0:HA].unsqueeze(2).broadcast_to([rows, HA, HEAD]), ALU.mult)
                    step(dve.tensor_tensor(C, C, st[0:rows, t, 2, HA:12].unsqueeze(2).broadcast_to([rows, HC, HEAD]),
                                           ALU.mult))
                    dve.tensor_tensor(A, A, ga[0:rows, :].unsqueeze(1).broadcast_to([rows, HA, HEAD]), ALU.mult)
                    step(dve.tensor_tensor(C, C, gc[0:rows, :].unsqueeze(1).broadcast_to([rows, HC, HEAD]), ALU.mult))
                    dve.wait_ge(gated, t + 1)
                    dve.tensor_tensor(A, A, heads(g[0:rows, i, 0:512]), ALU.mult)
                    dve.tensor_tensor(br[0], br[0], heads(g[0:rows, i, GW - 512:GW]), ALU.mult)
                    dve.tensor_tensor(C, C, heads(g[0:rows, i, GW:GW + 1024]), ALU.mult).then_inc(mixed, 1)
                for n in range(NSL):
                    dve.wait_ge(x_loaded[n % 2], 80 * (n // 2 + 1))
                    for t, (r0, rows) in enumerate(TILES):
                        dve.wait_ge(product_ready, 5 * n + t + 1)
                        dve.tensor_tensor(out[0:rows, n % 2, t, :], out[0:rows, n % 2, t, :], ps[t][0:rows, :],
                                          ALU.add).then_inc(y_ready, 1)

            @block.tensor
            def _(pe):
                def turn(t):
                    rows = TILES[t][1]
                    pe.wait_ge(mixed, t + 1)
                    for q in range(4):
                        m = 4 * t + q
                        if m >= 3:
                            pe.wait_ge(copied, m - 2)
                        src = (att, hc)[q // 2][:, t % 2, 512 * (q % 2):512 * (q % 2) + 512]
                        for c in range(4):
                            last = pe.transpose(tp[m % 3][:, c, 0:rows], src[0:rows, P * c:P * c + P],
                                                k.ident[0:rows, 0:rows])
                        last.then_inc(turned, 1)

                def multiply(n, t):
                    r0, rows = TILES[t]
                    if n == 0:
                        pe.wait_ge(copied, 4 * t + 4)
                    else:
                        pe.wait_ge(y_ready, 5 * n + t - 4)
                    for c in range(KC):
                        last = pe.matmul(ps[t][0:rows, :], mixT[:, c, r0:r0 + rows], w[:, n % 2, c, :],
                                         start=(c == 0), stop=(c == KC - 1))
                    last.then_inc(product_ready, 1)

                turn(0)
                for n in range(NSL):
                    pe.wait_ge(w_loaded[n % 2], 16 * (n // 2 + 1))
                    for t in range(5):
                        if n == 0 and t + 1 < 5:
                            turn(t + 1)
                        multiply(n, t)
                    pe.wait_ge(product_ready, 5 * n + 5)
                    pe.sem_inc(w_used, 1)


def stages(nc, d, k, s):
    k.eps = s.sb("eps", [P, 1])
    k.ones = s.sb("ones", [P, P])
    k.causal = s.sb("causal", [P, P])
    k.z = s.sb("z", [P, 94])
    k.pkv = s.sb("pkv", [32, 2 * DB, 2 * HEAD])
    k.neglam = s.sb("neglam", [P, 1])
    project(nc, d, k)
    constants(nc, d, k)
    with Stage(nc, "at") as a:
        k.rows_s = a.sb("rows_s", [NS, TW])
        k.attT = a.sb("attT", [P, XCH, ROWS])
        k.selb = a.sb("selb", [NBLK, DB, NBLK])
        with Stage(nc, "ap") as p:
            k.rows_p = p.sb("rows_p", [P, PT, TW])
            prepare(nc, d, k)
            prompt_attend(nc, d, k)
            compress(nc, d, k)
        decode_attend(nc, d, k)
    with Stage(nc, "ml") as c:
        k.qkT = c.sb("qkT", [P, 8, ROWS])
        k.k_rows = c.sb("k_rows", [P, 5, HC * DC])
        k.gate_i = c.sb("gate_i", [HC, ROWS])
        k.gate_f = c.sb("gate_f", [HC, ROWS])
        convolve(nc, d, k)
        mlstm(nc, d, k, False)
        mlstm(nc, d, k, True)
    output(nc, d, k)


class Names:
    pass


INPUTS = ["x_prompt", "x_sample", "cache_a_kv", "cache_b_kv", "state_b_win", "state_c_conv", "state_c_C",
          "state_c_n", "state_c_m", "page_table", "norm_g", "w_in", "w_out", "a_qk_g", "a_lambda", "a_out_g",
          "b_qk_g", "b_cmp_w", "c_conv_w", "c_conv_b", "c_gate_b", "c_out_g"]
QKC = 2 * HC * DC
OUTPUTS = [(1, SEQ, D), (DB, DT, D), (1, 1, SEQ, 2, HA, HEAD), (1, DB, DT, 2, HA, HEAD),
           (1, 1, SEQ, 4, HEAD), (1, DB, DT, 4, HEAD), (1, 1, WIN, 2, HEAD), (1, DB, WIN, 2, HEAD),
           (1, 1, 3, QKC), (1, DB, 3, QKC), (1, 1, HC, HEAD, DC), (1, DB, HC, HEAD, DC),
           (1, 1, HC, DC), (1, DB, HC, DC), (1, 1, HC), (1, DB, HC)]


def build(nc, a, o):
    d, k = Names(), Names()
    d.x_prompt = a["x_prompt"][0]
    d.x_sample = a["x_sample"].rearrange("b t d -> (b t) d")
    d.cache_a = a["cache_a_kv"][0].rearrange("n p a h d -> n p (a h d)")
    d.cache_b = a["cache_b_kv"][0].rearrange("n p a d -> n p (a d)")
    d.b_win = a["state_b_win"][0].rearrange("b w a d -> b w (a d)")
    d.c_conv = a["state_c_conv"][0]
    d.c_C, d.c_n, d.c_m = a["state_c_C"][0], a["state_c_n"][0], a["state_c_m"][0]
    d.page_table = a["page_table"]
    d.norm_g, d.w_in, d.w_out = a["norm_g"][0], a["w_in"][0], a["w_out"][0]
    d.a_qk_g, d.a_lambda, d.a_out_g = a["a_qk_g"][0], a["a_lambda"][0], a["a_out_g"][0]
    d.b_qk_g, d.b_cmp_w, d.c_conv_w = a["b_qk_g"][0], a["b_cmp_w"][0], a["c_conv_w"][0]
    d.c_conv_b, d.c_gate_b, d.c_out_g = a["c_conv_b"][0], a["c_gate_b"][0], a["c_out_g"][0]
    d.y_p, d.y_s = o[0][0], o[1].rearrange("b t d -> (b t) d")
    d.a_kv_p = o[2][0, 0].rearrange("t a h d -> t (a h d)")
    d.a_kv_s = o[3][0].rearrange("b t a h d -> (b t) (a h d)")
    d.b_kv_p = o[4][0, 0].rearrange("t a d -> t (a d)")
    d.b_kv_s = o[5][0].rearrange("b t a d -> (b t) (a d)")
    d.win_p = o[6][0, 0].rearrange("t a d -> t (a d)")
    d.win_s = o[7][0].rearrange("b t a d -> b t (a d)")
    d.conv_p, d.conv_s = o[8][0, 0], o[9][0]
    d.C_p, d.C_s, d.n_p, d.n_s = o[10][0, 0], o[11][0], o[12][0, 0], o[13][0]
    d.m_p, d.m_s = o[14][0, 0], o[15][0]
    d.proj = nc.dram_tensor("proj", [ROWS, N_IN], F32).ap()
    d.o_att = nc.dram_tensor("o_att", [ROWS, 4 * 512], F32).ap()
    d.h_c = nc.dram_tensor("h_c", [ROWS, HC * HEAD], F32).ap()
    with Stage(nc, "all") as s:
        k.ident = s.sb("ident", [P, P])
        stages(nc, d, k, s)


def kernel(**inputs):
    import numpy as np
    import concourse.bacc as bacc
    from concourse.bass_utils import run_bass_kernel_spmd

    nc = bacc.Bacc("TRN2", target_bir_lowering=False, num_devices=1)
    arrays, a = {}, {}
    for name in INPUTS:
        v = np.ascontiguousarray(inputs[name])
        arrays[f"in_{name}"] = v
        a[name] = nc.dram_tensor(f"in_{name}", v.shape, mybir.dt.from_np(v.dtype), kind="ExternalInput").ap()
    o = [nc.dram_tensor(f"out_{i}", shape, F32, kind="ExternalOutput").ap() for i, shape in enumerate(OUTPUTS)]
    build(nc, a, o)
    r = run_bass_kernel_spmd(nc, [arrays], core_ids=[0])
    return tuple(r.results[0][f"out_{i}"] for i in range(len(OUTPUTS)))
```

```python
from contextlib import ExitStack

import concourse.bass as bass
from concourse import mybir

F32 = mybir.dt.float32
I32 = mybir.dt.int32
F32R = mybir.dt.float32r
ACT = mybir.ActivationFunctionType
ALU = mybir.AluOpType
AX_X = mybir.AxisListType.X

P = 128
D = 2048
KC = D // P
SEQ = 512
DB, DT = 8, 4
NS = DB * DT
ROWS = SEQ + NS
PT = SEQ // P
TILES = [(P * t, P) for t in range(PT)] + [(SEQ, NS)]
N_IN = 7964
HEAD = 128
HA, HB, HC = 4, 4, 8
DC = 64
PAGE = 128
PAGES = 32
PAST = PAGE * PAGES
CMP = 64
NBLK = PAST // CMP
WIN = 512
EPS = 1e-6
LAM0 = 0.8 - 0.6
NEG = -1.0e30
A_SCALE = DC ** -0.5
B_SCALE = HEAD ** -0.5

C_AQ, C_AZ, C_BQ, C_BG, C_BZ = 0, 1536, 2048, 3328, 3340
C_CQK, C_CV, C_CIF, C_CO, C_CZ = 3852, 4876, 5900, 5916, 6940
T_AQ, T_AK, T_AV, T_BQ, T_KC = 0, 512, 1024, 1536, 2048
T_VC, T_KS, T_VS, T_KW, T_VW = 2176, 2304, 2432, 2560, 2688
TW = 2816
X_AQ, X_AK, X_BQ, X_KS, X_KW = 0, 4, 8, 12, 13
XCH = 14
X_COL = [T_AQ + HEAD * h for h in range(HA)] + [T_AK + HEAD * h for h in range(HA)] \
    + [T_BQ + HEAD * h for h in range(HB)] + [T_KS, T_KW]
SLAB = 512


class Stage:

    def __init__(self, nc, name):
        self.nc, self.name, self.stack, self.used = nc, name, ExitStack(), []

    def __enter__(self):
        self.stack.__enter__()
        return self

    def __exit__(self, *e):
        if self.used and e[0] is None:
            self.nc.clear_and_free_semaphores(self.used)
            self.nc.all_engine_barrier()
        return self.stack.__exit__(*e)

    def sb(self, name, shape, dt=F32):
        return self.stack.enter_context(self.nc.sbuf_tensor(f"{self.name}_{name}", shape, dt))

    def ps(self, name, shape, dt=F32):
        return self.stack.enter_context(self.nc.psum_tensor(f"{self.name}_{name}", shape, dt))

    def sem(self, name):
        self.used.append(self.nc.alloc_semaphore(f"{self.name}_{name}"))
        return self.used[-1]

    def sems(self, name, n):
        return [self.sem(f"{name}{i}") for i in range(n)]


class Chain:

    def __init__(self, eng, sem):
        self.eng, self.sem, self.n = eng, sem, 0

    def __call__(self, ins):
        self.n += 1
        ins.then_inc(self.sem, 1)
        self.eng.wait_ge(self.sem, self.n)


def project(nc, d, k):
    NSLAB = -(-N_IN // SLAB)
    LAST = N_IN - (NSLAB - 1) * SLAB
    PC, RING = 2, 4
    NP = KC // PC
    HALF = DB * PAGES // NSLAB
    assert HALF * 2 == PAGES and HALF == 16
    with Stage(nc, "pj") as s:
        x = s.sb("x", [P, 2, D])
        ssq = s.sb("ssq", [P, 8])
        rms = s.sb("rms", [P, 8])
        rstd = s.sb("rstd", [P, 8])
        gain = s.sb("gain", [P, KC])
        eps = s.sb("eps", [P, 1])
        w = s.sb("w", [P, 2, PC, SLAB])
        whi = s.sb("whi", [P, RING, PC, SLAB], F32R)
        wlo = s.sb("wlo", [P, RING, PC, SLAB], F32R)
        table = s.sb("table", [1, DB * PAGES], I32)
        pages = s.sb("pages", [P, 2, 4, 2 * HEAD])
        out = s.sb("out", [P, 5, SLAB])
        low = s.sb("low", [NS, SLAB])
        ps = [s.ps(f"ps{i}", [P, SLAB]) for i in range(8)]
        xg = s.sb("xg", [P, 2, 4, P])
        sq = out[:, 0:4, :].rearrange("p a n -> p (a n)")
        xhi = s.sb("xhi", [P, KC, SEQ], F32R)
        xlo = s.sb("xlo", [P, KC, SEQ], F32R)
        xs = s.sb("xs", [P, KC, 2 * NS], F32R)

        x_loaded = s.sems("x_loaded", 2)
        gain_loaded = s.sem("gain_loaded")
        ident_ready = s.sem("ident_ready")
        squared = s.sem("squared")
        rooted = s.sem("rooted")
        inverted = s.sem("inverted")
        scaled = s.sem("scaled")
        turned = s.sem("turned")
        xg_ready = s.sem("xg_ready")
        xhi_ready = s.sem("xhi_ready")
        xlo_ready = s.sem("xlo_ready")
        w_loaded = s.sems("w_loaded", 2)
        whi_ready = s.sem("whi_ready")
        wlo_ready = s.sem("wlo_ready")
        w_used = s.sem("w_used")
        store_turn = s.sem("store_turn")
        table_loaded = s.sem("table_loaded")
        z_zeroed = s.sem("z_zeroed")
        z_loaded = s.sem("z_loaded")
        pages_loaded = s.sems("pages_loaded", 2)
        pages_used = s.sem("pages_used")
        pool_out = s.sem("pool_out")
        product_ready = s.sems("product_ready", 5)
        low_out = s.sem("low_out")
        evacuated = s.sems("evacuated", 5)
        stored = s.sems("stored", 5)
        wv = d.w_in.rearrange("(c p) n -> p c n", p=P)

        def high(t):
            return xhi[:, :, P * t:P * t + P] if t < PT else xs[:, :, 0:NS]

        def low_part(t):
            return xlo[:, :, P * t:P * t + P] if t < PT else xs[:, :, NS:2 * NS]

        with nc.Block() as block:
            @block.sync
            def _(sp):
                def load_x(t):
                    r0, rows = TILES[t]
                    src = d.x_prompt[r0:r0 + rows, :] if t < PT else d.x_sample
                    if t >= 2:
                        sp.wait_ge(turned, 4 * (t - 1))
                    sp.dma_start(x[0:rows, t % 2, :], src).then_inc(x_loaded[t % 2], 16)

                def load_w(j, c, n):
                    sp.dma_start(w[:, c % 2, :, 0:n],
                                 wv[:, PC * c:PC * c + PC, bass.ds(j * SLAB, n)]).then_inc(w_loaded[c % 2], 16)

                def store(j, t, n):
                    r0, rows = TILES[t]
                    sp.wait_ge(evacuated[t], j + 2)
                    sp.sem_inc(store_turn, 1)
                    sp.dma_start(d.proj[r0:r0 + rows, bass.ds(j * SLAB, n)],
                                 out[0:rows, t, 0:n]).then_inc(stored[t], 16)

                def load_next(j, c, n):
                    sp.wait_ge(wlo_ready, j * NP + c + 1)
                    load_w(j + (c + 2) // NP, (c + 2) % NP, n)

                def step(j, here, after):
                    for c in range(RING, NP):
                        if c + 2 < NP or after:
                            load_next(j, c, here if c + 2 < NP else after)
                    for c in range(RING - 1):
                        if after:
                            load_next(j + 1, c, after)
                    for t in range(5):
                        store(j, t, here)
                    if after:
                        load_next(j + 1, RING - 1, after)

                for t in range(5):
                    sp.sem_inc(stored[t], 16)
                load_x(0)
                load_x(1)
                load_w(0, 0, SLAB)
                load_w(0, 1, SLAB)
                for t in range(2, 5):
                    load_x(t)
                for c in range(RING):
                    load_next(0, c, SLAB)
                with sp.Fori(0, NSLAB - 2) as j:
                    step(j, SLAB, SLAB)
                step(NSLAB - 2, SLAB, LAST)
                step(NSLAB - 1, LAST, None)
                for t in range(5):
                    sp.wait_ge(stored[t], 16 + 16 * NSLAB)

            @block.gpsimd
            def _(pool):
                pool.dma_start(gain[:], d.norm_g.rearrange("(c p) -> p c", p=P),
                               allow_slow_non_contiguous=True).then_inc(gain_loaded, 16)
                pool.memset(k.z[:], 0.0).then_inc(z_zeroed, 1)
                pool.wait_ge(z_zeroed, 1)
                for a in range(2):
                    for j in range(2):
                        pool.dma_start(k.z[CMP * j:CMP * (j + 1), 30 + 32 * a + j:31 + 32 * a + j],
                                       d.b_cmp_w[a, :].unsqueeze(1)).then_inc(z_loaded, 16)
                pool.memset(eps[:], EPS).then_inc(ident_ready, 1)
                pool.memset(k.ident[:], 0.0).then_inc(ident_ready, 1)
                pool.wait_ge(ident_ready, 2)
                pool.affine_select(out=k.ident[:], in_=k.ident[:], compare_op=ALU.not_equal, fill=1.0,
                                   base=0, pattern=[[-1, P]], channel_multiplier=1).then_inc(ident_ready, 1)

            @block.scalar
            def _(act):
                def split_x(t):
                    for q in range(4):
                        n = 4 * t + q
                        act.wait_ge(xg_ready, n + 1)
                        act.activation(high(t)[:, 4 * q:4 * q + 4, :], xg[:, n % 2, :, 0:TILES[t][1]],
                                       ACT.Copy).then_inc(xhi_ready, 1)

                def split_w(j, c, n):
                    act.wait_ge(w_loaded[c % 2], j * (8 * NP) + 16 * (c // 2) + 16)
                    act.wait_ge(w_used, j * NP + c + 1)
                    act.activation(whi[:, c % RING, :, 0:n], w[:, c % 2, :, 0:n], ACT.Copy).then_inc(whi_ready, 1)

                def load_pages(j, q):
                    act.wait_ge(pages_used, j * 4 + q + 1)
                    for i in range(4):
                        page = act.value_load(table[0:1, bass.ds(j * HALF + 4 * q + i, 1)],
                                              min_val=0, max_val=d.cache_b.shape[0] - 1)
                        act.dma_start(pages[:, q % 2, i, :], d.cache_b[bass.ds(page, 1), :, 0:2 * HEAD]
                                      .rearrange("a p n -> p (a n)")).then_inc(pages_loaded[q % 2], 16)

                act.dma_start(table[:], d.page_table.rearrange("(a b) n -> a (b n)", a=1)).then_inc(table_loaded, 16)
                act.sem_inc(pages_used, 2)
                act.sem_inc(pool_out, 1)
                act.wait_ge(ident_ready, 1)
                for t, (_, rows) in enumerate(TILES):
                    act.wait_ge(x_loaded[t % 2], 16 * (t // 2 + 1))
                    act.activation(sq[0:rows, :], x[0:rows, t % 2, :], ACT.Square,
                                   accum_out=ssq[0:rows, t:t + 1]).then_inc(squared, 1)
                    act.wait_ge(squared, t + 1)
                    act.activation(rms[0:rows, t:t + 1], ssq[0:rows, t:t + 1], ACT.Sqrt,
                                   bias=eps[0:rows, :], scale=1.0 / D).then_inc(rooted, 1)
                    if t:
                        split_x(t - 1)
                        split_w(0, t - 1, SLAB)
                split_x(4)
                act.wait_ge(table_loaded, 16)
                load_pages(0, 0)
                load_pages(0, 1)

                def step(j, width, after):
                    split_w(j, 4, width)
                    load_pages(j, 2)
                    split_w(j, 5, width)
                    split_w(j, 6, width)
                    load_pages(j, 3)
                    split_w(j, 7, width)
                    if after:
                        split_w(j + 1, 0, after)
                        load_pages(j + 1, 0)
                        split_w(j + 1, 1, after)
                        split_w(j + 1, 2, after)
                        load_pages(j + 1, 1)
                    act.wait_ge(pages_used, j * 4 + 6)
                    for a in range(2):
                        last = act.activation(k.pkv[:, bass.ds(j, 1), HEAD * a:HEAD * a + HEAD],
                                              ps[7][32 * a:32 * a + 32, HEAD * a:HEAD * a + HEAD].unsqueeze(1),
                                              ACT.Copy)
                    last.then_inc(pool_out, 1)
                    for t in (1, 3):
                        act.wait_ge(product_ready[t], j + 1)
                        act.wait_ge(stored[t], j * 16 + 16)
                        act.activation(out[:, t, 0:width], ps[t][:, 0:width], ACT.Copy).then_inc(evacuated[t], 1)
                    act.wait_ge(product_ready[4], j + 1)
                    act.wait_ge(evacuated[4], j + 1)
                    act.activation(low[:, 0:width], ps[4][NS:2 * NS, 0:width], ACT.Copy).then_inc(low_out, 1)
                    if after:
                        split_w(j + 1, 3, after)

                with act.Fori(0, NSLAB - 2) as j:
                    step(j, SLAB, SLAB)
                step(NSLAB - 2, SLAB, LAST)
                step(NSLAB - 1, LAST, None)

            @block.vector
            def _(dve):
                def split_x(n):
                    t, q = n // 4, n % 4
                    dve.wait_ge(xhi_ready, n + 1)
                    dve.tensor_tensor(low_part(t)[:, 4 * q:4 * q + 4, :], xg[:, n % 2, :, 0:TILES[t][1]],
                                      high(t)[:, 4 * q:4 * q + 4, :], ALU.subtract).then_inc(xlo_ready, 1)

                def split_w(j, c, n):
                    dve.wait_ge(whi_ready, j * NP + c + 1)
                    dve.tensor_tensor(wlo[:, c % RING, :, 0:n], w[:, c % 2, :, 0:n], whi[:, c % RING, :, 0:n],
                                      ALU.subtract).then_inc(wlo_ready, 1)

                for t in range(5):
                    dve.sem_inc(evacuated[t], 1)
                dve.sem_inc(w_used, RING)
                dve.wait_ge(gain_loaded, 16)
                for t, (r0, rows) in enumerate(TILES):
                    dve.wait_ge(rooted, t + 1)
                    dve.reciprocal(rstd[0:rows, t:t + 1], rms[0:rows, t:t + 1]).then_inc(inverted, 1)
                    dve.wait_ge(inverted, t + 1)
                    dve.tensor_scalar(x[0:rows, t % 2, :], x[0:rows, t % 2, :], rstd[0:rows, t:t + 1],
                                      None, ALU.mult).then_inc(scaled, 1)
                    for q in range(4):
                        n = 4 * t + q
                        dve.wait_ge(turned, n + 1)
                        if n >= 2:
                            dve.wait_ge(xlo_ready, n - 1)
                        dve.tensor_tensor(
                            xg[:, n % 2, :, 0:rows],
                            ps[n % 2 + 5][:, :].rearrange("p (c r) -> p c r", c=4)[:, :, 0:rows],
                            gain[:, 4 * q:4 * q + 4].unsqueeze(2).broadcast_to([P, 4, rows]),
                            ALU.mult).then_inc(xg_ready, 1)
                        if q:
                            split_x(n - 1)
                    split_x(4 * t + 3)
                    if t >= 2:
                        split_w(0, t - 2, SLAB)
                split_w(0, 3, SLAB)

                def step(j, width, after):
                    for c in range(RING, NP):
                        split_w(j, c, width)
                    if after:
                        for c in range(3):
                            split_w(j + 1, c, after)
                    for t in (0, 2):
                        dve.wait_ge(product_ready[t], j + 1)
                        dve.wait_ge(stored[t], j * 16 + 16)
                        dve.tensor_copy(out[:, t, 0:width], ps[t][:, 0:width]).then_inc(evacuated[t], 1)
                    dve.wait_ge(low_out, j + 1)
                    dve.wait_ge(stored[4], j * 16 + 16)
                    dve.tensor_tensor(out[0:NS, 4, 0:width], ps[4][0:NS, 0:width], low[:, 0:width],
                                      ALU.add).then_inc(evacuated[4], 1)
                    if after:
                        split_w(j + 1, 3, after)

                with dve.Fori(0, NSLAB - 2) as j:
                    step(j, SLAB, SLAB)
                step(NSLAB - 2, SLAB, LAST)
                step(NSLAB - 1, LAST, None)

            @block.tensor
            def _(pe):
                pe.wait_ge(ident_ready, 3)
                for t, (r0, rows) in enumerate(TILES):
                    pe.wait_ge(scaled, t + 1)
                    for q in range(4):
                        n = 4 * t + q
                        if n >= 2:
                            pe.wait_ge(xg_ready, n - 1)
                        for c in range(4):
                            col = (4 * q + c) * P
                            last = pe.transpose(ps[n % 2 + 5][:, c * P:c * P + rows],
                                                x[0:rows, t % 2, col:col + P], k.ident[0:rows, 0:rows])
                        last.then_inc(turned, 1)

                def pool_pages(j, q):
                    if q == 0:
                        pe.wait_ge(pool_out, j + 1)
                    pe.wait_ge(pages_loaded[q % 2], j * 128 + 64 * (q // 2) + 64)
                    for i in range(4):
                        p = 4 * q + i
                        last = pe.matmul(ps[7][0:64, 0:2 * HEAD], k.z[:, 30 - 2 * p:94 - 2 * p],
                                         pages[:, q % 2, i, :], start=(p == 0), stop=(p == HALF - 1))
                    last.then_inc(pages_used, 1)

                def multiply(j, width):
                    for c in range(NP):
                        pe.wait_ge(wlo_ready, j * NP + c + 1)
                        for t in range(5):
                            if c == 0:
                                pe.wait_ge(evacuated[t], j + 1)
                            for i in range(PC):
                                kc = PC * c + i
                                first, end = kc == 0, kc == KC - 1
                                high, low = whi[:, c % RING, i, 0:width], wlo[:, c % RING, i, 0:width]
                                if t < PT:
                                    acc = ps[t][:, 0:width]
                                    hi, lo = (v[:, kc, P * t:P * t + P] for v in (xhi, xlo))
                                    pe.matmul(acc, hi, high, start=first, stop=False)
                                    pe.matmul(acc, hi, low, start=False, stop=False)
                                    last = pe.matmul(acc, lo, high, start=False, stop=end)
                                else:
                                    acc = ps[t][0:2 * NS, 0:width]
                                    pe.matmul(acc, xs[:, kc, :], high, start=first, stop=False)
                                    last = pe.matmul(acc, xs[:, kc, :], low, start=False, stop=end)
                            if c == NP - 1:
                                last.then_inc(product_ready[t], 1)
                        if c < NP - 1:
                            last.then_inc(w_used, 1)
                        if c % 2 == 0:
                            pool_pages(j, c // 2)
                    pe.wait_ge(product_ready[4], j + 1)
                    pe.sem_inc(w_used, 1)

                pe.wait_ge(z_loaded, 64)
                pe.wait_ge(xlo_ready, 20)
                with pe.Fori(0, NSLAB - 1) as j:
                    multiply(j, SLAB)
                multiply(NSLAB - 1, LAST)


def prepare(nc, d, k):
    with Stage(nc, "pr") as s:
        sq = s.sb("sq", [P, 2, 1792])
        ss = s.sb("ss", [P, 5, 32])
        rms = s.sb("rms", [P, 5, 32])
        rstd = s.sb("rstd", [P, 5, 32])
        lp = s.sb("lp", [P, 4, DC])
        prod = s.sb("prod", [P, 2, DC])
        dots = s.sb("dots", [P, 2])
        exps = s.sb("exps", [P, 2])
        ga = s.sb("ga", [P, 2, DC])
        gb = s.sb("gb", [P, 4, HEAD])
        ps = [s.ps(f"ps{i}", [P, 512]) for i in range(4)]
        tiles_loaded = s.sems("tiles_loaded", 5)
        gains_loaded = s.sem("gains_loaded")
        dve_step = s.sem("dve_step")
        made = s.sem("made")
        lambda_loaded = s.sem("lambda_loaded")
        dotted = s.sem("dotted")
        exped = s.sem("exped")
        gains_ready = s.sem("gains_ready")
        squared = s.sem("squared")
        scaled = s.sem("scaled")
        summed = s.sem("summed")
        rooted = s.sem("rooted")
        normed = s.sem("normed")
        turned = s.sem("turned")
        copied = s.sem("copied")
        stored = s.sem("stored")
        NQ = -(-XCH // 4)

        def heads(t, rows):
            T = tile(t)
            v = lambda c0, n, w: T[0:rows, c0:c0 + n * w].rearrange("p (h w) -> p h w", w=w)
            return [(v(T_AQ, 8, DC), 0, ga[0:rows, 0, :]), (v(T_AK, 8, DC), 8, ga[0:rows, 1, :]),
                    (v(T_BQ, HB, HEAD), 16, gb[0:rows, 0, :]), (v(T_KS, 1, HEAD), 20, gb[0:rows, 2, :]),
                    (v(T_KW, 1, HEAD), 21, gb[0:rows, 3, :])]

        def tile(t):
            return k.rows_p[:, t, :] if t < PT else k.rows_s[:, :]

        with nc.Block() as block:
            @block.sync
            def _(sp):
                for t, (r0, rows) in enumerate(TILES):
                    sp.dma_start(tile(t)[0:rows, 0:T_BQ], d.proj[r0:r0 + rows, 0:C_AZ]).then_inc(tiles_loaded[t], 16)
                    sp.dma_start(tile(t)[0:rows, T_BQ:TW],
                                 d.proj[r0:r0 + rows, C_BQ:C_BG]).then_inc(tiles_loaded[t], 16)
                n = 0
                for b in range(DB):
                    sp.dma_start(d.win_s[b, 0:WIN - DT, :], d.b_win[b, DT:WIN, :]).then_inc(stored, 16)
                    n += 16
                for t, (r0, rows) in enumerate(TILES):
                    a, b, win = ((d.a_kv_p, d.b_kv_p, d.win_p) if t < PT else (d.a_kv_s, d.b_kv_s, None))
                    q0 = r0 if t < PT else 0
                    sp.wait_ge(normed, t + 1)
                    sp.dma_start(a[q0:q0 + rows, :], tile(t)[0:rows, T_AK:T_BQ]).then_inc(stored, 16)
                    sp.dma_start(b[q0:q0 + rows, :], tile(t)[0:rows, T_KC:T_KW]).then_inc(stored, 16)
                    n += 32
                    if win is not None:
                        sp.dma_start(win[q0:q0 + rows, :], tile(t)[0:rows, T_KW:TW]).then_inc(stored, 16)
                        n += 16
                for b in range(DB):
                    sp.dma_start(d.win_s[b, WIN - DT:WIN, :],
                                 tile(4)[DT * b:DT * b + DT, T_KW:TW]).then_inc(stored, 16)
                    n += 16
                sp.wait_ge(stored, n)

            @block.gpsimd
            def _(pool):
                pool.memset(k.eps[:], EPS).then_inc(made, 1)
                pool.dma_start(ga[:], d.a_qk_g.partition_broadcast(P)).then_inc(gains_loaded, 16)
                pool.dma_start(gb[:], d.b_qk_g.partition_broadcast(P)).then_inc(gains_loaded, 16)
                pool.dma_start(lp[:], d.a_lambda.partition_broadcast(P)).then_inc(lambda_loaded, 16)
                pool.memset(k.ones[:], 1.0).then_inc(made, 1)
                pool.memset(k.causal[:], 0.0).then_inc(made, 1)
                pool.wait_ge(made, 3)
                pool.affine_select(out=k.causal[:], in_=k.causal[:], compare_op=ALU.is_ge, fill=NEG,
                                   base=0, pattern=[[-1, P]], channel_multiplier=1).then_inc(made, 1)
                pool.wait_ge(gains_ready, 1)
                for t, (r0, rows) in enumerate(TILES):
                    pool.wait_ge(scaled, t + 1)
                    for v, _, g in heads(t, rows):
                        n, w = v.shape[1], v.shape[2]
                        last = pool.tensor_tensor(v, v, g.unsqueeze(1).broadcast_to([rows, n, w]), ALU.mult)
                    last.then_inc(normed, 1)

            @block.scalar
            def _(act):
                act.wait_ge(dotted, 1)
                act.activation(exps[:], dots[:], ACT.Exp).then_inc(exped, 1)
                act.wait_ge(made, 1)

                def root(t):
                    rows = TILES[t][1]
                    act.wait_ge(summed, t + 1)
                    act.activation(rms[0:rows, t, 0:22], ss[0:rows, t, 0:22], ACT.Sqrt,
                                   bias=k.eps[0:rows, :]).then_inc(rooted, 1)

                for t, (r0, rows) in enumerate(TILES):
                    act.wait_ge(tiles_loaded[t], 32)
                    if t >= 2:
                        act.wait_ge(summed, t - 1)
                    at = 0
                    for v, _, _ in heads(t, rows):
                        n, w = v.shape[1], v.shape[2]
                        last = act.activation(sq[0:rows, t % 2, at:at + n * w].rearrange("p (h w) -> p h w", w=w),
                                              v, ACT.Square)
                        at += n * w
                    last.then_inc(squared, 1)
                    if t:
                        root(t - 1)
                root(4)
                n = 0
                for t, (r0, rows) in enumerate(TILES):
                    for q in range(NQ):
                        m = min(4, XCH - 4 * q)
                        n += 1
                        act.wait_ge(turned, n)
                        act.activation(k.attT[:, 4 * q:4 * q + m, r0:r0 + rows],
                                       ps[n % 4][:, :].rearrange("p (c r) -> p c r", c=4)[:, 0:m, 0:rows],
                                       ACT.Copy).then_inc(copied, 1)

            @block.vector
            def _(dve):
                step = Chain(dve, dve_step)
                dve.wait_ge(lambda_loaded, 16)
                step(dve.tensor_tensor(prod[:], lp[:, 0:4:2, :], lp[:, 1:4:2, :], ALU.mult))
                dve.tensor_reduce(dots[:], prod[:], AX_X, ALU.add).then_inc(dotted, 1)
                dve.wait_ge(gains_loaded, 32)
                step(dve.tensor_scalar(ga[:, 0, :], ga[:, 0, :], A_SCALE, None, ALU.mult))
                step(dve.tensor_scalar(gb[:, 0, :], gb[:, 0, :], B_SCALE, None, ALU.mult))

                dve.sem_inc(gains_ready, 1)

                def scale(t):
                    rows = TILES[t][1]
                    dve.wait_ge(rooted, t + 1)
                    step(dve.reciprocal(rstd[0:rows, t, 0:22], rms[0:rows, t, 0:22]))
                    for v, c, _ in heads(t, rows):
                        n, w = v.shape[1], v.shape[2]
                        last = dve.tensor_tensor(v, v, rstd[0:rows, t, c:c + n].unsqueeze(2).broadcast_to(
                            [rows, n, w]), ALU.mult)
                    last.then_inc(scaled, 1)

                for t, (r0, rows) in enumerate(TILES):
                    dve.wait_ge(squared, t + 1)
                    dve.tensor_reduce(ss[0:rows, t, 0:16], sq[0:rows, t % 2, 0:1024].rearrange(
                        "p (h w) -> p h w", w=DC), AX_X, ALU.add)
                    step(dve.tensor_reduce(ss[0:rows, t, 16:22], sq[0:rows, t % 2, 1024:1792].rearrange(
                        "p (h w) -> p h w", w=HEAD), AX_X, ALU.add))
                    dve.tensor_scalar(ss[0:rows, t, 0:16], ss[0:rows, t, 0:16], 1.0 / DC, None, ALU.mult)
                    dve.tensor_scalar(ss[0:rows, t, 16:22], ss[0:rows, t, 16:22], 1.0 / HEAD, None,
                                      ALU.mult).then_inc(summed, 1)
                    if t:
                        scale(t - 1)
                scale(4)
                dve.wait_ge(exped, 1)
                step(dve.tensor_tensor(k.neglam[:], exps[:, 1:2], exps[:, 0:1], ALU.subtract))
                step(dve.tensor_scalar(k.neglam[:], k.neglam[:], -LAM0, None, ALU.add))

            @block.tensor
            def _(pe):
                n = 0
                for t, (r0, rows) in enumerate(TILES):
                    pe.wait_ge(normed, t + 1)
                    for q in range(NQ):
                        n += 1
                        if n > 4:
                            pe.wait_ge(copied, n - 4)
                        for c in range(4 * q, min(4 * q + 4, XCH)):
                            last = pe.transpose(ps[n % 4][:, (c % 4) * P:(c % 4) * P + rows],
                                                tile(t)[0:rows, X_COL[c]:X_COL[c] + P],
                                                k.ident[0:rows, 0:rows])
                        last.then_inc(turned, 1)


def prompt_attend(nc, d, k):
    units = []
    for t in range(PT):
        for h in range(HA):
            units += [(t, 0, X_AK + h, X_AQ + h, DC * c, T_AV + HEAD * h) for c in range(2)]
        units += [(t, 1, X_KS, X_BQ + h, 0, T_VS) for h in range(HB)]
        units += [(t, 2, X_KW, X_BQ + h, 0, T_VW) for h in range(HB)]
    pvs = []
    for u, (t, sec, _, _, p0, vcol) in enumerate(units):
        if sec == 0 and p0 == 0:
            continue
        head = (u % 16) // 2 if sec == 0 else (u % 16) % 4
        pvs.append((u, t, sec, head, vcol))
    NU, NV = len(units), len(pvs)
    NSEC = 3 * PT
    with Stage(nc, "pa") as s:
        e = s.sb("e", [P, 6, 512])
        w = s.sb("w", [P, 2, 512])
        wT = s.sb("wT", [P, 2, 4, P])
        nm = s.sb("nm", [P, NU])
        l = s.sb("l", [P, NU])
        r = s.sb("r", [P, NU])
        o = s.sb("o", [P, 2, 512])
        scores = [s.ps(f"scores{i}", [P, 512]) for i in range(3)]
        tp = [s.ps(f"tp{i}", [P, 4, P]) for i in range(2)]
        po = [s.ps(f"po{i}", [P, 4, HEAD]) for i in range(3)]
        scored = s.sem("scored")
        maxed = s.sem("maxed")
        exped = s.sem("exped")
        inverted = s.sem("inverted")
        divisors = s.sem("divisors")
        weighted = s.sem("weighted")
        scaled = s.sem("scaled")
        turned = s.sem("turned")
        copied = s.sem("copied")
        summed = s.sem("summed")
        finished = s.sem("finished")
        stored = s.sems("stored", 2)
        NA = [sum(1 for v in pvs[:i] if v[2] == 0) for i in range(NV + 1)]

        with nc.Block() as block:
            @block.sync
            def _(sp):
                for c in range(NSEC):
                    t, sec = c // 3, c % 3
                    sp.wait_ge(finished, c + 1)
                    sp.dma_start(d.o_att[P * t:P * t + P, 512 * sec:512 * sec + 512],
                                 o[:, c % 2, :]).then_inc(stored[c % 2], 16)
                for b in range(2):
                    sp.wait_ge(stored[b], 8 * NSEC)

            @block.tensor
            def _(pe):
                def score(u):
                    t, sec, kc, qc, p0, _ = units[u]
                    kn = DC if sec == 0 else P
                    n = P * (t + 1)
                    if u >= 3:
                        pe.wait_ge(exped, u - 2)
                    pe.matmul(scores[u % 3][:, 0:n], k.attT[p0:p0 + kn, qc, P * t:P * t + P],
                              k.attT[p0:p0 + kn, kc, 0:n], start=True, stop=False)
                    pe.matmul(scores[u % 3][:, n - P:n], k.ident[:], k.causal[:], start=False,
                              stop=True).then_inc(scored, 1)

                def turn(i):
                    u, t, sec, h, _ = pvs[i]
                    if sec == 0:
                        pe.wait_ge(weighted, NA[i] + 1)
                        src = w[:, NA[i] % 2, :]
                    else:
                        pe.wait_ge(exped, u + 1)
                        src = e[:, u % 6, :]
                    if i >= 2:
                        pe.wait_ge(copied, i - 1)
                    for b in range(t + 1):
                        last = pe.transpose(tp[i % 2][:, b, :], src[:, P * b:P * b + P], k.ident[:])
                    last.then_inc(turned, 1)

                def attend(i):
                    u, t, sec, h, vcol = pvs[i]
                    c = 3 * t + sec
                    if h == 0 and c >= 3:
                        pe.wait_ge(finished, c - 2)
                    pe.wait_ge(copied, i + 1)
                    for b in range(t + 1):
                        last = pe.matmul(po[c % 3][:, h, :], wT[:, i % 2, b, :],
                                         k.rows_p[:, b, vcol:vcol + HEAD], start=(b == 0), stop=(b == t))
                    last.then_inc(summed, 1)

                done = 0
                for i in range(NV + 2):
                    if i < NV:
                        while done <= min(pvs[i][0] + 1, NU - 1):
                            score(done)
                            done += 1
                    if 1 <= i <= NV:
                        turn(i - 1)
                    if i >= 2:
                        attend(i - 2)

            @block.scalar
            def _(act):
                for u in range(NU):
                    t = units[u][0]
                    n = P * (t + 1)
                    act.wait_ge(maxed, u + 1)
                    if u >= 6:
                        act.wait_ge(turned, sum(1 for v in pvs if v[0] <= u - 6))
                        act.wait_ge(weighted, sum(1 for v in pvs if v[2] == 0 and v[0] <= u - 5))
                    act.activation(e[:, u % 6, 0:n], scores[u % 3][:, 0:n], ACT.Exp, bias=nm[:, u:u + 1],
                                   accum_out=l[:, u:u + 1]).then_inc(exped, 1)

            @block.vector
            def _(dve):
                def row_max(u):
                    n = P * (units[u][0] + 1)
                    dve.wait_ge(scored, u + 1)
                    dve.tensor_reduce(nm[:, u:u + 1], scores[u % 3][:, 0:n], AX_X, ALU.max,
                                      negate=True).then_inc(maxed, 1)

                def weigh(i):
                    u, t, _, _, _ = pvs[i]
                    n = P * (t + 1)
                    a = NA[i]
                    dve.wait_ge(exped, u + 1)
                    dve.reciprocal(r[:, u - 1:u + 1], l[:, u - 1:u + 1]).then_inc(inverted, 1)
                    dve.wait_ge(inverted, 2 * a + 1)
                    if i >= 2 and a >= 2:
                        j = next(x for x in range(NV) if NA[x] == a - 2 and pvs[x][2] == 0)
                        dve.wait_ge(turned, j + 1)
                    dve.tensor_scalar(w[:, a % 2, 0:n], e[:, (u - 1) % 6, 0:n], r[:, u - 1:u], None,
                                      ALU.mult).then_inc(scaled, 1)
                    dve.tensor_scalar(r[:, u:u + 1], r[:, u:u + 1], k.neglam[:, 0:1], None,
                                      ALU.mult).then_inc(inverted, 1)
                    dve.wait_ge(scaled, a + 1)
                    dve.wait_ge(inverted, 2 * a + 2)
                    dve.scalar_tensor_tensor(w[:, a % 2, 0:n], e[:, u % 6, 0:n], r[:, u:u + 1],
                                             w[:, a % 2, 0:n], ALU.mult, ALU.add).then_inc(weighted, 1)

                def copy(i):
                    t = pvs[i][1]
                    dve.wait_ge(turned, i + 1)
                    if i >= 2:
                        dve.wait_ge(summed, i - 1)
                    dve.tensor_copy(wT[:, i % 2, 0:t + 1, :], tp[i % 2][:, 0:t + 1, :]).then_inc(copied, 1)

                def finish(i):
                    u, t, sec, h, _ = pvs[i]
                    c = 3 * t + sec
                    dve.wait_ge(summed, i + 1)
                    if c >= 2:
                        dve.wait_ge(stored[c % 2], 16 * (c // 2))
                    out = o[:, c % 2, :].rearrange("p (h w) -> p h w", h=4)
                    if sec == 0:
                        dve.tensor_copy(out, po[c % 3][:]).then_inc(finished, 1)
                        return
                    dve.wait_ge(exped, u + 1)
                    dve.reciprocal(r[:, u - 3:u + 1], l[:, u - 3:u + 1]).then_inc(divisors, 1)
                    dve.wait_ge(divisors, 2 * t + sec)
                    dve.tensor_tensor(out, po[c % 3][:], r[:, u - 3:u + 1].unsqueeze(2).broadcast_to(
                        [P, 4, HEAD]), ALU.mult).then_inc(finished, 1)

                done = 0
                for i in range(NV + 3):
                    if i < NV:
                        while done <= min(pvs[i][0] + 1, NU - 1):
                            row_max(done)
                            done += 1
                        if pvs[i][2] == 0:
                            weigh(i)
                    if 1 <= i <= NV:
                        copy(i - 1)
                    if i >= 3 and pvs[i - 3][3] == 3:
                        finish(i - 3)


def compress(nc, d, k):
    with Stage(nc, "cm") as s:
        kc = s.sb("kc", [NBLK, DB + 1, HEAD])
        vc = s.sb("vc", [NBLK, DB + 1, HEAD])
        sq = s.sb("sq", [NBLK, DB + 1, HEAD])
        ss = s.sb("ss", [NBLK, 3, DB + 1])
        g = s.sb("g", [NBLK, HEAD])
        kcT = s.sb("kcT", [P, DB + 1, NBLK])
        qpad = s.sb("qpad", [P, DB * 144])
        same = s.sb("same", [P, P])
        shift = s.sb("shift", [P, 176])
        mul = s.sb("mul", [P, PT, 8])
        bias = s.sb("bias", [P, PT, 8])
        st = s.sb("st", [P, 8, 16])
        pc = s.sb("pc", [P, PT * HB, 8])
        pcT = s.sb("pcT", [8, PT, HB, P])
        pd = s.sb("pd", [P, NBLK])
        imp = s.sb("imp", [P, 3, NBLK])
        top = s.sb("top", [P, 2, 8])
        pdT = s.sb("pdT", [NBLK, HB, 288])
        o = s.sb("o", [P, 2, 512])
        acc = s.ps("acc", [NBLK, 2 * HEAD])
        tp = [s.ps(f"tp{i}", [P, 512]) for i in range(2)]
        sc = s.ps("sc", [P, 512])
        sd = s.ps("sd", [P, 512])
        po = [s.ps(f"po{i}", [P, HB, HEAD]) for i in range(2)]

        pooled = s.sem("pooled")
        drained = s.sem("drained")
        g_loaded = s.sem("g_loaded")
        zeroed = s.sem("zeroed")
        masks_ready = s.sem("masks_ready")
        dve_step = s.sem("dve_step")
        summed = s.sem("summed")
        rooted = s.sem("rooted")
        normed = s.sem("normed")
        turned = s.sem("turned")
        copied = s.sem("copied")
        qpad_ready = s.sem("qpad_ready")
        p_scored, p_centred, p_exped, p_ready = (s.sem(n) for n in ("p_scored", "p_centred", "p_exped", "p_ready"))
        p_turned, p_copied, p_summed, p_out = (s.sem(n) for n in ("p_turned", "p_copied", "p_summed", "p_out"))
        p_stored = s.sems("p_stored", 2)
        d_scored, d_maxed, d_exped, d_ready = (s.sem(n) for n in ("d_scored", "d_maxed", "d_exped", "d_ready"))
        imp_ready, d_turned, d_copied, d_summed, d_out = (
            s.sem(n) for n in ("imp_ready", "d_turned", "d_copied", "d_summed", "d_out"))
        d_stored = s.sem("d_stored")
        chosen, moved, bias_out = (s.sem(n) for n in ("chosen", "moved", "bias_out"))

        with nc.Block() as block:
            @block.sync
            def _(sp):
                sp.wait_ge(d_out, 1)
                sp.dma_start(d.o_att[SEQ:ROWS, 1536:2048], o[0:NS, 0, :]).then_inc(d_stored, 16)
                for t in range(PT):
                    sp.wait_ge(p_out, t + 1)
                    sp.dma_start(d.o_att[P * t:P * t + P, 1536:2048], o[:, t % 2, :]).then_inc(p_stored[t % 2], 16)
                for i in range(2):
                    sp.wait_ge(p_stored[i], 16 * PT // 2)
                sp.wait_ge(d_stored, 16)

            @block.gpsimd
            def _(pool):
                pool.dma_start(g[:], d.b_qk_g[1, :].partition_broadcast(NBLK)).then_inc(g_loaded, 16)
                pool.memset(qpad[:], 0.0).then_inc(zeroed, 1)
                pool.memset(pdT[:], 0.0).then_inc(zeroed, 1)
                pool.memset(same[:], 0.0).then_inc(zeroed, 1)
                pool.memset(shift[:], 0.0).then_inc(zeroed, 1)
                pool.memset(mul[:], 1.0).then_inc(zeroed, 1)
                pool.wait_ge(zeroed, 5)
                pool.affine_select(out=shift[:], in_=shift[:], compare_op=ALU.not_equal, fill=1.0,
                                   base=32, pattern=[[-1, 176]], channel_multiplier=1).then_inc(masks_ready, 1)
                pool.affine_select(out=mul[:], in_=mul[:], compare_op=ALU.is_ge, fill=0.0, base=-CMP,
                                   pattern=[[P, PT], [-CMP, 8]], channel_multiplier=1).then_inc(masks_ready, 1)
                n = 2
                for h in range(1 - HB, HB):
                    pool.affine_select(out=same[:], in_=same[:], compare_op=ALU.not_equal, fill=1.0,
                                       base=DT * h, pattern=[[-1, P]], channel_multiplier=1).then_inc(masks_ready, 1)
                    n += 1
                    pool.wait_ge(masks_ready, n)
                v = same[:].rearrange("p (b r) -> p b r", b=DB)
                pool.affine_select(out=v, in_=v, compare_op=ALU.is_ge, fill=0.0, base=0,
                                   pattern=[[-16, DB], [0, 16]], channel_multiplier=1).then_inc(masks_ready, 1)
                pool.wait_ge(masks_ready, n + 1)
                pool.affine_select(out=v, in_=v, compare_op=ALU.is_ge, fill=0.0, base=15,
                                   pattern=[[16, DB], [0, 16]], channel_multiplier=-1).then_inc(masks_ready, 1)

            @block.tensor
            def _(pe):
                for p in range(PT):
                    last = pe.matmul(acc[:], k.z[:, 30 - 2 * p:94 - 2 * p], k.rows_p[:, p, T_KC:T_KC + 2 * HEAD],
                                     start=(p == 0), stop=(p == PT - 1))
                last.then_inc(pooled, 1)
                pe.wait_ge(normed, 1)
                for b in range(DB + 1):
                    i = b // 8
                    last = pe.transpose(tp[i][:, NBLK * (b % 8):NBLK * (b % 8) + NBLK], kc[:, b, :],
                                        k.ident[0:NBLK, 0:NBLK])
                last.then_inc(turned, 1)
                pe.wait_ge(copied, 1)
                for t in range(PT):
                    for h in range(HB):
                        c = 8 * (HB * t + h)
                        last = pe.matmul(sc[:, c:c + 8], k.attT[:, X_BQ + h, P * t:P * t + P],
                                         kcT[:, DB, 0:8], start=True, stop=True)
                last.then_inc(p_scored, 1)
                pe.wait_ge(qpad_ready, 1)
                for b in range(DB):
                    last = pe.matmul(sd[:, 0:NBLK], qpad[:, P * b:P * b + P], kcT[:, b, :],
                                     start=(b == 0), stop=(b == DB - 1))
                last.then_inc(d_scored, 1)
                pe.wait_ge(masks_ready, 11)
                pe.wait_ge(d_ready, 1)
                pe.matmul(sd[:, 128:128 + NBLK], same[:], pd[:], start=True, stop=True).then_inc(imp_ready, 1)
                pe.transpose(tp[0][0:NBLK, 0:P], pd[:], k.ident[:]).then_inc(d_turned, 1)
                pe.wait_ge(d_copied, 1)
                for h in range(HB):
                    for b in range(DB):
                        last = pe.matmul(po[0][0:NS, h, :], pdT[:, h, NS * b:NS * b + NS], vc[:, b, :],
                                         start=(b == 0), stop=(b == DB - 1))
                last.then_inc(d_summed, 1)
                pe.wait_ge(chosen, 1)
                for b in range(DB):
                    last = pe.matmul(tp[1][0:NBLK, NBLK * b:NBLK * b + NBLK], shift[:, 16 * b:16 * b + 64],
                                     imp[:, 2, :], start=True, stop=True)
                last.then_inc(moved, 1)
                pe.wait_ge(p_ready, 1)
                for t in range(PT):
                    if t == 0:
                        pe.wait_ge(d_copied, 1)
                    else:
                        pe.wait_ge(p_copied, t)
                    for h in range(HB):
                        last = pe.transpose(tp[0][0:8, P * h:P * h + P], pc[:, HB * t + h, :], k.ident[:])
                    last.then_inc(p_turned, 1)
                    pe.wait_ge(p_copied, t + 1)
                    pe.wait_ge(p_out, t) if t >= 1 else pe.wait_ge(d_out, 1)
                    for h in range(HB):
                        last = pe.matmul(po[t % 2][:, h, :], pcT[:, t, h, :], vc[0:8, DB, :], start=True, stop=True)
                    last.then_inc(p_summed, 1)

            @block.scalar
            def _(act):
                for h in range(2):
                    for a, v in ((0, kc), (1, vc)):
                        act.activation(v[32 * h:32 * h + 32, 0:DB, :], k.pkv[:, h:2 * DB:2, HEAD * a:HEAD * a + HEAD],
                                       ACT.Copy).then_inc(drained, 1)
                act.wait_ge(pooled, 1)
                act.activation(kc[0:32, DB, :], acc[0:32, 0:HEAD], ACT.Copy).then_inc(drained, 1)
                act.activation(vc[0:32, DB, :], acc[32:64, HEAD:2 * HEAD], ACT.Copy).then_inc(drained, 1)
                act.wait_ge(summed, 1)
                act.activation(ss[:, 1, :], ss[:, 0, :], ACT.Sqrt, bias=k.eps[0:NBLK, :],
                               scale=1.0 / HEAD).then_inc(rooted, 1)
                act.wait_ge(p_centred, 1)
                act.activation(pc[:], pc[:], ACT.Exp).then_inc(p_exped, 1)
                act.wait_ge(d_maxed, 1)
                act.activation(pd[:], sd[:, 0:NBLK], ACT.Exp, bias=st[:, 4, 0:1],
                               accum_out=st[:, 5, 0:1]).then_inc(d_exped, 1)

            @block.vector
            def _(dve):
                step = Chain(dve, dve_step)
                step(dve.memset(kc[32:64, DB, :], 0.0))
                step(dve.memset(k.selb[0:32, :, :], 0.0))
                step(dve.memset(k.selb[32:64, :, :], NEG))
                dve.wait_ge(zeroed, 5)
                dve.tensor_copy(qpad[:].rearrange("p (b x) -> p b x", x=144)[:, :, 0:16].rearrange(
                    "p b (h t) -> p b h t", h=HB),
                    k.attT[:, X_BQ:X_BQ + HB, SEQ:ROWS].rearrange("p h (b t) -> p b h t", b=DB)).then_inc(qpad_ready, 1)
                dve.wait_ge(masks_ready, 2)
                step(dve.tensor_scalar(bias[:], mul[:], -1.0, -NEG, ALU.add, ALU.mult))
                dve.wait_ge(g_loaded, 16)
                dve.wait_ge(drained, 6)
                step(dve.tensor_tensor(sq[:], kc[:], kc[:], ALU.mult))
                dve.tensor_reduce(ss[:, 0, :], sq[:], AX_X, ALU.add).then_inc(summed, 1)
                dve.wait_ge(rooted, 1)
                step(dve.reciprocal(ss[:, 2, :], ss[:, 1, :]))
                step(dve.tensor_tensor(kc[:], kc[:], ss[:, 2, :].unsqueeze(2).broadcast_to(
                    [NBLK, DB + 1, HEAD]), ALU.mult))
                dve.tensor_tensor(kc[:], kc[:], g[:].unsqueeze(1).broadcast_to([NBLK, DB + 1, HEAD]),
                                  ALU.mult).then_inc(normed, 1)
                dve.wait_ge(turned, 1)
                step(dve.tensor_copy(kcT[:, 0:8, :], tp[0][:].rearrange("p (b n) -> p b n", b=8)))
                dve.tensor_copy(kcT[:, 8, :], tp[1][:, 0:NBLK]).then_inc(copied, 1)
                dve.wait_ge(p_scored, 1)
                step(dve.tensor_tensor(pc[:].rearrange("p (t h) n -> p t h n", t=PT),
                                       sc[:, 0:128].rearrange("p (t h n) -> p t h n", t=PT, h=HB),
                                       bias[:].unsqueeze(2).broadcast_to([P, PT, HB, 8]), ALU.add))
                step(dve.tensor_reduce(st[:, 0, :], pc[:], AX_X, ALU.max))
                dve.tensor_tensor(pc[:], pc[:], st[:, 0, :].unsqueeze(2).broadcast_to([P, 16, 8]),
                                  ALU.subtract).then_inc(p_centred, 1)
                dve.wait_ge(d_scored, 1)
                dve.tensor_reduce(st[:, 4, 0:1], sd[:, 0:NBLK], AX_X, ALU.max, negate=True).then_inc(d_maxed, 1)
                dve.wait_ge(p_exped, 1)
                step(dve.tensor_tensor(pc[:].rearrange("p (t h) n -> p t h n", t=PT),
                                       pc[:].rearrange("p (t h) n -> p t h n", t=PT),
                                       mul[:].unsqueeze(2).broadcast_to([P, PT, HB, 8]), ALU.mult))
                step(dve.tensor_reduce(st[:, 1, :], pc[:], AX_X, ALU.add))
                step(dve.tensor_scalar(st[:, 2, :], st[:, 1, :], 1e-30, None, ALU.max))
                step(dve.reciprocal(st[:, 3, :], st[:, 2, :]))
                dve.tensor_tensor(pc[:], pc[:], st[:, 3, :].unsqueeze(2).broadcast_to([P, 16, 8]),
                                  ALU.mult).then_inc(p_ready, 1)
                dve.wait_ge(d_exped, 1)
                step(dve.reciprocal(st[:, 6, 0:1], st[:, 5, 0:1]))
                dve.tensor_scalar(pd[:], pd[:], st[:, 6, 0:1], None, ALU.mult).then_inc(d_ready, 1)
                dve.wait_ge(imp_ready, 1)
                dve.wait_ge(d_turned, 1)
                step(dve.tensor_copy(imp[:, 0, :], sd[:, 128:128 + NBLK]))
                dve.tensor_copy(pdT[:, :, :].rearrange("p h (b x) -> p h b x", x=36)[:, :, :, 0:DT],
                                tp[0][0:NBLK, 0:P].rearrange("p (b h t) -> p h b t", b=DB, h=HB)).then_inc(d_copied, 1)
                step(dve.max(top[:, 0, :], imp[:, 0, :]))
                step(dve.match_replace(imp[:, 1, :], top[:, 0, :], imp[:, 0, :], -1.0))
                step(dve.max(top[:, 1, :], imp[:, 1, :]))
                step(dve.match_replace(imp[:, 0, :], top[:, 1, :], imp[:, 1, :], -1.0))
                dve.tensor_scalar(imp[:, 2, :], imp[:, 0, :], 0.0, NEG, ALU.is_ge, ALU.mult).then_inc(chosen, 1)
                dve.wait_ge(d_summed, 1)
                dve.tensor_copy(o[0:NS, 0, :].rearrange("p (h w) -> p h w", h=HB), po[0][0:NS, :, :]).then_inc(d_out, 1)
                dve.wait_ge(moved, 1)
                dve.tensor_copy(k.selb[32:48, :, :], tp[1][32:48, 0:512].rearrange("p (b n) -> p b n", b=DB)) \
                    .then_inc(bias_out, 1)
                dve.wait_ge(bias_out, 1)
                for t in range(PT):
                    dve.wait_ge(p_turned, t + 1)
                    dve.tensor_copy(pcT[:, t, :, :], tp[0][0:8, :].rearrange("p (h r) -> p h r", h=HB)).then_inc(p_copied, 1)
                    dve.wait_ge(p_summed, t + 1)
                    if t == 0:
                        dve.wait_ge(d_stored, 16)
                    elif t >= 2:
                        dve.wait_ge(p_stored[t % 2], 16)
                    dve.tensor_copy(o[:, t % 2, :].rearrange("p (h w) -> p h w", h=HB), po[t % 2][:]).then_inc(p_out, 1)


def decode_attend(nc, d, k):
    NG = PAGES // 4
    WING, NEWG, G = 2, 5, NG + 2
    page_groups = [g for g in range(G) if g not in (WING, NEWG)]
    R = 64
    HEADS = HA + 2
    batches = []
    for g in range(G):
        batches += [(g, HA + 1)] if g == WING else [] if g == NEWG else [(g, j) for j in range(HA + 1)]
    NT = len(batches)
    last_batch = [max(i for i, (x, _) in enumerate(batches) if x < g or x == g != NEWG) for g in range(G)]
    last_batch[NEWG] += 1
    uses = [len(range(r, NT, 3)) for r in range(3)]
    with Stage(nc, "da") as s:
        table = s.sb("table", [1, DB * PAGES], I32)
        pa = s.sb("pa", [P, 4, 4, 1024])
        pb = s.sb("pb", [P, 4, 4, 256])
        pw = s.sb("pw", [P, 4, 256])
        khi = s.sb("khi", [P, 3, 512], F32R)
        klo = s.sb("klo", [P, 3, 512], F32R)
        q = s.sb("q", [P, HEADS * R])
        qs = s.sb("qs", [P, HEADS, 2 * R], F32R)
        low = s.sb("low", [R, 2, 512])
        sb_ = s.sb("scores", [R, 2, 512])
        e = s.sb("e", [R, 2, 512])
        pT = s.sb("pT", [P, 2, 4, HEADS * R])
        winb = s.sb("winb", [R, 512])
        newb = s.sb("newb", [R, DB, NS])
        nm = s.sb("nm", [R, G])
        l = s.sb("l", [R, G])
        wt = s.sb("wt", [R, 4, G])
        st = s.sb("st", [R, 8])
        ob = s.sb("ob", [R, G, HEAD])
        oall = s.sb("oall", [R, DB, HEAD])
        coef = s.sb("coef", [R, 2])
        hot = s.sb("hot", [8, 2, R])
        late = s.sb("late", [8, DB * NS + 8])
        both = s.sb("both", [R, 4 * HA])
        oa = s.sb("oa", [4 * HA, DB, HEAD])
        tp = [s.ps(f"tp{i}", [P, 4, P]) for i in range(3)]
        ps = [s.ps(f"ps{i}", [2 * R, 512]) for i in range(2)]
        pt = s.ps("pt", [P, 4, R])
        po = [s.ps(f"po{i}", [R, HEAD]) for i in range(2)]

        table_loaded = s.sem("table_loaded")
        loaded = s.sems("loaded", 4)
        win_loaded = s.sem("win_loaded")
        win_used = s.sem("win_used")
        zeroed = s.sem("zeroed")
        made = s.sem("made")
        spread = s.sem("spread")
        dve_step = s.sem("dve_step")
        consts_ready = s.sem("consts_ready")
        q_placed = s.sem("q_placed")
        q_high = s.sem("q_high")
        q_ready = s.sem("q_ready")
        low_out = s.sem("low_out")
        turned = s.sem("turned")
        split = s.sem("split")
        copied = s.sems("copied", 3)
        multiplied = s.sem("multiplied")
        scored = s.sem("scored")
        joined = s.sem("joined")
        added = s.sem("added")
        maxed = s.sem("maxed")
        exped = s.sem("exped")
        turning = s.sem("turning")
        p_turned = s.sem("p_turned")
        p_copied = s.sem("p_copied")
        summed = s.sem("summed")
        o_copied = s.sem("o_copied")
        minned = s.sem("minned")
        weighed = s.sem("weighed")
        shared = s.sem("shared")
        combined = s.sem("combined")
        gathered = s.sem("gathered")
        out_ready = s.sem("out_ready")
        stored = s.sem("stored")

        with nc.Block() as block:
            @block.sync
            def _(sp):
                sp.dma_start(table[:], d.page_table.rearrange("(a b) n -> a (b n)", a=1)).then_inc(table_loaded, 16)
                sp.sem_inc(win_used, 1)
                sp.wait_ge(table_loaded, 16)
                with sp.Fori(0, DB) as b:
                    for p in range(NG):
                        sp.wait_ge(summed, b * G + (page_groups[p - 4] + 7 if p >= 4 else page_groups[p + 4] - 3))
                        for i in range(4):
                            page = sp.value_load(table[0:1, bass.ds(b * PAGES + 4 * p + i, 1)],
                                                 min_val=0, max_val=d.cache_b.shape[0] - 1)
                            sp.dma_start(pa[:, p % 4, i, :], d.cache_a[bass.ds(page, 1), :, :]
                                         .rearrange("a p n -> p (a n)")).then_inc(loaded[p % 4], 16)
                            sp.dma_start(pb[:, p % 4, i, :], d.cache_b[bass.ds(page, 1), :, 256:512]
                                         .rearrange("a p n -> p (a n)")).then_inc(loaded[p % 4], 16)
                        if p == 1:
                            sp.wait_ge(win_used, b + 1)
                            sp.dma_start(pw[:], d.b_win[bass.ds(b, 1), :, :].rearrange(
                                "a (i p) n -> p (a i) n", p=P)).then_inc(win_loaded, 16)
                place = d.o_att[SEQ:ROWS, :].rearrange("(b t) n -> t b n", t=DT)
                sp.wait_ge(combined, DB + 1)
                for j in range(2 * HB):
                    sp.dma_start(place[:, :, 512 + HEAD * j:512 + HEAD * j + HEAD],
                                 oall[32 + 4 * j:36 + 4 * j, :, :]).then_inc(stored, 16)
                sp.wait_ge(out_ready, 2)
                for h in range(HA):
                    sp.dma_start(place[:, :, HEAD * h:HEAD * h + HEAD],
                                 oa[4 * h:4 * h + 4, :, :]).then_inc(stored, 16)
                sp.wait_ge(stored, 16 * (2 * HB + HA))

            @block.gpsimd
            def _(pool):
                for v in (q, pT, winb, hot, late, both):
                    pool.memset(v[:], 0.0).then_inc(zeroed, 1)
                pool.wait_ge(zeroed, 6)
                pool.affine_select(out=winb[:], in_=winb[:], compare_op=ALU.is_ge, fill=NEG, base=-48,
                                   pattern=[[0, 512]], channel_multiplier=1).then_inc(made, 1)
                pool.affine_select(out=hot[0:4, 0, :].rearrange("p (a t) -> p a t", t=4),
                                   in_=hot[0:4, 0, :].rearrange("p (a t) -> p a t", t=4),
                                   compare_op=ALU.not_equal, fill=1.0, base=0, pattern=[[0, 16], [-1, 4]],
                                   channel_multiplier=1).then_inc(made, 1)
                pool.affine_select(out=hot[:, 1, 0:32].rearrange("p (a t) -> p a t", t=8),
                                   in_=hot[:, 1, 0:32].rearrange("p (a t) -> p a t", t=8),
                                   compare_op=ALU.not_equal, fill=1.0, base=0, pattern=[[0, 4], [-1, 8]],
                                   channel_multiplier=1).then_inc(made, 1)
                v = late[0:4, 0:DB * NS].rearrange("p (b n) -> p b n", b=DB)
                pool.affine_select(out=v, in_=v, compare_op=ALU.is_ge, fill=NEG, base=0,
                                   pattern=[[4, DB], [-1, NS]], channel_multiplier=1).then_inc(made, 1)
                pool.wait_ge(made, 4)
                pool.affine_select(out=v, in_=v, compare_op=ALU.is_ge, fill=NEG, base=0,
                                   pattern=[[-4, DB], [1, NS]], channel_multiplier=0).then_inc(made, 1)
                v = late[0:4, DB * NS:DB * NS + 4]
                pool.affine_select(out=v, in_=v, compare_op=ALU.is_gt, fill=NEG, base=0,
                                   pattern=[[1, 4]], channel_multiplier=-1).then_inc(made, 1)
                v = late[:, DB * NS + 4:DB * NS + 5]
                pool.affine_select(out=v, in_=v, compare_op=ALU.is_gt, fill=1.0, base=4,
                                   pattern=[[0, 1]], channel_multiplier=-1).then_inc(made, 1)
                v = both[:].rearrange("p (h t) -> p h t", t=4)
                for c in range(2):
                    pool.affine_select(out=v, in_=v, compare_op=ALU.not_equal, fill=1.0, base=-4 * c,
                                       pattern=[[-8, HA], [-1, 4]], channel_multiplier=1).then_inc(made, 1)
                    pool.wait_ge(made, 8 + c)

            @block.tensor
            def _(pe):
                def turn(b, i):
                    g, j = batches[i]
                    if j == 0:
                        p = page_groups.index(g)
                        pe.wait_ge(loaded[p % 4], b * 256 + 128 * (p // 4) + 128)
                    if g == WING:
                        pe.wait_ge(win_loaded, b * 16 + 16)
                    pe.wait_ge(copied[i % 3], b * uses[i % 3] + i // 3 + 1)
                    for c in range(4):
                        src = (pw[:, c, 0:HEAD] if g == WING else
                               pa[:, page_groups.index(g) % 4, c, HEAD * j:HEAD * j + HEAD] if j < HA else
                               pb[:, page_groups.index(g) % 4, c, 0:HEAD])
                        last = pe.transpose(tp[i % 3][:, c, :], src, k.ident[:])
                    last.then_inc(turned, 1)

                def multiply(b, i):
                    g, j = batches[i]
                    first = j == 0 or g == WING
                    if i == 0:
                        pe.wait_ge(q_ready, b + 1)
                    if first:
                        pe.wait_ge(added, b * G + g + 1)
                    pe.wait_ge(copied[i % 3], b * uses[i % 3] + i // 3 + 2)
                    pe.matmul(ps[g % 2][:], qs[:, j, :], khi[:, i % 3, :], start=first, stop=False)
                    last = pe.matmul(ps[g % 2][:], qs[:, j, :], klo[:, i % 3, :], start=False,
                                     stop=j == HA or g == WING)
                    last.then_inc(multiplied, 1)
                    if j == HA or g == WING:
                        pe.wait_ge(multiplied, b * NT + i + 4)
                        pe.sem_inc(scored, 1)

                def attend(b, g):
                    n = NS if g == NEWG else P
                    pe.wait_ge(exped, b * G + g + 3)
                    pe.wait_ge(p_copied, b * G + g + 1)
                    pe.sem_inc(turning, 1)
                    for c in range(1 if g == NEWG else 4):
                        last = pe.transpose(pt[0:n, c, :], e[:, g % 2, P * c:P * c + n], k.ident[0:R, 0:R])
                    last.then_inc(p_turned, 1)

                def values(b, g):
                    n = NS if g == NEWG else P
                    pe.wait_ge(p_copied, b * G + g + 2)
                    pe.wait_ge(o_copied, b * G + g + 1)
                    new = [k.rows_s[:, T_AV + HEAD * j:T_AV + HEAD * j + HEAD] for j in range(HA)] \
                        + [k.rows_s[:, T_VS:T_VS + HEAD], k.rows_s[:, T_VW:T_VW + HEAD]]
                    todo = []
                    if g in page_groups:
                        p = page_groups.index(g)
                        for c in range(4):
                            todo += [(c, j, pa[:, p % 4, c, 512 + HEAD * j:512 + HEAD * j + HEAD]) for j in range(HA)]
                            todo.append((c, HA, pb[:, p % 4, c, HEAD:2 * HEAD]))
                    elif g == WING:
                        todo = [(c, HA + 1, pw[:, c, HEAD:2 * HEAD]) for c in range(4)]
                    else:
                        todo = [(0, j, new[j]) for j in range(HEADS)]
                    for x, (c, j, v) in enumerate(todo):
                        last = pe.matmul(po[g % 2][:], pT[0:n, g % 2, c, R * j:R * j + R], v, start=(x == 0),
                                         stop=(x == len(todo) - 1))
                    last.then_inc(summed, 1)
                    if g == WING:
                        pe.wait_ge(summed, b * G + g + 7)
                        pe.sem_inc(win_used, 1)

                pe.wait_ge(made, 9)
                pe.matmul(ps[0][0:R, 0:DB * NS + 4], hot[0:4, 0, :], late[0:4, 0:DB * NS + 4], start=True, stop=True)
                pe.matmul(ps[1][0:R, 0:1], hot[:, 1, :], late[:, DB * NS + 4:DB * NS + 5], start=True,
                          stop=True).then_inc(spread, 1)
                pe.wait_ge(consts_ready, 1)
                pe.sem_inc(multiplied, 3)
                pe.sem_inc(scored, 1)
                pe.sem_inc(p_turned, 2)
                pe.sem_inc(summed, 6)
                new_keys = [X_AK + j for j in range(HA)] + [X_KS, X_KW]

                def new_scores(b):
                    pe.wait_ge(added, b * G + NEWG + 1)
                    for j in range(HEADS):
                        last = pe.matmul(ps[NEWG % 2][0:R, 0:NS], q[:, R * j:R * j + R],
                                         k.attT[:, new_keys[j], SEQ:ROWS], start=(j == 0), stop=(j == HEADS - 1))
                    last.then_inc(scored, 1)

                def due(b, n):
                    for g in range(G):
                        if n == last_batch[g] + 4:
                            attend(b, g)
                        if n == last_batch[g] + 6:
                            values(b, g)
                    if n == last_batch[NEWG] - 1:
                        new_scores(b)

                def sequence(b, before):
                    for n in range(NT):
                        turn(b, n)
                        if n < 2:
                            if before is not None:
                                multiply(before, NT + n - 2)
                        else:
                            multiply(b, n - 2)
                        if before is not None:
                            due(before, NT + n - 2)
                        if n >= 2:
                            due(b, n - 2)

                sequence(0, None)
                with pe.Fori(0, DB - 1) as b:
                    sequence(b + 1, b)
                for n in range(NT - 2, NT + 6):
                    if n < NT:
                        multiply(DB - 1, n)
                    due(DB - 1, n)
                pe.wait_ge(combined, DB + 1)
                for x in range(2):
                    pe.matmul(tp[x][0:4 * HA, :, :], both[:], oall[:, 4 * x:4 * x + 4, :], start=True,
                              stop=True).then_inc(gathered, 1)

            @block.scalar
            def _(act):
                act.wait_ge(consts_ready, 1)
                act.sem_inc(exped, 2)
                act.sem_inc(o_copied, 2)

                def high(b, i):
                    act.wait_ge(turned, b * NT + i + 1)
                    act.wait_ge(multiplied, b * NT + (2, 3, 3)[i] if i < 3 else b * NT + i + 1)
                    act.activation(khi[:, i % 3, :].rearrange("p (c n) -> p c n", c=4), tp[i % 3][:],
                                   ACT.Copy).then_inc(split, 1)

                def low_scores(b, g):
                    act.wait_ge(scored, b * G + g + 2)
                    act.wait_ge(added, b * G + g + 1)
                    act.activation(low[:, g % 2, :], ps[g % 2][R:2 * R, :], ACT.Copy).then_inc(low_out, 1)

                def softmax(b, g):
                    n = NS if g == NEWG else 512
                    act.wait_ge(maxed, b * G + g + 1)
                    act.wait_ge(p_turned, b * G + g + 1)
                    if g == 0:
                        act.wait_ge(shared, b + 1)
                    act.activation(e[:, g % 2, 0:n], sb_[:, g % 2, 0:n], ACT.Exp, bias=nm[:, g:g + 1],
                                   accum_out=l[:, g:g + 1]).then_inc(exped, 1)

                def out(b, g):
                    act.wait_ge(summed, b * G + g + 7)
                    if g == 0:
                        act.wait_ge(combined, b + 1)
                    act.activation(ob[:, g, :], po[g % 2][:], ACT.Copy).then_inc(o_copied, 1)

                def due(b, n):
                    for g in range(G):
                        if n == last_batch[g] + 2 and g != NEWG:
                            low_scores(b, g)
                        if n == last_batch[g] + 8:
                            out(b, g)
                        if n == last_batch[g] + 4:
                            softmax(b, g)
                    if n == NT + 4:
                        act.wait_ge(minned, b + 1)
                        act.activation(wt[:, 0, :], nm[:], ACT.Exp, bias=st[:, 0:1], scale=-1.0).then_inc(weighed, 1)

                def sequence(b, before):
                    for n in range(NT):
                        high(b, n)
                        if before is not None:
                            due(before, NT + n)
                        due(b, n)

                sequence(0, None)
                with act.Fori(0, DB - 1) as b:
                    sequence(b + 1, b)
                for n in range(NT, NT + 8):
                    due(DB - 1, n)

            @block.vector
            def _(dve):
                step = Chain(dve, dve_step)
                dve.wait_ge(spread, 1)
                dve.wait_ge(made, 9)
                step(dve.tensor_copy(newb[:].rearrange("p b n -> p (b n)"), ps[0][0:R, 0:DB * NS]))
                step(dve.tensor_tensor(winb[:, 0:4], winb[:, 0:4], ps[0][0:R, DB * NS:DB * NS + 4], ALU.add))
                step(dve.tensor_copy(coef[:, 1:2], ps[1][0:R, 0:1]))
                step(dve.tensor_scalar(coef[:, 0:1], k.neglam[0:R, :], -1.0, None, ALU.add))
                step(dve.tensor_tensor(coef[:, 0:1], coef[:, 0:1], coef[:, 1:2], ALU.mult))
                step(dve.tensor_scalar(coef[:, 0:1], coef[:, 0:1], 1.0, None, ALU.add))
                for r in range(3):
                    dve.sem_inc(copied[r], 1)
                dve.sem_inc(added, 2)
                dve.sem_inc(p_copied, 1)
                dve.sem_inc(combined, 1)
                dve.sem_inc(shared, 1)
                dve.sem_inc(consts_ready, 1)
                own = step.n

                def queries(b):
                    dve.wait_ge(scored, b * G + 1)
                    A = q[:, 0:288].rearrange("p (h x) -> p h x", x=72)
                    for c in range(2):
                        dve.tensor_copy(A[DC * c:DC * c + DC, :, 4 * c:4 * c + 4],
                                        k.attT[DC * c:DC * c + DC, X_AQ:X_AQ + HA, bass.ds(b * DT + SEQ, DT)])
                    for x in (288, 368):
                        last = dve.tensor_copy(q[:, x:x + 16].rearrange("p (h t) -> p h t", h=HB),
                                               k.attT[:, X_BQ:X_BQ + HB, bass.ds(b * DT + SEQ, DT)])
                    last.then_inc(q_placed, 1)
                    dve.wait_ge(q_placed, b + 1)
                    v = q[:].rearrange("p (j r) -> p j r", j=HEADS)
                    dve.tensor_copy(qs[:, :, 0:R], v).then_inc(q_high, 1)
                    dve.wait_ge(q_high, b + 1)
                    dve.tensor_tensor(qs[:, :, R:2 * R], v, qs[:, :, 0:R], ALU.subtract).then_inc(q_ready, 1)

                def low_part(b, i):
                    dve.wait_ge(split, b * NT + i + 1)
                    dve.tensor_tensor(klo[:, i % 3, :].rearrange("p (c n) -> p c n", c=4), tp[i % 3][:],
                                      khi[:, i % 3, :].rearrange("p (c n) -> p c n", c=4),
                                      ALU.subtract).then_inc(copied[i % 3], 1)

                def row_max(b, g):
                    dve.wait_ge(scored, b * G + g + 2)
                    dve.wait_ge(exped, b * G + g + 1)
                    if g != NEWG:
                        dve.wait_ge(low_out, b * (G - 1) + g + (g < NEWG))
                        dve.tensor_tensor(sb_[:, g % 2, :], ps[g % 2][0:R, :], low[:, g % 2, :],
                                          ALU.add).then_inc(joined, 1)
                        dve.wait_ge(joined, b * (G - 1) + g + (g < NEWG))
                    if g in page_groups:
                        v = sb_[:, g % 2, :].rearrange("p (n r) -> p n r", n=8)
                        n = 8 * page_groups.index(g)
                        dve.tensor_tensor(v, v, k.selb[:, bass.ds(b, 1), n:n + 8].rearrange(
                            "p a n -> p (a n)").unsqueeze(2).broadcast_to([R, 8, CMP]), ALU.add).then_inc(added, 1)
                    elif g == WING:
                        dve.tensor_tensor(sb_[:, g % 2, :], sb_[:, g % 2, :], winb[:], ALU.add).then_inc(added, 1)
                    else:
                        dve.tensor_tensor(sb_[:, g % 2, 0:NS], ps[g % 2][0:R, 0:NS],
                                          newb[:, bass.ds(b, 1), :].rearrange("p a n -> p (a n)"),
                                          ALU.add).then_inc(added, 1)
                    n = NS if g == NEWG else 512
                    dve.wait_ge(added, b * G + g + 3)
                    dve.tensor_reduce(nm[:, g:g + 1], sb_[:, g % 2, 0:n], AX_X, ALU.max,
                                      negate=True).then_inc(maxed, 1)

                def weights(b, g):
                    dve.wait_ge(p_turned, b * G + g + 3)
                    dve.wait_ge(summed, b * G + g + 5)
                    n, c = (NS, 1) if g == NEWG else (P, 4)
                    if g != WING:
                        dve.tensor_copy(pT[0:n, g % 2, 0:c, 0:288].rearrange("p c (h x) -> p c h x", x=72)[:, :, :, 0:8],
                                        pt[0:n, 0:c, 0:32].rearrange("p c (h x) -> p c h x", h=HA))
                        last = dve.tensor_copy(pT[0:n, g % 2, 0:c, 288:304], pt[0:n, 0:c, 32:48])
                    if g in (WING, NEWG):
                        last = dve.tensor_copy(pT[0:n, g % 2, 0:c, 368:384], pt[0:n, 0:c, 48:64])
                    last.then_inc(p_copied, 1)

                def then(b, n, ins):
                    ins.then_inc(dve_step, 1)
                    dve.wait_ge(dve_step, b * 6 + own + n)

                def due(b, n):
                    for g in range(G):
                        if n == last_batch[g] + 6:
                            weights(b, g)
                        if n == last_batch[g] + 2:
                            row_max(b, g)
                    if n == NT + 2:
                        dve.wait_ge(maxed, b * G + G)
                        dve.tensor_reduce(st[:, 0:1], nm[:], AX_X, ALU.min).then_inc(minned, 1)
                    if n == NT + 5:
                        dve.wait_ge(weighed, b + 1)
                        dve.wait_ge(exped, b * G + G + 2)
                        then(b, 1, dve.tensor_tensor(wt[:, 1, :], wt[:, 0, :], l[:], ALU.mult))
                        then(b, 2, dve.tensor_reduce(st[:, 1:2], wt[:, 1, :], AX_X, ALU.add))
                        then(b, 3, dve.reciprocal(st[:, 2:3], st[:, 1:2]))
                        then(b, 4, dve.tensor_scalar(wt[:, 2, :], wt[:, 0, :], st[:, 2:3], coef[:, 0:1],
                                                     ALU.mult, ALU.mult))
                        dve.sem_inc(shared, 1)
                    if n == NT + 8:
                        dve.wait_ge(o_copied, b * G + G + 2)
                        then(b, 5, dve.tensor_tensor(ob[:], ob[:], wt[:, 2, :].unsqueeze(2).broadcast_to(
                            [R, G, HEAD]), ALU.mult))
                        then(b, 6, dve.tensor_reduce(oall[:, bass.ds(b, 1), :].rearrange("p a n -> p (a n)"),
                                                     ob[:].rearrange("p g n -> p n g"), AX_X, ALU.add))
                        dve.sem_inc(combined, 1)

                def sequence(b, before):
                    for n in range(NT):
                        low_part(b, n)
                        if n == 0:
                            queries(b)
                        if before is not None:
                            due(before, NT + n)
                        due(b, n)

                sequence(0, None)
                with dve.Fori(0, DB - 1) as b:
                    sequence(b + 1, b)
                for n in range(NT, NT + 9):
                    due(DB - 1, n)
                for x in range(2):
                    dve.wait_ge(gathered, x + 1)
                    dve.tensor_copy(oa[:, 4 * x:4 * x + 4, :], tp[x][0:4 * HA, :, :]).then_inc(out_ready, 1)


def convolve(nc, d, k):
    with Stage(nc, "cv") as s:
        x = s.sb("x", [P, 5, QKC])
        w = s.sb("w", [5, QKC])
        old = s.sb("old", [3 * DB, QKC])
        wT = s.sb("wT", [P, 8, 5])
        xp = s.sb("xp", [P, 8, SEQ + 3])
        xs = s.sb("xs", [P, 8, DB, DT + 3])
        sig = s.sb("sig", [P, 8, ROWS])
        gin = s.sb("gin", [P, 5, 2 * HC])
        gbias = s.sb("gbias", [HC, 2])
        t0 = s.sb("t0", [HC, ROWS])
        t1 = s.sb("t1", [HC, ROWS])
        tp = [s.ps(f"tp{i}", [P, 4, P]) for i in range(4)]
        gi = [s.ps(f"gi{i}", [HC, 512]) for i in range(4)]
        x_loaded = s.sems("x_loaded", 5)
        w_loaded = s.sem("w_loaded")
        g_loaded = s.sem("g_loaded")
        zeroed = s.sem("zeroed")
        turned = s.sem("turned")
        copied = s.sem("copied")
        g_turned = s.sem("g_turned")
        conv_done = s.sem("conv_done")
        sig_done = s.sem("sig_done")
        silu_done = s.sem("silu_done")
        f_ready = s.sem("f_ready")
        f_exped = s.sem("f_exped")
        f_logged = s.sem("f_logged")
        k_turned = s.sem("k_turned")
        k_copied = s.sem("k_copied")
        dve_step = s.sem("dve_step")
        stored = s.sem("stored")
        CQ = C_CQK
        jobs = [("w", 0, h) for h in range(2)] + [("old", 0, h) for h in range(2)] \
            + [("x", t, h) for t in range(5) for h in range(2)]

        with nc.Block() as block:
            @block.sync
            def _(sp):
                sp.dma_start(w[0:4, :], d.c_conv_w).then_inc(w_loaded, 16)
                sp.dma_start(w[4:5, :], d.c_conv_b.unsqueeze(0)).then_inc(w_loaded, 16)
                sp.dma_start(old[:], d.c_conv.rearrange("b t n -> (b t) n")).then_inc(w_loaded, 16)
                for t, (r0, rows) in enumerate(TILES):
                    sp.dma_start(x[0:rows, t, :], d.proj[r0:r0 + rows, CQ:CQ + QKC]).then_inc(x_loaded[t], 16)
                for t, (r0, rows) in enumerate(TILES):
                    sp.dma_start(gin[0:rows, t, :], d.proj[r0:r0 + rows, C_CIF:C_CIF + 2 * HC]).then_inc(g_loaded, 16)
                sp.dma_start(gbias[:], d.c_gate_b.rearrange("a h -> h a"), allow_slow_non_contiguous=True).then_inc(g_loaded, 16)
                sp.dma_start(d.conv_p, d.proj[SEQ - 3:SEQ, CQ:CQ + QKC]).then_inc(stored, 16)
                for b in range(DB):
                    r = SEQ + DT * b
                    sp.dma_start(d.conv_s[b], d.proj[r + 1:r + DT, CQ:CQ + QKC]).then_inc(stored, 16)
                sp.wait_ge(stored, 16 * (DB + 1))

            @block.tensor
            def _(pe):
                for n, (what, t, h) in enumerate(jobs):
                    if what == "w":
                        pe.wait_ge(w_loaded, 48)
                        src, rows = w, 5
                    elif what == "old":
                        src, rows = old, 3 * DB
                    else:
                        pe.wait_ge(x_loaded[t], 16)
                        src, rows = x[:, t, :], TILES[t][1]
                    if n >= 2:
                        pe.wait_ge(copied, n - 1)
                    for c in range(4):
                        col = P * (4 * h + c)
                        last = pe.transpose(tp[n % 2][:, c, 0:rows], src[0:rows, col:col + P], k.ident[0:rows, 0:rows])
                    last.then_inc(turned, 1)
                pe.wait_ge(g_loaded, 96)
                for t, (r0, rows) in enumerate(TILES):
                    for a in range(2):
                        out = gi[a][:, r0:r0 + rows] if t < PT else gi[2 + a][:, 0:rows]
                        last = pe.transpose(out, gin[0:rows, t, HC * a:HC * a + HC], k.ident[0:rows, 0:rows])
                last.then_inc(g_turned, 1)
                pe.wait_ge(silu_done, 1)
                for t, (r0, rows) in enumerate(TILES):
                    if t >= 2:
                        pe.wait_ge(k_copied, t - 1)
                    for c in range(4):
                        last = pe.transpose(tp[2 + t % 2][0:rows, c, :], k.qkT[:, 4 + c, r0:r0 + rows], k.ident[:])
                    last.then_inc(k_turned, 1)

            @block.scalar
            def _(act):
                act.wait_ge(f_ready, 1)
                act.activation(t1[:], t0[:], ACT.Exp).then_inc(f_exped, 1)
                act.wait_ge(f_exped, 1)
                act.activation(t1[:], t1[:], ACT.Ln, bias=1.0).then_inc(f_logged, 1)
                act.wait_ge(conv_done, 1)
                act.activation(sig[:], k.qkT[:], ACT.Sigmoid).then_inc(sig_done, 1)

            @block.vector
            def _(dve):
                step = Chain(dve, dve_step)
                step(dve.memset(xp[:, :, 0:3], 0.0))
                for n, (what, t, h) in enumerate(jobs):
                    dve.wait_ge(turned, n + 1)
                    c = slice(4 * h, 4 * h + 4)
                    if what == "w":
                        last = dve.tensor_copy(wT[:, c, :], tp[n % 2][:, :, 0:5])
                    elif what == "old":
                        last = dve.tensor_copy(xs[:, c, :, 0:3], tp[n % 2][:, :, 0:3 * DB].rearrange(
                            "p c (b t) -> p c b t", b=DB))
                    elif t < PT:
                        last = dve.tensor_copy(xp[:, c, 3 + P * t:3 + P * t + P], tp[n % 2][:])
                    else:
                        last = dve.tensor_copy(xs[:, c, :, 3:3 + DT], tp[n % 2][:, :, 0:NS].rearrange(
                            "p c (b t) -> p c b t", b=DB))
                    last.then_inc(copied, 1)
                dve.wait_ge(g_turned, 1)
                for a, dst in ((0, k.gate_i), (1, k.gate_f)):
                    for src, r0, n in ((gi[a], 0, SEQ), (gi[2 + a], SEQ, NS)):
                        step(dve.tensor_scalar(dst[:, r0:r0 + n], src[:, 0:n], gbias[:, a:a + 1], None, ALU.add))
                dve.scalar_tensor_tensor(t0[:], k.gate_f[:], -1.0, k.gate_f[:], ALU.mult, ALU.min).then_inc(f_ready, 1)
                dve.wait_ge(f_logged, 1)
                step(dve.tensor_scalar(k.gate_f[:], k.gate_f[:], 0.0, None, ALU.min))
                step(dve.tensor_tensor(k.gate_f[:], k.gate_f[:], t1[:], ALU.subtract))
                dve.wait_ge(copied, len(jobs))
                for j in range(4):
                    for c in range(8):
                        outs = ((k.qkT[:, c, 0:SEQ], xp[:, c, j:j + SEQ]),
                                (k.qkT[:, c, SEQ:ROWS].rearrange("p (b t) -> p b t", b=DB), xs[:, c, :, j:j + DT]))
                        for out, src in outs:
                            if j == 0:
                                last = dve.tensor_scalar(out, src, wT[:, c, 0:1], wT[:, c, 4:5], ALU.mult, ALU.add)
                            else:
                                last = dve.scalar_tensor_tensor(out, src, wT[:, c, j:j + 1], out, ALU.mult, ALU.add)
                    if j < 3:
                        step(last)
                last.then_inc(conv_done, 1)
                dve.wait_ge(sig_done, 1)
                step(dve.tensor_tensor(k.qkT[:], k.qkT[:], sig[:], ALU.mult))
                dve.tensor_scalar(k.qkT[:, 0:4, :], k.qkT[:, 0:4, :], DC ** -0.5, None, ALU.mult).then_inc(silu_done, 1)
                for t, (r0, rows) in enumerate(TILES):
                    dve.wait_ge(k_turned, t + 1)
                    dve.tensor_copy(k.k_rows[0:rows, t, :].rearrange("p (c n) -> p c n", c=4),
                                    tp[2 + t % 2][0:rows, :, :]).then_inc(k_copied, 1)
                dve.wait_ge(k_copied, 5)


def mlstm(nc, d, k, decode):
    NC, n, tile0 = (1, NS, PT) if decode else (PT, P, 0)
    NB, L = (DB, DT) if decode else (1, P)
    V = HEAD + 1
    with Stage(nc, "md" if decode else "mp") as s:
        v = s.sb("v", [P, NC, HC, V])
        ones = s.sb("ones8", [HC, P])
        m = s.sb("m", [HC, NB])
        b = s.sb("b", [HC, NC, n])
        row = s.sb("row", [HC, NC, 4, n])
        nca = s.sb("nca", [HC, NC, n])
        mt = s.sb("mt", [HC, NC, n])
        cs = s.sb("cs", [HC, NC, NB])
        diag = s.sb("diag", [HC, NC, HC, NB])
        pick = s.sb("pick", [HC, HC, P])
        mask = s.sb("mask", [n, n])
        col = s.sb("col", [P, NC, 4, HC])
        w = s.sb("w", [P, 4, n])
        qk = s.sb("qk", [P, 4, n])
        kw = s.sb("kw", [P, NC, HC, DC])
        inter = s.sb("inter", [P, 4, V])
        num = s.sb("num", [P, 4, V])
        den = s.sb("den", [P, 4, 4])
        h_out = s.sb("h_out", [P, 2, HC, HEAD])
        S = s.sb("S", [P, DB if decode else 1, 4, V])
        csb = s.sb("csb", [P, NC, HC, NB])
        sc = [s.ps(f"sc{i}", [P, 2, P]) for i in range(2)]
        small = sc[1][:, 0, 0:4 * HC].rearrange("p (x h) -> p x h", x=4)
        dd = s.ps("dd", [P, 4, n])
        pn = [s.ps(f"pn{i}", [P, 2, V]) for i in range(2)]
        pi = [s.ps(f"pi{i}", [P, 2, V]) for i in range(2)]
        pu = s.ps("pu", [P, 512])

        loaded = s.sem("loaded")
        st_loaded = s.sem("st_loaded")
        zeroed = s.sem("zeroed")
        made = s.sem("made")
        dve_step = s.sem("dve_step")
        rows_ready = s.sem("rows_ready")
        cs_exped = s.sem("cs_exped")
        diag_ready = s.sem("diag_ready")
        r_turned = s.sem("r_turned")
        r_copied = s.sem("r_copied")
        col_exped = s.sem("col_exped")
        cs_spread = s.sem("cs_spread")
        csb_ready = s.sem("csb_ready")
        kw_ready = s.sem("kw_ready")
        scored = s.sem("scored")
        exped = s.sem("exped")
        weighed = s.sem("weighed")
        summed = s.sem("summed")
        in_copied = s.sem("in_copied")
        state_ready = s.sem("state_ready")
        taken = s.sem("taken")
        h_ready = s.sem("h_ready")
        h_stored = s.sems("h_stored", 2)
        turned = s.sem("turned")
        copied = s.sem("copied")
        fin = s.sem("fin")
        out_stored = s.sem("out_stored")
        extra = [s.sem(f"extra{i}") for i in range(6)]
        if decode:
            c0 = s.sb("c0", [P, DB, HC, DC])
            c1 = s.sb("c1", [P, DB, HC, DC])
            n0 = s.sb("n0", [NS, P])
            n0b = s.sb("n0b", [DB, HC, DC])
            qpad = s.sb("qpad", [P, 4, 288])
            blk = s.sb("blk", [NS, DB])
            kwb = s.sb("kwb", [NS, 2, DB, DC])
            bh = s.sb("bh", [DB, 2, HC])
        else:
            cT = s.sb("cT", [P, 4, P])

        units = [(c, hf) for c in range(NC) for hf in range(2)]

        def q_of(h, c):
            r0 = TILES[tile0 + c][0]
            return k.qkT[DC * (h % 2):DC * (h % 2) + DC, h // 2, r0:r0 + n]

        def k_of(h, c):
            r0 = TILES[tile0 + c][0]
            return k.qkT[DC * (h % 2):DC * (h % 2) + DC, 4 + h // 2, r0:r0 + n]

        with nc.Block() as block:
            @block.sync
            def _(sp):
                for c in range(NC):
                    r0, rows = TILES[tile0 + c]
                    sp.dma_start(v[0:rows, c, :, 0:HEAD], d.proj[r0:r0 + rows, C_CV:C_CV + HC * HEAD].rearrange(
                        "r (h n) -> r h n", h=HC)).then_inc(loaded, 16)
                if decode:
                    sp.dma_start(m[:], d.c_m.rearrange("b h -> h b"), allow_slow_non_contiguous=True).then_inc(st_loaded, 16)
                    sp.dma_start(n0[:], d.c_n.rearrange("b (x y) n -> (b x) (y n)", y=2)).then_inc(st_loaded, 16)
                    sp.dma_start(n0b[:], d.c_n).then_inc(st_loaded, 16)
                    for i in range(DB):
                        sp.dma_start(c0[:, i, :, :], d.c_C[i].rearrange("h v n -> v h n")).then_inc(st_loaded, 16)
                for c in range(NC):
                    r0, rows = TILES[tile0 + c]
                    sp.wait_ge(h_ready, 2 * c + 2)
                    sp.dma_start(d.h_c[r0:r0 + rows, :], h_out[0:rows, c % 2, :, :].rearrange(
                        "p h n -> p (h n)")).then_inc(h_stored[c % 2], 16)
                sp.wait_ge(fin, 1)
                n_out = 0
                if decode:
                    for i in range(DB):
                        sp.dma_start(d.C_s[i].rearrange("h v n -> v h n"), c1[:, i, :, :]).then_inc(out_stored, 16)
                    sp.dma_start(d.n_s, n0b[:]).then_inc(out_stored, 16)
                    sp.dma_start(d.m_s, bh[:, 1, :]).then_inc(out_stored, 16)
                    n_out = DB + 2
                else:
                    for x in range(4):
                        sp.dma_start(d.C_p[2 * x:2 * x + 2].rearrange("y v n -> v y n"),
                                     cT[:, x, :].rearrange("p (y n) -> p y n", y=2)).then_inc(out_stored, 16)
                    for y in range(2):
                        sp.dma_start(d.n_p[y:HC:2, :].rearrange("x n -> n x").unsqueeze(2),
                                     S[DC * y:DC * y + DC, 0, :, HEAD:V],
                                     allow_slow_non_contiguous=True).then_inc(out_stored, 16)
                    sp.dma_start(d.m_p.unsqueeze(1), m[:]).then_inc(out_stored, 16)
                    n_out = 7
                sp.wait_ge(out_stored, 16 * n_out)
                for i in range(min(2, NC)):
                    sp.wait_ge(h_stored[i], 16 * max(1, NC // 2))

            @block.gpsimd
            def _(pool):
                pool.memset(ones[:], 1.0).then_inc(made, 1)
                pool.memset(v[:, :, :, HEAD:V], 1.0).then_inc(made, 1)
                z = [mask, pick, S] + ([qpad] if decode else [m])
                for x in z:
                    pool.memset(x[:], 0.0).then_inc(zeroed, 1)
                pool.wait_ge(zeroed, 4)
                pool.affine_select(out=mask[:], in_=mask[:], compare_op=ALU.is_ge, fill=NEG, base=0,
                                   pattern=[[1, n]], channel_multiplier=-1).then_inc(made, 1)
                pool.affine_select(out=pick[:], in_=pick[:], compare_op=ALU.not_equal, fill=1.0, base=0,
                                   pattern=[[-1, HC], [0, P]], channel_multiplier=1).then_inc(made, 1)
                if decode:
                    pool.wait_ge(made, 4)
                    mv = mask[:].rearrange("p (b t) -> p b t", b=DB)
                    pool.affine_select(out=mv, in_=mv, compare_op=ALU.is_ge, fill=NEG, base=0,
                                       pattern=[[-DT, DB], [0, DT]], channel_multiplier=1).then_inc(made, 1)
                    pool.memset(blk[:], 1.0).then_inc(made, 1)
                    pool.wait_ge(made, 6)
                    pool.affine_select(out=blk[:], in_=blk[:], compare_op=ALU.is_ge, fill=0.0, base=0,
                                       pattern=[[-DT, DB]], channel_multiplier=1).then_inc(made, 1)
                    pool.wait_ge(made, 7)
                    pool.affine_select(out=blk[:], in_=blk[:], compare_op=ALU.is_ge, fill=0.0, base=DT - 1,
                                       pattern=[[DT, DB]], channel_multiplier=-1).then_inc(made, 1)

            @block.tensor
            def _(pe):
                pe.wait_ge(made, 8 if decode else 4)
                if decode:
                    pe.wait_ge(st_loaded, 16 * (DB + 3))
                    for i in range(DB):
                        if i >= 2:
                            pe.wait_ge(copied, i - 1)
                        bank = (pn[0], pn[1])[i % 2]
                        for x in range(2):
                            last = pe.transpose(bank[:, x, 0:P], c0[:, i, 2 * x:2 * x + 2, :].rearrange("p y n -> p (y n)"), k.ident[:])
                        bank = (pi[0], pi[1])[i % 2]
                        for x in range(2, 4):
                            last = pe.transpose(bank[:, x - 2, 0:P], c0[:, i, 2 * x:2 * x + 2, :].rearrange("p y n -> p (y n)"), k.ident[:])
                        last.then_inc(turned, 1)
                    pe.transpose(pu[:, 0:NS], n0[:], k.ident[0:NS, 0:NS]).then_inc(extra[0], 1)
                for c in range(NC):
                    pe.wait_ge(rows_ready, c + 1)
                    if c:
                        pe.wait_ge(r_copied, c)
                    for x in range(4):
                        last = pe.transpose(small[0:n, x, :], row[:, c, x, :], k.ident[0:HC, 0:HC])
                    last.then_inc(r_turned, 1)
                pe.wait_ge(r_copied, NC)
                pe.wait_ge(diag_ready, 1)
                if decode:
                    pe.wait_ge(copied, DB + 1)
                pe.matmul(pu[:, 64:64 + NC * HC * NB], ones[:], diag[:].rearrange("p c h b -> p (c h b)"),
                          start=True, stop=True).then_inc(cs_spread, 1)
                pe.wait_ge(csb_ready, 1)
                pe.wait_ge(loaded, 16 * NC)
                pe.wait_ge(kw_ready, 1)
                if decode:
                    pe.wait_ge(copied, DB + 2)
                for u, (c, hf) in enumerate(units):
                    if u:
                        pe.wait_ge(weighed, u)
                        pe.wait_ge(exped, u)
                    for x in range(4):
                        h = 4 * hf + x
                        pe.matmul(dd[0:n, x, :], pick[:, h, 0:n], nca[:, c, :], start=True, stop=False)
                        pe.matmul(dd[0:n, x, :], k.ident[0:n, 0:n], mask[:], start=False, stop=True)
                        last = pe.matmul(sc[x % 2][0:n, x // 2, 0:n], k_of(h, c), q_of(h, c), start=True, stop=True)
                    last.then_inc(scored, 1)
                    if u:
                        pe.wait_ge(taken, u)
                    if not decode and c:
                        pe.wait_ge(state_ready, u - 1)
                    for x in range(4):
                        h = 4 * hf + x
                        rows = slice(DC * (h % 2), DC * (h % 2) + DC)
                        if decode:
                            for i in range(DB):
                                pe.matmul(pi[x % 2][0:n, x // 2, :], qpad[rows, h // 2, NS * i:NS * i + NS],
                                          S[rows, i, h // 2, :], start=(i == 0), stop=(i == DB - 1))
                        else:
                            pe.matmul(pi[x % 2][:, x // 2, :], q_of(h, c), S[rows, 0, h // 2, :], start=True, stop=True)
                    if not decode:
                        for x in range(4):
                            h = 4 * hf + x
                            rows = slice(DC * (h % 2), DC * (h % 2) + DC)
                            pe.matmul(pu[rows, V * (x // 2):V * (x // 2) + V], kw[:, c, h, :], v[:, c, h, :],
                                      start=True, stop=True)
                    pe.wait_ge(weighed, u + 1)
                    for x in range(4):
                        h = 4 * hf + x
                        last = pe.matmul(pn[x // 2][0:n, x % 2, :], qk[0:n, x, :], v[0:n, c, h, :], start=True, stop=True)
                    last.then_inc(summed, 1)
                if decode:
                    for h in range(HC):
                        pe.wait_ge(extra[1], h + 1)
                        if h:
                            pe.wait_ge(extra[3], h)
                        pe.matmul(pu[:], v[0:NS, 0, h, 0:HEAD], kwb[:, h % 2, :, :].rearrange("p b n -> p (b n)"),
                                  start=True, stop=True).then_inc(extra[2], 1)
                    pe.wait_ge(extra[3], HC)
                    pe.matmul(pu[0:DB, :], blk[:], kw[0:NS, 0, :, :].rearrange("p h n -> p (h n)"), start=True, stop=True)
                    pe.transpose(small[0:DB, 0, :], cs[:, 0, :], k.ident[0:HC, 0:HC])
                    pe.transpose(small[0:DB, 1, :], mt[:, 0, :].rearrange("p (b t) -> p b t", b=DB)[:, :, DT - 1],
                                 k.ident[0:HC, 0:HC]).then_inc(extra[4], 1)
                else:
                    pe.wait_ge(state_ready, 2 * NC)
                    for x in range(4):
                        last = pe.transpose(dd[:, x, :], S[:, 0, x, 0:HEAD], k.ident[:])
                    last.then_inc(turned, 1)

            @block.scalar
            def _(act):
                act.wait_ge(extra[5], 1)
                act.activation(cs[:], cs[:], ACT.Exp).then_inc(cs_exped, 1)
                for c in range(NC):
                    act.wait_ge(r_turned, c + 1)
                    act.activation(col[0:n, c, 0, :], small[0:n, 0, :], ACT.Copy)
                    act.activation(col[0:n, c, 1:4, :], small[0:n, 1:4, :], ACT.Exp).then_inc(r_copied, 1)
                act.wait_ge(r_copied, NC)
                for u, (c, hf) in enumerate(units):
                    act.wait_ge(scored, u + 1)
                    if u:
                        act.wait_ge(weighed, u)
                    for x in range(4):
                        h = 4 * hf + x
                        last = act.activation(w[0:n, x, :], dd[0:n, x, :], ACT.Exp, bias=col[0:n, c, 0, h:h + 1])
                    last.then_inc(exped, 1)
                    act.wait_ge(summed, u + 1)
                    if u:
                        act.wait_ge(taken, u)
                    for x in range(4):
                        h = 4 * hf + x
                        last = act.activation(inter[0:n, x, :], pi[x % 2][0:n, x // 2, :], ACT.Copy,
                                              scale=col[0:n, c, 1, h:h + 1])
                    last.then_inc(in_copied, 1)

            @block.vector
            def _(dve):
                step = Chain(dve, dve_step)
                if decode:
                    dve.wait_ge(st_loaded, 16 * (DB + 3))
                dve.wait_ge(zeroed, 4)
                dve.wait_ge(made, 4)
                for c in range(NC):
                    g0 = TILES[tile0 + c][0]
                    for i in range(NB):
                        r = slice(L * i, L * i + L)
                        gr = slice(g0 + L * i, g0 + L * i + L)
                        init = m[:, i:i + 1]
                        step(dve.tensor_tensor_scan(b[:, c, r], ones[:, 0:L], k.gate_f[:, gr], 0.0, ALU.mult, ALU.add))
                        step(dve.tensor_tensor(row[:, c, 0, r], k.gate_i[:, gr], b[:, c, r], ALU.subtract))
                        step(dve.tensor_tensor_scan(nca[:, c, r], row[:, c, 0, r], row[:, c, 0, r], init, ALU.max, ALU.max))
                    ca = nca[:, c, :].rearrange("p (b t) -> p b t", b=NB)
                    last_ca = ca[:, :, L - 1:L]
                    step(dve.tensor_tensor(row[:, c, 1, :].rearrange("p (b t) -> p b t", b=NB),
                                           m[:].unsqueeze(2).broadcast_to([HC, NB, L]), ca, ALU.subtract))
                    step(dve.tensor_tensor(mt[:, c, :], b[:, c, :], nca[:, c, :], ALU.add))
                    step(dve.tensor_scalar(row[:, c, 2, :], mt[:, c, :], -1.0, None, ALU.mult))
                    step(dve.tensor_tensor(row[:, c, 3, :].rearrange("p (b t) -> p b t", b=NB),
                                           row[:, c, 0, :].rearrange("p (b t) -> p b t", b=NB),
                                           last_ca.broadcast_to([HC, NB, L]), ALU.subtract))
                    step(dve.tensor_tensor(cs[:, c, :].unsqueeze(2), m[:].unsqueeze(2), last_ca, ALU.subtract))
                    if not decode:
                        step(dve.tensor_copy(m[:], mt[:, c, L - 1:L]))
                    dve.tensor_scalar(nca[:, c, :], nca[:, c, :], -1.0, None, ALU.mult).then_inc(rows_ready, 1)
                dve.sem_inc(extra[5], 1)
                dve.wait_ge(cs_exped, 1)
                for c in range(NC):
                    last = dve.tensor_tensor(diag[:, c, :, :], k.ident[0:HC, 0:HC].unsqueeze(2).broadcast_to([HC, HC, NB]),
                                             cs[:, c, :].unsqueeze(1).broadcast_to([HC, HC, NB]), ALU.mult)
                last.then_inc(diag_ready, 1)
                if decode:
                    for i in range(DB):
                        dve.wait_ge(turned, i + 1)
                        dve.tensor_copy(S[:, i, 0:2, 0:HEAD], pn[i % 2][:, :, 0:HEAD])
                        dve.tensor_copy(S[:, i, 2:4, 0:HEAD], pi[i % 2][:, :, 0:HEAD]).then_inc(copied, 1)
                    dve.wait_ge(extra[0], 1)
                    dve.tensor_copy(S[:, :, :, HEAD:V], pu[:, 0:NS].rearrange("p (b x) -> p b x", b=DB).unsqueeze(3)) \
                        .then_inc(copied, 1)
                    dve.tensor_copy(qpad[:].rearrange("p x (b y) -> p x b y", y=36)[:, :, :, 0:DT],
                                    k.qkT[:, 0:4, SEQ:ROWS].rearrange("p x (b t) -> p x b t", b=DB)).then_inc(copied, 1)
                dve.wait_ge(cs_spread, 1)
                dve.tensor_copy(csb[:].rearrange("p c h b -> p (c h b)"), pu[:, 64:64 + NC * HC * NB]).then_inc(csb_ready, 1)
                dve.wait_ge(csb_ready, 1)
                dve.wait_ge(r_copied, NC)
                for c in range(NC):
                    last = dve.tensor_tensor(kw[0:n, c, :, :], k.k_rows[0:n, tile0 + c, :].rearrange(
                        "p (h n) -> p h n", h=HC), col[0:n, c, 3, :].unsqueeze(2).broadcast_to([n, HC, DC]), ALU.mult)
                last.then_inc(kw_ready, 1)
                for u, (c, hf) in enumerate(units):
                    dve.wait_ge(exped, u + 1)
                    if u:
                        dve.wait_ge(summed, u)
                    for y in range(2):
                        last = dve.tensor_tensor(qk[0:n, y:4:2, :], sc[y][0:n, :, 0:n], w[0:n, y:4:2, :], ALU.mult)
                    last.then_inc(weighed, 1)
                    dve.wait_ge(summed, u + 1)
                    dve.wait_ge(in_copied, u + 1)
                    for x in range(2):
                        last = dve.tensor_tensor(num[0:n, 2 * x:2 * x + 2, :], inter[0:n, 2 * x:2 * x + 2, :],
                                                 pn[x][0:n, :, :], ALU.add)
                    step(last)
                    if not decode:
                        st = S[:, 0, 2 * hf:2 * hf + 2, :]
                        for y in range(2):
                            rows = slice(DC * y, DC * y + DC)
                            sy = S[rows, 0, 2 * hf:2 * hf + 2, :]
                            step(dve.tensor_tensor(sy, sy, csb[rows, c, 4 * hf + y:4 * hf + 4:2, :].broadcast_to(
                                [DC, 2, V]), ALU.mult))
                        dve.tensor_tensor(st, st, pu[:, 0:2 * V].rearrange("p (x n) -> p x n", x=2),
                                          ALU.add).then_inc(state_ready, 1)
                        dve.wait_ge(state_ready, u + 1)
                    dve.sem_inc(taken, 1)
                    dn = num[0:n, :, HEAD:V].rearrange("p x a -> p (x a)")
                    step(dve.scalar_tensor_tensor(den[0:n, 0, :], dn, -1.0, dn, ALU.mult, ALU.max))
                    step(dve.tensor_tensor(den[0:n, 1, :], den[0:n, 0, :], col[0:n, c, 2, 4 * hf:4 * hf + 4], ALU.max))
                    step(dve.reciprocal(den[0:n, 2, :], den[0:n, 1, :]))
                    if c >= 2:
                        dve.wait_ge(h_stored[c % 2], 16 * (c // 2))
                    dve.tensor_tensor(h_out[0:n, c % 2, 4 * hf:4 * hf + 4, :], num[0:n, :, 0:HEAD],
                                      den[0:n, 2, :].unsqueeze(2).broadcast_to([n, 4, HEAD]), ALU.mult).then_inc(h_ready, 1)
                if decode:
                    for h in range(HC):
                        if h >= 2:
                            dve.wait_ge(extra[2], h - 1)
                        dve.tensor_tensor(kwb[:, h % 2, :, :], kw[0:NS, 0, h, :].unsqueeze(1).broadcast_to([NS, DB, DC]),
                                          blk[:].unsqueeze(2).broadcast_to([NS, DB, DC]), ALU.mult).then_inc(extra[1], 1)
                        step(dve.tensor_tensor(c1[:, :, h, :], c0[:, :, h, :], csb[:, 0, h, :].unsqueeze(2).broadcast_to(
                            [P, DB, DC]), ALU.mult))
                        dve.wait_ge(extra[2], h + 1)
                        dve.tensor_tensor(c1[:, :, h, :], c1[:, :, h, :], pu[:].rearrange("p (b n) -> p b n", b=DB),
                                          ALU.add).then_inc(extra[3], 1)
                    dve.wait_ge(extra[4], 1)
                    step(dve.tensor_copy(bh[:], small[0:DB, 0:2, :]))
                    step(dve.tensor_tensor(n0b[:], n0b[:], bh[:, 0, :].unsqueeze(2).broadcast_to([DB, HC, DC]), ALU.mult))
                    dve.tensor_tensor(n0b[:], n0b[:], pu[0:DB, :].rearrange("p (h n) -> p h n", h=HC),
                                      ALU.add).then_inc(fin, 1)
                else:
                    dve.wait_ge(turned, 1)
                    dve.tensor_copy(cT[:], dd[:]).then_inc(fin, 1)


def output(nc, d, k):
    GW = 1036
    CW = 2 * HC * HEAD
    NSL = D // SLAB
    PC, RING = 2, 4
    NP = KC // PC
    with Stage(nc, "ou") as s:
        att = s.sb("att", [P, 2, 2048])
        hc = s.sb("hc", [P, 2, HC * HEAD])
        g = s.sb("g", [P, 2, GW + CW])
        sg = s.sb("sg", [P, GW + CW])
        sq = s.sb("sq", [P, 1536])
        st = s.sb("st", [P, 5, 3, 12])
        ga = s.sb("ga", [P, HEAD])
        gc = s.sb("gc", [P, HEAD])
        mhi = s.sb("mhi", [P, KC, SEQ], F32R)
        mlo = s.sb("mlo", [P, KC, SEQ], F32R)
        ms = s.sb("ms", [P, KC, 2 * NS], F32R)
        w = s.sb("w", [P, 2, PC, SLAB])
        whi = s.sb("whi", [P, RING, PC, SLAB], F32R)
        wlo = s.sb("wlo", [P, RING, PC, SLAB], F32R)
        out = s.sb("out", [P, 5, SLAB])
        low = s.sb("low", [NS, SLAB])
        ps = [s.ps(f"ps{i}", [P, SLAB]) for i in range(8)]
        tp = [v[:].rearrange("p (c n) -> p c n", c=4) for v in ps]
        loaded = s.sems("loaded", 2)
        gains_loaded = s.sem("gains_loaded")
        w_loaded = s.sems("w_loaded", 2)
        x_loaded = s.sems("x_loaded", 5)
        store_turn = s.sem("store_turn")
        gains_ready = s.sem("gains_ready")
        squashed = s.sem("squashed")
        squared = s.sem("squared")
        gated = s.sem("gated")
        summed = s.sem("summed")
        rooted = s.sem("rooted")
        dve_step = s.sem("dve_step")
        pool_step = s.sem("pool_step")
        mixed = s.sem("mixed")
        turned = s.sem("turned")
        mhi_ready = s.sem("mhi_ready")
        copied = s.sem("copied")
        whi_ready = s.sem("whi_ready")
        wlo_ready = s.sem("wlo_ready")
        w_used = s.sem("w_used")
        product_ready = s.sems("product_ready", 5)
        low_added = s.sem("low_added")
        low_out = s.sem("low_out")
        y_ready = s.sems("y_ready", 5)
        stored = s.sems("stored", 5)
        wv = d.w_out.rearrange("(c p) n -> p c n", p=P)

        def high(t):
            return mhi[:, :, P * t:P * t + P] if t < PT else ms[:, :, 0:NS]

        def low_part(t):
            return mlo[:, :, P * t:P * t + P] if t < PT else ms[:, :, NS:2 * NS]

        with nc.Block() as block:
            @block.sync
            def _(sp):
                def load_tile(t):
                    r0, rows = TILES[t]
                    i = t % 2
                    if t >= 2:
                        sp.wait_ge(turned, 4 * (t - 1))
                        sp.wait_ge(gated, t - 1)
                    for dst, src in ((att[0:rows, i, :], d.o_att[r0:r0 + rows, :]),
                                     (hc[0:rows, i, :], d.h_c[r0:r0 + rows, :]),
                                     (g[0:rows, i, 0:512], d.proj[r0:r0 + rows, C_AZ:C_BQ]),
                                     (g[0:rows, i, 512:GW], d.proj[r0:r0 + rows, C_BG:C_CQK]),
                                     (g[0:rows, i, GW:GW + CW], d.proj[r0:r0 + rows, C_CO:N_IN])):
                        sp.dma_start(dst, src).then_inc(loaded[i], 16)

                def load_w(j, c):
                    sp.dma_start(w[:, c % 2, :, :],
                                 wv[:, PC * c:PC * c + PC, bass.ds(j * SLAB, SLAB)]).then_inc(w_loaded[c % 2], 16)

                def load_next(j, c):
                    sp.wait_ge(wlo_ready, j * NP + c + 1)
                    load_w(j + (c + 2) // NP, (c + 2) % NP)

                def load_x(j, t):
                    r0, rows = TILES[t]
                    src = d.x_prompt[r0:r0 + rows, :] if t < PT else d.x_sample
                    sp.dma_start(out[0:rows, t, :], src[:, bass.ds(j * SLAB, SLAB)]).then_inc(x_loaded[t], 16)

                def step(j, after):
                    for c in range(RING, NP):
                        if c + 2 < NP or after:
                            load_next(j, c)
                    if after:
                        for c in range(RING - 1):
                            load_next(j + 1, c)
                    for t, (r0, rows) in enumerate(TILES):
                        dst = d.y_p[r0:r0 + rows, :] if t < PT else d.y_s
                        sp.wait_ge(y_ready[t], j + 2)
                        sp.sem_inc(store_turn, 1)
                        sp.dma_start(dst[:, bass.ds(j * SLAB, SLAB)], out[0:rows, t, :]).then_inc(stored[t], 16)
                    if after:
                        load_next(j + 1, RING - 1)
                        for t in range(5):
                            sp.wait_ge(stored[t], j * 16 + 16)
                            sp.sem_inc(store_turn, 1)
                            load_x(j + 1, t)

                load_tile(0)
                load_tile(1)
                load_w(0, 0)
                load_w(0, 1)
                for t in range(2, 5):
                    load_tile(t)
                for t in range(5):
                    load_x(0, t)
                for c in range(RING):
                    load_next(0, c)
                with sp.Fori(0, NSL - 1) as j:
                    step(j, True)
                step(NSL - 1, False)
                for t in range(5):
                    sp.wait_ge(stored[t], 16 * NSL)

            @block.gpsimd
            def _(pool):
                pool.dma_start(ga[:], d.a_out_g.partition_broadcast(P)).then_inc(gains_loaded, 16)
                pool.dma_start(gc[:], d.c_out_g.partition_broadcast(P)).then_inc(gains_loaded, 16)
                n = 0
                for t, (r0, rows) in enumerate(TILES):
                    i = t % 2
                    pool.wait_ge(squashed, t + 1)
                    br = [att[0:rows, i, 512 * (x + 1):512 * (x + 2)].rearrange("p (h n) -> p h n", n=HEAD)
                          for x in range(3)]
                    gates = sg[0:rows, 512:524].rearrange("p (h n) -> p h n", n=3)
                    for x, gate in ((0, 1), (1, 2), (2, 0)):
                        pool.tensor_tensor(br[x], br[x], gates[:, :, gate:gate + 1].broadcast_to(
                            [rows, HB, HEAD]), ALU.mult).then_inc(pool_step, 1)
                    for a, b in ((0, 512), (GW - 512, GW), (GW + 1024, GW + CW)):
                        pool.tensor_tensor(g[0:rows, i, a:b], g[0:rows, i, a:b], sg[0:rows, a:b],
                                           ALU.mult).then_inc(pool_step, 1)
                    n += 6
                    pool.wait_ge(pool_step, n)
                    pool.sem_inc(gated, 1)

            @block.scalar
            def _(act):
                def copy_out(t):
                    for q in range(4):
                        act.wait_ge(turned, 4 * t + q + 1)
                        act.activation(high(t)[:, 4 * q:4 * q + 4, :], tp[(4 * t + q) % 8][:, :, 0:TILES[t][1]],
                                       ACT.Copy).then_inc(mhi_ready, 1)

                def split_w(j, c):
                    act.wait_ge(w_loaded[c % 2], j * (8 * NP) + 16 * (c // 2) + 16)
                    act.wait_ge(w_used, j * NP + c + 1)
                    act.activation(whi[:, c % RING, :, :], w[:, c % 2, :, :], ACT.Copy).then_inc(whi_ready, 1)

                act.sem_inc(w_used, RING)
                for t, (r0, rows) in enumerate(TILES):
                    act.wait_ge(loaded[t % 2], 80 * (t // 2 + 1))
                    if t:
                        act.wait_ge(summed, t)
                    act.activation(sq[0:rows, 0:512], att[0:rows, t % 2, 0:512], ACT.Square)
                    act.activation(sq[0:rows, 512:1536], hc[0:rows, t % 2, :], ACT.Square).then_inc(squared, 1)
                    if t:
                        act.wait_ge(mixed, t)
                    act.activation(sg[0:rows, :], g[0:rows, t % 2, :], ACT.Sigmoid).then_inc(squashed, 1)
                    act.wait_ge(summed, t + 1)
                    act.activation(st[0:rows, t, 1, :], st[0:rows, t, 0, :], ACT.Sqrt, bias=k.eps[0:rows, :],
                                   scale=1.0 / HEAD).then_inc(rooted, 1)
                    if t:
                        copy_out(t - 1)
                        split_w(0, t - 1)
                copy_out(4)

                def step(j, after):
                    for c in range(RING, NP):
                        split_w(j, c)
                    if after:
                        for c in range(RING - 1):
                            split_w(j + 1, c)
                    act.wait_ge(product_ready[4], j + 1)
                    act.wait_ge(y_ready[4], j + 1)
                    act.activation(low[:], ps[4][NS:2 * NS, :], ACT.Copy).then_inc(low_out, 1)
                    if after:
                        split_w(j + 1, RING - 1)

                with act.Fori(0, NSL - 1) as j:
                    step(j, True)
                step(NSL - 1, False)

            @block.vector
            def _(dve):
                step = Chain(dve, dve_step)

                def copy_out(t):
                    for q in range(4):
                        dve.wait_ge(mhi_ready, 4 * t + q + 1)
                        dve.tensor_tensor(low_part(t)[:, 4 * q:4 * q + 4, :], tp[(4 * t + q) % 8][:, :, 0:TILES[t][1]],
                                          high(t)[:, 4 * q:4 * q + 4, :], ALU.subtract).then_inc(copied, 1)

                def split_w(j, c):
                    dve.wait_ge(whi_ready, j * NP + c + 1)
                    dve.tensor_tensor(wlo[:, c % RING, :, :], w[:, c % 2, :, :], whi[:, c % RING, :, :],
                                      ALU.subtract).then_inc(wlo_ready, 1)

                for t in range(5):
                    dve.sem_inc(y_ready[t], 1)
                dve.wait_ge(gains_loaded, 32)
                step(dve.tensor_scalar(ga[:], ga[:], 1.0 - LAM0, None, ALU.mult))
                for t, (r0, rows) in enumerate(TILES):
                    i = t % 2
                    heads = lambda v: v.rearrange("p (h n) -> p h n", n=HEAD)
                    A, C = heads(att[0:rows, i, 0:512]), heads(hc[0:rows, i, :])
                    dve.wait_ge(squared, t + 1)
                    dve.tensor_reduce(st[0:rows, t, 0, :], heads(sq[0:rows, :]), AX_X, ALU.add).then_inc(summed, 1)
                    dve.wait_ge(rooted, t + 1)
                    step(dve.reciprocal(st[0:rows, t, 2, :], st[0:rows, t, 1, :]))
                    dve.tensor_tensor(A, A, st[0:rows, t, 2, 0:HA].unsqueeze(2).broadcast_to([rows, HA, HEAD]), ALU.mult)
                    step(dve.tensor_tensor(C, C, st[0:rows, t, 2, HA:12].unsqueeze(2).broadcast_to([rows, HC, HEAD]),
                                           ALU.mult))
                    dve.tensor_tensor(A, A, ga[0:rows, :].unsqueeze(1).broadcast_to([rows, HA, HEAD]), ALU.mult)
                    step(dve.tensor_tensor(C, C, gc[0:rows, :].unsqueeze(1).broadcast_to([rows, HC, HEAD]), ALU.mult))
                    dve.wait_ge(gated, t + 1)
                    br = [heads(att[0:rows, i, 512 * (x + 1):512 * (x + 2)]) for x in range(3)]
                    gate = heads(g[0:rows, i, GW:GW + 1024])
                    dve.tensor_tensor(A, A, heads(g[0:rows, i, 0:512]), ALU.mult)
                    dve.tensor_tensor(gate, heads(g[0:rows, i, GW + 1024:GW + CW]), heads(sg[0:rows, GW:GW + 1024]),
                                      ALU.mult)
                    step(dve.tensor_tensor(br[1], br[1], br[2], ALU.add))
                    step(dve.tensor_tensor(br[0], br[0], br[1], ALU.add))
                    dve.tensor_tensor(br[0], br[0], heads(g[0:rows, i, GW - 512:GW]), ALU.mult)
                    dve.tensor_tensor(C, C, gate, ALU.mult).then_inc(mixed, 1)
                    if t:
                        copy_out(t - 1)
                        split_w(0, t - 1)
                copy_out(4)

                def slab(j, after):
                    for c in range(RING, NP):
                        split_w(j, c)
                    if after:
                        for c in range(RING - 1):
                            split_w(j + 1, c)
                    for t, (_, rows) in enumerate(TILES):
                        dve.wait_ge(x_loaded[t], j * 16 + 16)
                        dve.wait_ge(product_ready[t], j + 1)
                        if t == PT:
                            dve.wait_ge(low_out, j + 1)
                            dve.tensor_tensor(low[:], low[:], out[0:NS, t, :], ALU.add).then_inc(low_added, 1)
                            dve.wait_ge(low_added, j + 1)
                        dve.tensor_tensor(out[0:rows, t, :], low[:] if t == PT else out[:, t, :], ps[t][0:rows, :],
                                          ALU.add).then_inc(y_ready[t], 1)
                    if after:
                        split_w(j + 1, RING - 1)

                with dve.Fori(0, NSL - 1) as j:
                    slab(j, True)
                slab(NSL - 1, False)

            @block.tensor
            def _(pe):
                def turn(t):
                    rows = TILES[t][1]
                    pe.wait_ge(mixed, t + 1)
                    for q in range(4):
                        m = 4 * t + q
                        if m >= 8:
                            pe.wait_ge(copied, m - 7)
                        src = (att, hc)[q // 2][:, t % 2, 512 * (q % 2):512 * (q % 2) + 512]
                        for c in range(4):
                            last = pe.transpose(tp[m % 8][:, c, 0:rows], src[0:rows, P * c:P * c + P],
                                                k.ident[0:rows, 0:rows])
                        last.then_inc(turned, 1)

                def multiply(j):
                    for c in range(NP):
                        pe.wait_ge(wlo_ready, j * NP + c + 1)
                        for t in range(5):
                            if c == 0:
                                pe.wait_ge(y_ready[t], j + 1)
                            for i in range(PC):
                                kc = PC * c + i
                                first, end = kc == 0, kc == KC - 1
                                wh, wl = whi[:, c % RING, i, :], wlo[:, c % RING, i, :]
                                if t < PT:
                                    hi, lo = (v[:, kc, P * t:P * t + P] for v in (mhi, mlo))
                                    pe.matmul(ps[t][:], hi, wh, start=first, stop=False)
                                    pe.matmul(ps[t][:], hi, wl, start=False, stop=False)
                                    last = pe.matmul(ps[t][:], lo, wh, start=False, stop=end)
                                else:
                                    acc = ps[t][0:2 * NS, :]
                                    pe.matmul(acc, ms[:, kc, :], wh, start=first, stop=False)
                                    last = pe.matmul(acc, ms[:, kc, :], wl, start=False, stop=end)
                            if c == NP - 1:
                                last.then_inc(product_ready[t], 1)
                        if c < NP - 1:
                            last.then_inc(w_used, 1)
                    pe.wait_ge(product_ready[4], j + 1)
                    pe.sem_inc(w_used, 1)

                for t in range(5):
                    turn(t)
                pe.wait_ge(copied, 20)
                with pe.Fori(0, NSL - 1) as j:
                    multiply(j)
                multiply(NSL - 1)




def stages(nc, d, k, s):
    k.eps = s.sb("eps", [P, 1])
    with Stage(nc, "mx") as m:
        k.ones = m.sb("ones", [P, P])
        k.causal = m.sb("causal", [P, P])
        k.z = m.sb("z", [P, 94])
        k.pkv = m.sb("pkv", [32, 2 * DB, 2 * HEAD])
        k.neglam = m.sb("neglam", [P, 1])
        project(nc, d, k)
        with Stage(nc, "at") as a:
            k.rows_s = a.sb("rows_s", [NS, TW])
            k.attT = a.sb("attT", [P, XCH, ROWS])
            k.selb = a.sb("selb", [NBLK, DB, NBLK])
            with Stage(nc, "ap") as p:
                k.rows_p = p.sb("rows_p", [P, PT, TW])
                prepare(nc, d, k)
                prompt_attend(nc, d, k)
                compress(nc, d, k)
            decode_attend(nc, d, k)
        with Stage(nc, "ml") as c:
            k.qkT = c.sb("qkT", [P, 8, ROWS])
            k.k_rows = c.sb("k_rows", [P, 5, HC * DC])
            k.gate_i = c.sb("gate_i", [HC, ROWS])
            k.gate_f = c.sb("gate_f", [HC, ROWS])
            convolve(nc, d, k)
            mlstm(nc, d, k, False)
            mlstm(nc, d, k, True)
    output(nc, d, k)


class Names:
    pass


INPUTS = ["x_prompt", "x_sample", "cache_a_kv", "cache_b_kv", "state_b_win", "state_c_conv", "state_c_C",
          "state_c_n", "state_c_m", "page_table", "norm_g", "w_in", "w_out", "a_qk_g", "a_lambda", "a_out_g",
          "b_qk_g", "b_cmp_w", "c_conv_w", "c_conv_b", "c_gate_b", "c_out_g"]
QKC = 2 * HC * DC
OUTPUTS = [(1, SEQ, D), (DB, DT, D), (1, 1, SEQ, 2, HA, HEAD), (1, DB, DT, 2, HA, HEAD),
           (1, 1, SEQ, 4, HEAD), (1, DB, DT, 4, HEAD), (1, 1, WIN, 2, HEAD), (1, DB, WIN, 2, HEAD),
           (1, 1, 3, QKC), (1, DB, 3, QKC), (1, 1, HC, HEAD, DC), (1, DB, HC, HEAD, DC),
           (1, 1, HC, DC), (1, DB, HC, DC), (1, 1, HC), (1, DB, HC)]


def build(nc, a, o):
    d, k = Names(), Names()
    d.x_prompt = a["x_prompt"][0]
    d.x_sample = a["x_sample"].rearrange("b t d -> (b t) d")
    d.cache_a = a["cache_a_kv"][0].rearrange("n p a h d -> n p (a h d)")
    d.cache_b = a["cache_b_kv"][0].rearrange("n p a d -> n p (a d)")
    d.b_win = a["state_b_win"][0].rearrange("b w a d -> b w (a d)")
    d.c_conv = a["state_c_conv"][0]
    d.c_C, d.c_n, d.c_m = a["state_c_C"][0], a["state_c_n"][0], a["state_c_m"][0]
    d.page_table = a["page_table"]
    d.norm_g, d.w_in, d.w_out = a["norm_g"][0], a["w_in"][0], a["w_out"][0]
    d.a_qk_g, d.a_lambda, d.a_out_g = a["a_qk_g"][0], a["a_lambda"][0], a["a_out_g"][0]
    d.b_qk_g, d.b_cmp_w, d.c_conv_w = a["b_qk_g"][0], a["b_cmp_w"][0], a["c_conv_w"][0]
    d.c_conv_b, d.c_gate_b, d.c_out_g = a["c_conv_b"][0], a["c_gate_b"][0], a["c_out_g"][0]
    d.y_p, d.y_s = o[0][0], o[1].rearrange("b t d -> (b t) d")
    d.a_kv_p = o[2][0, 0].rearrange("t a h d -> t (a h d)")
    d.a_kv_s = o[3][0].rearrange("b t a h d -> (b t) (a h d)")
    d.b_kv_p = o[4][0, 0].rearrange("t a d -> t (a d)")
    d.b_kv_s = o[5][0].rearrange("b t a d -> (b t) (a d)")
    d.win_p = o[6][0, 0].rearrange("t a d -> t (a d)")
    d.win_s = o[7][0].rearrange("b t a d -> b t (a d)")
    d.conv_p, d.conv_s = o[8][0, 0], o[9][0]
    d.C_p, d.C_s, d.n_p, d.n_s = o[10][0, 0], o[11][0], o[12][0, 0], o[13][0]
    d.m_p, d.m_s = o[14][0, 0], o[15][0]
    d.proj = nc.dram_tensor("proj", [ROWS, N_IN], F32).ap()
    d.o_att = nc.dram_tensor("o_att", [ROWS, 4 * 512], F32).ap()
    d.h_c = nc.dram_tensor("h_c", [ROWS, HC * HEAD], F32).ap()
    with Stage(nc, "all") as s:
        k.ident = s.sb("ident", [P, P])
        stages(nc, d, k, s)


def kernel(**inputs):
    import numpy as np
    import concourse.bacc as bacc
    from concourse.bass_utils import run_bass_kernel_spmd

    nc = bacc.Bacc("TRN2", target_bir_lowering=False, num_devices=1)
    arrays, a = {}, {}
    for name in INPUTS:
        v = np.ascontiguousarray(inputs[name])
        arrays[f"in_{name}"] = v
        a[name] = nc.dram_tensor(f"in_{name}", v.shape, mybir.dt.from_np(v.dtype), kind="ExternalInput").ap()
    o = [nc.dram_tensor(f"out_{i}", shape, F32, kind="ExternalOutput").ap() for i, shape in enumerate(OUTPUTS)]
    build(nc, a, o)
    r = run_bass_kernel_spmd(nc, [arrays], core_ids=[0])
    return tuple(r.results[0][f"out_{i}"] for i in range(len(OUTPUTS)))
```
